# Optimizing a Trainium2 kernel written in Bass

```python
import math
import jax, jax.numpy as jnp
from jax import lax
import numpy as np

D_MODEL = 1024
BATCH = 1
SEQ = 512
DEPTH = 1

CHUNK = 64
Q_BLOCK = 128
MEM_TOKENS = 256
D_MIX = D_MODEL
RWKV_HEAD = 64
RWKV_WIDTH = D_MIX // 2
RWKV_HEADS = RWKV_WIDTH // RWKV_HEAD
DECAY_LORA = 64
AAA_LORA = 64
GATE_LORA = 128
RWKV_COLS = 3 * RWKV_WIDTH + DECAY_LORA + AAA_LORA + GATE_LORA
GN_EPS = 64e-5
DIFF_WIDTH = D_MIX - RWKV_WIDTH
DIFF_HEADS = 4
DIFF_VDIM = DIFF_WIDTH // DIFF_HEADS
DIFF_QKDIM = DIFF_VDIM // 2
DIFF_COLS = 3 * DIFF_WIDTH
D_IN_TOTAL = RWKV_COLS + DIFF_COLS
MEM_HEADS = 4
MEM_HEAD_DIM = D_MODEL // MEM_HEADS
D_FF = 4 * D_MODEL
RMS_EPS = 1e-5
NEG_INF = -1e30


def rms_norm(x, w, eps=RMS_EPS):
    xf = x.astype(jnp.float32)
    y = xf * lax.rsqrt(jnp.mean(jnp.square(xf), axis=-1, keepdims=True) + eps)
    return (y * w.astype(jnp.float32)).astype(x.dtype)

def rwkv7_scan(r, decay, k, v, kk, a):
    B, S, H, N = r.shape
    xs = tuple(jnp.moveaxis(t, 1, 0) for t in (r, decay, k, v, kk, a))

    def step(state, inp):
        r_t, w_t, k_t, v_t, kk_t, a_t = inp
        sa = jnp.einsum("bhvk,bhk->bhv", state, -kk_t)
        state = (state * w_t[:, :, None, :]
                 + sa[..., None] * (kk_t * a_t)[:, :, None, :]
                 + v_t[..., None] * k_t[:, :, None, :])
        y = jnp.einsum("bhvk,bhk->bhv", state, r_t)
        return state, y

    s0 = jnp.zeros((B, H, N, N), jnp.float32)
    _, ys = lax.scan(step, s0, xs)
    return jnp.moveaxis(ys, 0, 1)

def rwkv7_group(p, mu, w0, w_dec_up, a0, a_up, g_up, k_k, k_a, r_k, lnx_w, lnx_b):
    B, S, _ = p.shape
    p_prev = jnp.pad(p, ((0, 0), (1, 0), (0, 0)))[:, :-1]
    p = p + (p_prev - p) * mu
    r, k, v, wd, ad, gd = jnp.split(
        p, [RWKV_WIDTH, 2 * RWKV_WIDTH, 3 * RWKV_WIDTH,
            3 * RWKV_WIDTH + DECAY_LORA, 3 * RWKV_WIDTH + DECAY_LORA + AAA_LORA], axis=-1)
    f32 = jnp.float32
    w_log = -jax.nn.softplus(-(w0 + jnp.tanh(wd) @ w_dec_up)) - 0.5
    decay = jnp.exp(-jnp.exp(w_log.astype(f32)))
    a = jax.nn.sigmoid((a0 + ad @ a_up).astype(f32))
    g = jax.nn.sigmoid(gd) @ g_up
    heads = lambda t: t.astype(f32).reshape(B, S, RWKV_HEADS, RWKV_HEAD)
    kk = heads(k * k_k)
    kk = kk / jnp.maximum(jnp.sqrt(jnp.sum(jnp.square(kk), -1, keepdims=True)), 1e-12)
    k_mod = k.astype(f32) * (1.0 + (a - 1.0) * k_a)
    rh, kh, vh, ah, wh = heads(r), heads(k_mod), heads(v), heads(a), heads(decay)
    y = rwkv7_scan(rh, wh, kh, vh, kk, ah)
    mean = jnp.mean(y, -1, keepdims=True)
    var = jnp.mean(jnp.square(y - mean), -1, keepdims=True)
    y = ((y - mean) * lax.rsqrt(var + GN_EPS)).reshape(B, S, RWKV_WIDTH)
    y = y * lnx_w + lnx_b
    bonus = jnp.sum(rh * kh * r_k, -1, keepdims=True) * vh
    y = y + bonus.reshape(B, S, RWKV_WIDTH)
    return (y * g).astype(p.dtype)

def diff_attn_group(p, lam_q1, lam_k1, lam_q2, lam_k2, subln_w, lam_init):
    B, S, _ = p.shape
    q, k, v = jnp.split(p, [DIFF_WIDTH, 2 * DIFF_WIDTH], axis=-1)
    q = q.reshape(B, S, DIFF_HEADS, 2, DIFF_QKDIM)
    k = k.reshape(B, S, DIFF_HEADS, 2, DIFF_QKDIM)
    v = v.reshape(B, S, DIFF_HEADS, DIFF_VDIM)
    q1, q2 = q[..., 0, :], q[..., 1, :]
    k1, k2 = k[..., 0, :], k[..., 1, :]
    f32 = jnp.float32
    lam = (jnp.exp(jnp.sum(lam_q1 * lam_k1).astype(f32))
           - jnp.exp(jnp.sum(lam_q2 * lam_k2).astype(f32)) + lam_init)
    scale = DIFF_QKDIM ** -0.5
    outs = []
    for qb in range(S // Q_BLOCK):
        qs, qe = qb * Q_BLOCK, (qb + 1) * Q_BLOCK
        mask = (jnp.arange(qe) // CHUNK)[None, :] <= (jnp.arange(qs, qe) // CHUNK)[:, None]
        s1 = jnp.einsum("bqhd,bkhd->bhqk", q1[:, qs:qe], k1[:, :qe]).astype(f32) * scale
        s2 = jnp.einsum("bqhd,bkhd->bhqk", q2[:, qs:qe], k2[:, :qe]).astype(f32) * scale
        p1 = jax.nn.softmax(jnp.where(mask, s1, NEG_INF), axis=-1)
        p2 = jax.nn.softmax(jnp.where(mask, s2, NEG_INF), axis=-1)
        attn = (p1 - lam * p2).astype(v.dtype)
        outs.append(jnp.einsum("bhqk,bkhd->bqhd", attn, v[:, :qe]))
    o = jnp.concatenate(outs, axis=1)
    o = rms_norm(o, subln_w) * (1.0 - lam_init)
    return o.reshape(B, S, DIFF_WIDTH)

def memory_cross_attn(hn, memn, w_mq, w_mk, w_mv, w_mo):
    B, S, _ = hn.shape
    M = memn.shape[1]
    q = (hn @ w_mq).reshape(B, S, MEM_HEADS, MEM_HEAD_DIM)
    k = (memn @ w_mk).reshape(B, M, MEM_HEADS, MEM_HEAD_DIM)
    v = (memn @ w_mv).reshape(B, M, MEM_HEADS, MEM_HEAD_DIM)
    s = jnp.einsum("bshd,bmhd->bhsm", q, k).astype(jnp.float32) * (MEM_HEAD_DIM ** -0.5)
    pr = jax.nn.softmax(s, axis=-1).astype(v.dtype)
    o = jnp.einsum("bhsm,bmhd->bshd", pr, v).reshape(B, S, D_MODEL)
    return o @ w_mo

def first_inputs(seed: int = 0) -> dict:
    key = jax.random.key(seed)
    ks = jax.random.split(key, 32)
    f32 = jnp.float32
    nrm = lambda k, shape, s: jax.random.normal(k, shape, f32) * s
    L = DEPTH
    return {
        "x": nrm(ks[0], (BATCH, SEQ, D_MODEL), 1.0),
        "mem": nrm(ks[1], (BATCH, MEM_TOKENS, D_MODEL), 1.0),
        "norm_mix_w": 1.0 + nrm(ks[2], (L, D_MODEL), 0.05),
        "w_in": nrm(ks[3], (L, D_MODEL, D_IN_TOTAL), D_MODEL ** -0.5),
        "mu_shift": jax.random.uniform(ks[4], (L, RWKV_COLS), f32),
        "w_decay0": jnp.linspace(-6.0, -1.0, RWKV_WIDTH, dtype=f32)[None] + nrm(ks[5], (L, RWKV_WIDTH), 0.1),
        "w_decay_up": nrm(ks[6], (L, DECAY_LORA, RWKV_WIDTH), 0.1),
        "a0": nrm(ks[7], (L, RWKV_WIDTH), 0.1),
        "a_up": nrm(ks[8], (L, AAA_LORA, RWKV_WIDTH), AAA_LORA ** -0.5),
        "g_up": nrm(ks[9], (L, GATE_LORA, RWKV_WIDTH), GATE_LORA ** -0.5),
        "k_k": 0.85 + nrm(ks[10], (L, RWKV_WIDTH), 0.05),
        "k_a": 1.0 + nrm(ks[11], (L, RWKV_WIDTH), 0.05),
        "r_k": nrm(ks[12], (L, RWKV_HEADS, RWKV_HEAD), 0.1),
        "lnx_w": 1.0 + nrm(ks[13], (L, RWKV_WIDTH), 0.05),
        "lnx_b": nrm(ks[14], (L, RWKV_WIDTH), 0.02),
        "lam_q1": nrm(ks[15], (L, DIFF_QKDIM), 0.1),
        "lam_k1": nrm(ks[16], (L, DIFF_QKDIM), 0.1),
        "lam_q2": nrm(ks[17], (L, DIFF_QKDIM), 0.1),
        "lam_k2": nrm(ks[18], (L, DIFF_QKDIM), 0.1),
        "subln_w": 1.0 + nrm(ks[19], (L, DIFF_VDIM), 0.05),
        "w_out": nrm(ks[20], (L, D_MIX, D_MODEL), D_MIX ** -0.5),
        "norm_mem_w": 1.0 + nrm(ks[21], (L, D_MODEL), 0.05),
        "norm_src_w": 1.0 + nrm(ks[22], (L, D_MODEL), 0.05),
        "w_mq": nrm(ks[23], (L, D_MODEL, D_MODEL), D_MODEL ** -0.5),
        "w_mk": nrm(ks[24], (L, D_MODEL, D_MODEL), D_MODEL ** -0.5),
        "w_mv": nrm(ks[25], (L, D_MODEL, D_MODEL), D_MODEL ** -0.5),
        "w_mo": nrm(ks[26], (L, D_MODEL, D_MODEL), D_MODEL ** -0.5),
        "norm_mlp_w": 1.0 + nrm(ks[27], (L, D_MODEL), 0.05),
        "w_up": nrm(ks[28], (L, D_MODEL, D_FF), D_MODEL ** -0.5),
        "w_down": nrm(ks[29], (L, D_FF, D_MODEL), D_FF ** -0.5),
        "norm_final_w": 1.0 + nrm(ks[30], (D_MODEL,), 0.05),
    }

def first_block(x, mem, norm_mix_w, w_in, mu_shift, w_decay0, w_decay_up, a0, a_up, g_up,
              k_k, k_a, r_k, lnx_w, lnx_b, lam_q1, lam_k1, lam_q2, lam_k2, subln_w, w_out,
              norm_mem_w, norm_src_w, w_mq, w_mk, w_mv, w_mo, norm_mlp_w, w_up, w_down,
              norm_final_w):
    h = x
    for l in range(DEPTH):
        lam_init = 0.8 - 0.6 * math.exp(-0.3 * l)
        proj = rms_norm(h, norm_mix_w[l]) @ w_in[l]
        p_rwkv, p_diff = proj[..., :RWKV_COLS], proj[..., RWKV_COLS:]
        y_rwkv = rwkv7_group(p_rwkv, mu_shift[l], w_decay0[l], w_decay_up[l], a0[l], a_up[l],
                             g_up[l], k_k[l], k_a[l], r_k[l], lnx_w[l], lnx_b[l])
        y_diff = diff_attn_group(p_diff, lam_q1[l], lam_k1[l], lam_q2[l], lam_k2[l],
                                 subln_w[l], lam_init)
        h = h + jnp.concatenate([y_rwkv, y_diff], axis=-1) @ w_out[l]
        h = h + memory_cross_attn(rms_norm(h, norm_mem_w[l]), rms_norm(mem, norm_src_w[l]),
                                  w_mq[l], w_mk[l], w_mv[l], w_mo[l])
        hn = rms_norm(h, norm_mlp_w[l])
        h = h + jnp.square(jax.nn.relu(hn @ w_up[l])) @ w_down[l]
    return rms_norm(h, norm_final_w)


DEPTH_2 = 2

HEAD_DIM = 128
EPS = 1e-6
N_HEADS_A = 4
A_WIDTH = N_HEADS_A * HEAD_DIM
IDX_HEADS = 8
IDX_DIM = 64
IDX_TOPK_MAX = 256
N_HEADS_B = 4
GLA_DK = 64
GLA_DV = 128
GLA_GATE_RANK = 16
GLA_TAU = 16.0
B_WIDTH = N_HEADS_B * GLA_DV
N_HEADS_C = 8
C_WIDTH = N_HEADS_C * HEAD_DIM
SB_QBLOCK = 128
ROPE_THETA = 500000.0
ROPE_FRACTION = 4
D_FF_2 = 4 * D_MODEL
N_EVEN = (DEPTH_2 + 1) // 2
N_ODD = DEPTH_2 // 2
AB_SIZES = (
    A_WIDTH, A_WIDTH, A_WIDTH,
    IDX_HEADS * IDX_DIM, IDX_DIM, IDX_HEADS,
    N_HEADS_B * GLA_DK, N_HEADS_B * GLA_DK,
    B_WIDTH,
    GLA_GATE_RANK,
    B_WIDTH,
)
AB_PROJ = sum(AB_SIZES)


def _split(a, sizes):
    out, o = [], 0
    for s in sizes:
        out.append(a[..., o:o + s])
        o += s
    return out

def rmsnorm(x, g):
    xf = x.astype(jnp.float32)
    y = xf * lax.rsqrt(jnp.mean(xf * xf, axis=-1, keepdims=True) + EPS)
    return (y * g.astype(jnp.float32)).astype(x.dtype)

def rope_partial(x, pos):
    d = x.shape[-1]
    rot = d // ROPE_FRACTION
    half = rot // 2
    inv = jnp.power(ROPE_THETA, -jnp.arange(half, dtype=jnp.float32) * 2.0 / rot)
    ang = pos.astype(jnp.float32)[:, None] * inv[None, :]
    cos = jnp.cos(ang)[None, :, None, :]
    sin = jnp.sin(ang)[None, :, None, :]
    xf = x.astype(jnp.float32)
    x1, x2, rest = xf[..., :half], xf[..., half:rot], xf[..., rot:]
    out = jnp.concatenate([x1 * cos - x2 * sin, x2 * cos + x1 * sin, rest], axis=-1)
    return out.astype(x.dtype)

def dsa_attention(q, k, v, iq, ik, iw):
    bsz, s_len, n_h, d_h = q.shape
    topk = min(IDX_TOPK_MAX, s_len // 4)
    n_blk = s_len // CHUNK
    key_pos = jnp.arange(s_len)

    def blk_fn(args):
        c, qb, iqb, iwb = args
        logits = jnp.einsum('bthd,bsd->bths', iqb, ik).astype(jnp.float32) * IDX_DIM ** -0.5
        score = jnp.einsum('bths,bth->bts', jax.nn.relu(logits),
                           iwb.astype(jnp.float32) * IDX_HEADS ** -0.5)
        limit = (c + 1) * CHUNK
        score = jnp.where((key_pos < limit)[None, None, :], score, -jnp.inf)
        _, idx = lax.top_k(score, topk)
        valid = idx < limit
        ks = jax.vmap(lambda a, i: a[i])(k, idx)
        vs = jax.vmap(lambda a, i: a[i])(v, idx)
        s = jnp.einsum('bthd,btkhd->bthk', qb, ks).astype(jnp.float32) * HEAD_DIM ** -0.5
        s = jnp.where(valid[:, :, None, :], s, -jnp.inf)
        p = jax.nn.softmax(s, axis=-1)
        return jnp.einsum('bthk,btkhd->bthd', p.astype(v.dtype), vs)

    def to_blocks(a):
        return a.reshape(bsz, n_blk, CHUNK, *a.shape[2:]).swapaxes(0, 1)

    out = lax.map(blk_fn, (jnp.arange(n_blk), to_blocks(q), to_blocks(iq), to_blocks(iw)))
    return out.swapaxes(0, 1).reshape(bsz, s_len, n_h, d_h)

def gla_chunked(q, k, v, lg):
    bsz, s_len, n_h, dk = q.shape
    dv = v.shape[-1]
    n_c = s_len // CHUNK
    causal = jnp.tril(jnp.ones((CHUNK, CHUNK), dtype=bool))

    def chunks(a):
        return a.astype(jnp.float32).reshape(bsz, n_c, CHUNK, n_h, a.shape[-1]).transpose(1, 0, 3, 2, 4)

    def step(state, inp):
        qc, kc, vc, gc = inp
        b = jnp.cumsum(gc, axis=2)
        o_inter = jnp.einsum('bhtd,bhde->bhte', qc * jnp.exp(b), state)
        diff = b[:, :, :, None, :] - b[:, :, None, :, :]
        decay = jnp.exp(jnp.where(causal[:, :, None], diff, -jnp.inf))
        att = jnp.einsum('bhtd,bhsd,bhtsd->bhts', qc, kc, decay)
        o = o_inter + jnp.einsum('bhts,bhse->bhte', att, vc)
        b_last = b[:, :, -1:, :]
        state = (jnp.exp(b_last[:, :, 0, :])[..., None] * state
                 + jnp.einsum('bhsd,bhse->bhde', kc * jnp.exp(b_last - b), vc))
        return state, o

    s0 = jnp.zeros((bsz, n_h, dk, dv), jnp.float32)
    _, o = lax.scan(step, s0, (chunks(q), chunks(k), chunks(v), chunks(lg)))
    return o.transpose(1, 0, 3, 2, 4).reshape(bsz, s_len, n_h, dv)

def stick_breaking(q, k, v):
    bsz, s_len, n_h, d_h = q.shape
    n_blk = s_len // SB_QBLOCK
    key_pos = jnp.arange(s_len)

    def blk_fn(args):
        i, qb = args
        z = jnp.einsum('bthd,bshd->bhts', qb, k).astype(jnp.float32) * d_h ** -0.5
        t_pos = i * SB_QBLOCK + jnp.arange(SB_QBLOCK)
        mask = key_pos[None, :] < t_pos[:, None]
        lo = jnp.where(mask, jax.nn.log_sigmoid(-z), 0.0)
        rc = lax.cumsum(lo, axis=3, reverse=True)
        log_a = jax.nn.log_sigmoid(z) + (rc - lo)
        a = jnp.where(mask, jnp.exp(log_a), 0.0)
        return jnp.einsum('bhts,bshd->bthd', a.astype(v.dtype), v)

    qb = q.reshape(bsz, n_blk, SB_QBLOCK, n_h, d_h).swapaxes(0, 1)
    out = lax.map(blk_fn, (jnp.arange(n_blk), qb))
    return out.swapaxes(0, 1).reshape(bsz, s_len, n_h, d_h)

def mixer_ab(n, pos, w_in, gq, gk, w_gate_up, b_gate, g_gla, w_out):
    bsz, s_len, _ = n.shape
    proj = n @ w_in
    (qa, ka, va, iq, ik, iw, qb, kb, vb, g_low, og) = _split(proj, AB_SIZES)
    qa = rope_partial(rmsnorm(qa.reshape(bsz, s_len, N_HEADS_A, HEAD_DIM), gq), pos)
    ka = rope_partial(rmsnorm(ka.reshape(bsz, s_len, N_HEADS_A, HEAD_DIM), gk), pos)
    va = va.reshape(bsz, s_len, N_HEADS_A, HEAD_DIM)
    iq = rope_partial(iq.reshape(bsz, s_len, IDX_HEADS, IDX_DIM), pos)
    ik = rope_partial(ik[:, :, None, :], pos)[:, :, 0, :]
    oa = dsa_attention(qa, ka, va, iq, ik, iw).reshape(bsz, s_len, A_WIDTH)
    qb = qb.reshape(bsz, s_len, N_HEADS_B, GLA_DK) * GLA_DK ** -0.5
    kb = kb.reshape(bsz, s_len, N_HEADS_B, GLA_DK)
    vb = vb.reshape(bsz, s_len, N_HEADS_B, GLA_DV)
    gate = (g_low @ w_gate_up + b_gate).astype(jnp.float32)
    lg = (jax.nn.log_sigmoid(gate) / GLA_TAU).reshape(bsz, s_len, N_HEADS_B, GLA_DK)
    ob = gla_chunked(qb, kb, vb, lg).astype(n.dtype)
    ob = rmsnorm(ob, g_gla).reshape(bsz, s_len, B_WIDTH) * jax.nn.silu(og)
    return jnp.concatenate([oa, ob], axis=-1) @ w_out

def mixer_c(n, w_in, gq, gk, w_out):
    bsz, s_len, _ = n.shape
    q, k, v = _split(n @ w_in, (C_WIDTH, C_WIDTH, C_WIDTH))
    q = rmsnorm(q.reshape(bsz, s_len, N_HEADS_C, HEAD_DIM), gq)
    k = rmsnorm(k.reshape(bsz, s_len, N_HEADS_C, HEAD_DIM), gk)
    v = v.reshape(bsz, s_len, N_HEADS_C, HEAD_DIM)
    return stick_breaking(q, k, v).reshape(bsz, s_len, C_WIDTH) @ w_out

def squared_relu_mlp(n, w_up, w_down):
    return jnp.square(jax.nn.relu(n @ w_up)) @ w_down

def second_inputs(seed: int = 0) -> dict:
    key = jax.random.key(seed)
    ks = jax.random.split(key, 16)
    f32 = jnp.float32

    def w(k, shape, fan_in):
        return jax.random.normal(k, shape, f32) * fan_in ** -0.5

    def gain(k, shape):
        return 1.0 + 0.02 * jax.random.normal(k, shape, f32)

    return {
        "x": jax.random.normal(ks[0], (BATCH, SEQ, D_MODEL), f32),
        "g_mix": gain(ks[1], (DEPTH_2, D_MODEL)),
        "g_ffn": gain(ks[2], (DEPTH_2, D_MODEL)),
        "w_in_ab": w(ks[3], (N_EVEN, D_MODEL, AB_PROJ), D_MODEL),
        "gq_a": gain(ks[4], (N_EVEN, HEAD_DIM)),
        "gk_a": gain(ks[5], (N_EVEN, HEAD_DIM)),
        "w_gate_up": w(ks[6], (N_EVEN, GLA_GATE_RANK, N_HEADS_B * GLA_DK), GLA_GATE_RANK),
        "b_gate": 0.1 * jax.random.normal(ks[7], (N_EVEN, N_HEADS_B * GLA_DK), f32),
        "g_gla": gain(ks[8], (N_EVEN, GLA_DV)),
        "w_out_ab": w(ks[9], (N_EVEN, A_WIDTH + B_WIDTH, D_MODEL), A_WIDTH + B_WIDTH),
        "w_in_c": w(ks[10], (N_ODD, D_MODEL, 3 * C_WIDTH), D_MODEL),
        "gq_c": gain(ks[11], (N_ODD, HEAD_DIM)),
        "gk_c": gain(ks[12], (N_ODD, HEAD_DIM)),
        "w_out_c": w(ks[13], (N_ODD, C_WIDTH, D_MODEL), C_WIDTH),
        "w_up": w(ks[14], (DEPTH_2, D_MODEL, D_FF_2), D_MODEL),
        "w_down": w(ks[15], (DEPTH_2, D_FF_2, D_MODEL), D_FF_2),
    }

def second_block(x, g_mix, g_ffn, w_in_ab, gq_a, gk_a, w_gate_up, b_gate, g_gla, w_out_ab,
              w_in_c, gq_c, gk_c, w_out_c, w_up, w_down):
    pos = jnp.arange(x.shape[1])
    h = x
    for layer in range(DEPTH_2):
        n = rmsnorm(h, g_mix[layer])
        if layer % 2 == 0:
            i = layer // 2
            h = h + mixer_ab(n, pos, w_in_ab[i], gq_a[i], gk_a[i], w_gate_up[i],
                             b_gate[i], g_gla[i], w_out_ab[i])
        else:
            i = layer // 2
            h = h + mixer_c(n, w_in_c[i], gq_c[i], gk_c[i], w_out_c[i])
        h = h + squared_relu_mlp(rmsnorm(h, g_ffn[layer]), w_up[layer], w_down[layer])
    return h


def setup_inputs(seed=0):
    out = dict(first_inputs(seed))
    for name, value in second_inputs(seed + 1).items():
        if name != "x":
            out[name + "_2"] = value
    return out


def reference(
    x, mem, norm_mix_w, w_in, mu_shift, w_decay0, w_decay_up, a0, a_up, g_up, k_k, k_a, r_k,
    lnx_w, lnx_b, lam_q1, lam_k1, lam_q2, lam_k2, subln_w, w_out, norm_mem_w, norm_src_w, w_mq,
    w_mk, w_mv, w_mo, norm_mlp_w, w_up, w_down, norm_final_w, g_mix_2, g_ffn_2, w_in_ab_2,
    gq_a_2, gk_a_2, w_gate_up_2, b_gate_2, g_gla_2, w_out_ab_2, w_in_c_2, gq_c_2, gk_c_2,
    w_out_c_2, w_up_2, w_down_2,
):
    x = first_block(
        x, mem, norm_mix_w, w_in, mu_shift, w_decay0, w_decay_up, a0, a_up, g_up, k_k, k_a, r_k,
        lnx_w, lnx_b, lam_q1, lam_k1, lam_q2, lam_k2, subln_w, w_out, norm_mem_w, norm_src_w,
        w_mq, w_mk, w_mv, w_mo, norm_mlp_w, w_up, w_down, norm_final_w,
    )
    return second_block(
        x, g_mix_2, g_ffn_2, w_in_ab_2, gq_a_2, gk_a_2, w_gate_up_2, b_gate_2, g_gla_2,
        w_out_ab_2, w_in_c_2, gq_c_2, gk_c_2, w_out_c_2, w_up_2, w_down_2,
    )


_drawn_inputs = setup_inputs


def setup_inputs(seed=0):
    import zlib

    import numpy as np

    out = dict(_drawn_inputs(seed))
    spreads = {}
    factors = {'a0': 2.705,
     'k_k': 2.719,
     'lnx_b': 4.222,
     'norm_mem_w': 6.081,
     'norm_src_w': 4.614,
     'gq_a_2': 8.0,
     'gk_a_2': 8.0,
     'g_gla_2': 6.909,
     'gq_c_2': 8.0,
     'gk_c_2': 8.0}
    for name, (base, spread) in spreads.items():
        noise = np.random.default_rng([zlib.crc32(name.encode()), seed]).standard_normal(out[name].shape)
        drawn = base * np.exp(spread * noise) if base else spread * noise
        out[name] = __import__('jax').numpy.asarray(drawn.astype(out[name].dtype))
    for name, factor in factors.items():
        out[name] = (out[name] * factor).astype(out[name].dtype)
    return out
```

```python
from contextlib import ExitStack
import math
import numpy as np
import concourse.bass as bass
from concourse import mybir

F32 = mybir.dt.float32
ACT = mybir.ActivationFunctionType
ALU = mybir.AluOpType
AX = mybir.AxisListType

P = 128
S = 512
KT = 8
TT = S // P
MEM = 256
RING = 8
DEC = math.exp(-0.5)
NEG = -1.0e30

STREAM = [("rwkv_lora", 2), ("rwkv_k", 4), ("rwkv_r", 4), ("rwkv_v", 4),
          ("diff_q", 4), ("diff_k", 4), ("diff_v", 4), ("out", 8),
          ("mem_k", 8), ("mem_v", 8), ("mem_q", 8), ("mem_o", 8), ("up", 32), ("down", 32),
          ("i_q", 4), ("i_k", 1), ("misc", 1), ("b_q", 2), ("b_k", 2),
          ("a_q", 4), ("a_k", 4), ("a_v", 4), ("b_v", 4), ("b_og", 4), ("out_ab", 8),
          ("up_0", 32), ("down_0", 32),
          ("c_q", 8), ("c_k", 8), ("c_v", 8), ("out_c", 8), ("up_1", 32), ("down_1", 32)]
UNIT = {}
UNITS = 0
for _name, _n in STREAM:
    UNIT[_name] = UNITS
    UNITS += _n
STREAM_UNITS = -(-UNITS // RING) * RING

CONSTS = [("ident", 128), ("ones", 128), ("bd_ones", 128), ("rope_a", 128), ("rope_i", 128),
          ("cos_a", 512), ("sin_a", 512), ("cos_i", 512), ("sin_i", 512),
          ("reset64", 512), ("reset128", 512),
          ("bd_strict", 128), ("bd_incl", 128), ("low_mask", 6 * 128), ("gla_mask", 8 * 128),
          ("chunk_bias", 64), ("strict", 128), ("strict_bias", 128), ("scalars", 8)]
CO = {}
N_CONST = 0
for _name, _n in CONSTS:
    CO[_name] = (N_CONST, _n)
    N_CONST += _n

VECS = [("norm_mix", 8), ("norm_mem", 8), ("norm_src", 8), ("norm_mlp", 8), ("norm_final", 8),
        ("g_mix0", 8), ("g_ffn0", 8), ("g_mix1", 8), ("g_ffn1", 8),
        ("mu", 14), ("w0", 4), ("a0", 4), ("k_k", 4), ("k_a", 4), ("r_k", 4), ("lnx_w", 4), ("lnx_b", 4),
        ("lam", 4), ("subln", 1), ("gq_a", 1), ("gk_a", 1), ("gq_c", 1), ("gk_c", 1), ("g_gla", 1),
        ("b_gate", 2), ("dec_aaa_up", 512), ("g_up", 512), ("gate_up", 256)]
VO = {}
N_VEC = 0
for _name, _n in VECS:
    VO[_name] = (N_VEC, _n)
    N_VEC += _n

RMS_EPS, EPS2, GN_EPS = 1e-5, 1e-6, 64e-5
SC = {"eps1": 0, "eps2": 1, "gn": 2, "kkb": 3, "one": 4}
KK_SCALE = 65536.0


def constants():
    c = np.zeros((P, N_CONST), np.float32)

    def put(name, a):
        o, n = CO[name]
        c[:, o:o + n] = a.reshape(P, n)
    i = np.arange(P)
    row, col = i[:, None], i[None, :]
    put("ident", np.eye(P))
    put("ones", np.ones((P, P)))
    put("bd_ones", (row // 64 == col // 64) * 1.0)
    t = np.arange(S)

    def rope(name, head, width):
        rot = width // 4
        half = rot // 2
        inv = np.power(500000.0, -np.arange(half, dtype=np.float32) * 2.0 / rot).astype(np.float32)
        ang = t.astype(np.float32)[None, :] * inv[:, None]
        cos, sin, m = np.ones((P, S)), np.zeros((P, S)), np.zeros((P, P))
        for base in range(0, P, width):
            for j in range(half):
                cos[base + j] = cos[base + half + j] = np.cos(ang[j])
                sin[base + j] = sin[base + half + j] = np.sin(ang[j])
                m[base + half + j, base + j] = -1.0
                m[base + j, base + half + j] = 1.0
        put("cos_" + name, cos)
        put("sin_" + name, sin)
        put("rope_" + name, m)
    rope("a", 0, 128)
    rope("i", 0, 64)
    put("reset64", np.broadcast_to((t % 64 != 0) * 1.0, (P, S)))
    put("reset128", np.broadcast_to((t % 128 != 0) * 1.0, (P, S)))
    same = row // 64 == col // 64
    put("bd_strict", (same & (row < col)) * 1.0)
    put("bd_incl", (same & (row <= col)) * 1.0)
    low = [((row // (2 * s) == col // (2 * s)) & (row % (2 * s) >= s) & (col % (2 * s) < s)) * 1.0
           for s in (1, 2, 4, 8, 16, 32)]
    put("low_mask", np.concatenate(low, 1))
    gla = [((row // (2 * s) == col // (2 * s)) & (col % (2 * s) >= s) & (row % (2 * s) < s)) * 1.0
           for s in (1, 2, 4, 8, 16, 32, 64)] + [(row == col) * 1.0]
    put("gla_mask", np.concatenate(gla, 1))
    put("chunk_bias", np.broadcast_to(np.where(row < 64, NEG, 0.0), (P, 64)))
    put("strict", (col < row) * 1.0)
    put("strict_bias", np.where(col < row, 0.0, NEG))
    s = np.zeros((P, 8))
    s[:, SC["eps1"]], s[:, SC["eps2"]], s[:, SC["gn"]] = RMS_EPS, EPS2, GN_EPS
    s[:, SC["kkb"]] = 0.5 * math.log(KK_SCALE)
    s[:, SC["one"]] = 1.0
    put("scalars", s)
    return c


class Count:

    def __init__(self, sems, own):
        self.sems, self.own, self.n, self.latest = sems, own, {}, None

    def inc(self, name=None):
        name = name or self.own
        self.n[name] = self.n.get(name, 0) + 1
        self.latest = (self.sems[name], self.n[name])
        return self.sems[name], 1


def build(nc, x_d, mem_d, w_d, c_d, v_d, out_d, stop=None):
    ctx = ExitStack()
    with ctx:
        def sb(name, shape):
            return ctx.enter_context(nc.sbuf_tensor(name, shape, F32))
        H = sb("H", [P, KT, S])
        HN = sb("HN", [P, KT, S])
        W = sb("W", [P, RING, KT * P])
        C = sb("C", [P, N_CONST])
        V = sb("V", [P, N_VEC])
        NA = 61
        AR = sb("AR", [P, NA, S])
        SM = sb("SM", [P, 192])
        PB = [ctx.enter_context(nc.psum_tensor(f"PB{i}", [P, S], F32)) for i in range(8)]

        names = ["w_used", "act_step", "dve_step", "pool_step", "stage", "x_in", "mem_in", "c_in", "v_in", "stored",
                 "norm_h", "norm_sq", "norm_acc", "norm_ms", "norm_rs", "norm_out",
                 "ev_act", "ev_dve", "lora_in", "kk_sq", "bonus_in", "prep_mm", "prep_act", "prep_dve",
                 "sig_ready", "a_ready", "kkln_in", "kk_rs", "cs_ready", "exp_ready", "exp_used", "lam_in", "lam_mm", "lam_exp",
                 "sc_mm", "sc_max", "sc_exp", "prob", "tr_mm", "tr_ev", "pv_mm", "o_ev",
                 "on_sq", "on_mm", "on_rs", "on_out",
                 "ch_in", "ch_tr", "ch_trev", "ch_aq", "ch_aqev", "ch_t0", "ch_t0ev", "lv_x", "lv_xev", "lv_y", "lv_yev",
                 "w1_mm", "w1_ev", "kv_mm", "g_ev", "sa_mm", "sa_ev", "gu_mm", "y_mm", "y_ev",
                 "gn_in", "gn_mm", "gn_c", "gn_sq", "gn_rs", "mix_out",
                 "relu", "mlp_a",
                 "rope_mm", "rope_ev", "iw_tr", "iw_ev", "gate_mm", "gate_in", "gate_ln", "gb_ready", "idx_mm", "idx_r", "idx_acc",
                 "a_sq", "a_mm", "a_rs", "a_sc", "lv_d", "lv_e", "lv_in", "lvl_mm", "lvl_ev", "att",
                 "g_eb", "g_ed", "g_ede", "ke_in", "ke_tr", "ke_ev", "kv2_mm", "sh_ev", "go_mm", "go_sq", "go_nm", "go_rs", "go_ev",
                 "c_sq", "c_nm", "c_rs", "c_sc", "c_l", "c_nl", "c_la", "c_prob"]
        sems = {n: ctx.enter_context(nc.semaphore(n)) for n in names}
        slot_loaded = [ctx.enter_context(nc.semaphore(f"slot_loaded{i}")) for i in range(RING)]

        def cst(name, a=0, b=None):
            o, n = CO[name]
            return C[:, o + a:o + (n if b is None else b)]

        def vec(name, a=0, b=None):
            o, n = VO[name]
            return V[:, o + a:o + (n if b is None else b)]

        def sc(name):
            return cst("scalars", SC[name], SC[name] + 1)

        flat = AR[:, :, :].rearrange("p a n -> p (a n)")
        PW = S + 1
        PX = flat[:, 0:14 * PW].rearrange("p (m n) -> p m n", n=PW)
        LORA, GD, K0, R0, V0 = 0, 1, 2, 6, 10
        SIG, CS, AG, KK, BON, GT = (AR[:, a:a + 4, :] for a in (15, 19, 23, 27, 31, 35))
        TMP = AR[:, 39:41, :]
        DQ, DK, DV = (AR[:, a:a + 4, :] for a in (41, 45, 49))
        SQ, ACC, LN, RS = AR[:, 48:56, :], AR[:, 56, :], AR[:, 57, :], AR[:, 58, :]
        PR1, PR2, PT, OSQ, OLN = AR[:, 53:55, :], AR[:, 55:57, :], AR[:, 57:59, :], AR[:, 59, :], AR[:, 60, :]
        MA, RL = AR[:, 0:32, :], AR[:, 32:34, :]

        STEPS = {"diff": [(h, t) for h in range(4) for t in range(TT)],
                 "mem": [(h, t) for h in range(4) for t in range(TT)],
                 "A": [(h, t) for t in range(TT) for h in range(4)],
                 "C": [(h, t) for h in range(8) for t in range(TT)]}
        MAPS = {"diff": 2, "mem": 1, "A": 1, "C": 0}
        BASE, EXPB, s0, e0 = {}, {}, 0, 0
        for a in STEPS:
            BASE[a], EXPB[a] = s0, e0
            s0 += len(STEPS[a])
            e0 += len(STEPS[a]) * MAPS[a]
        PIPE = 3
        N_MIX, N_SRC, N_MEM, N_MLP, N_FINAL, N_MIX0, N_FFN0, N_MIX1, N_FFN1 = range(9)
        RES = {N_MEM: 0, N_MLP: 8, N_FINAL: 16, N_FFN0: 24, N_MIX1: 32, N_FFN1: 40, None: 48}

        LAMP, LAME, NLAM, SUBW, KA1 = SM[:, 0:2], SM[:, 2:4], SM[:, 4:5], SM[:, 5:6], SM[:, 6:10]
        ECH = SM[:, 16:48].rearrange("p (a c) -> p a c", c=8)

        def nmax(i, m=0, n=1):
            return SM[:, 48 + 2 * (i % 4) + m:48 + 2 * (i % 4) + m + n]

        def psum_of(i, m=0, n=1):
            return SM[:, 56 + 2 * (i % 4) + m:56 + 2 * (i % 4) + m + n]

        def recip(i, m=0, n=1):
            return SM[:, 64 + 2 * (i % 4) + m:64 + 2 * (i % 4) + m + n]

        def tile(t):
            return slice(t * P, (t + 1) * P)

        def pk(a, n=1, w=None):
            return AR[:, a:a + n, :].rearrange("p a (h n) -> p (a h) n", n=w)
        AQ, BQ = pk(41, 4, 256), pk(45, 4, 256)
        TI, UI, XI = pk(49, 2, 128), pk(51, 2, 128), pk(53, 2, 128)
        TOKA, TOKB, TOKK, TOKV = (pk(a, 1, 128) for a in (55, 56, 57, 58))
        BP, KP = pk(59, 1, 128), pk(60, 1, 128)
        TA, W1, SA, P1 = pk(39, 1, 128), pk(40, 1, 128), pk(18, 1, 128), pk(14 + 7, 1, 128)
        GS = [pk(a, 1, 128) for a in (15, 16, 17)]
        TG = pk(19, 1, 128)

        mview = AR[:, 0:8, :].rearrange("p a (b m) -> p (a b) m", m=MEM)
        MT, MN = mview[:, 0:8, :], mview[:, 8:16, :]
        MK = AR[:, 8:12, :].rearrange("p a (b m) -> p (a b) m", m=MEM)
        MV = AR[:, 12:16, :].rearrange("p (t a) n -> p t (a n)", t=2)
        MQ, MO = AR[:, 16:24, :], AR[:, 24:32, :]
        MPR, MPT = AR[:, 32:34, :], AR[:, 34:36, :]



        IQ, IK, MISC = AR[:, 0:4, :], AR[:, 4, :], AR[:, 5, :]
        QA, KA, VA = AR[:, 6:10, :], AR[:, 10:14, :], AR[:, 14:18, :]
        GQ, GK, GV, OG = AR[:, 18:20, :], AR[:, 20:22, :], AR[:, 22:26, :], AR[:, 26:30, :]
        SCORE, WORK, RLU, T1 = AR[:, 30:34, :], AR[:, 34, :], AR[:, 35:37, :], AR[:, 37, :]
        SQA, RA, GB = AR[:, 38:40, :], AR[:, 40:42, :], AR[:, 42:44, :]
        GE = [AR[:, 44:46, :], AR[:, 46:48, :]]
        GQE, GKE, ATT, LV = AR[:, 48:50, :], AR[:, 50:52, :], AR[:, 52:56, :], AR[:, 56:60, :]
        GEB, GED = AR[:, 0:2, :], AR[:, 2:4, :]
        GKT = AR[:, 56:58, :].rearrange("p a (t n) -> p (a t) n", n=256)
        GSH = AR[:, 58:60, :].rearrange("p a (t n) -> p (a t) n", n=256)
        GSQ = AR[:, 44:48, :]
        APR, APT = AR[:, 35:37, :], AR[:, 38:40, :]
        EQ, PRE = AR[:, 37, :], AR[:, 40, :]
        IW = SM[:, 80:112].rearrange("p (t h) -> p t h", h=8)
        TOP = SM[:, 112:120]
        NGT = SM[:, 120:121]
        GQS, GCS = SM[:, 121:122], SM[:, 122:123]
        EV2 = 50
        EV3 = EV2 + 30
        LEVELS = [None, 1, 2, 4, 8, 16, 32, 64]
        INDEX_STEPS = [(t, h) for t in range(1, TT) for h in range(8)]

        def rope_plane(j):
            return IQ[:, j, :] if j < 4 else IK if j == 4 else QA[:, j - 5, :] if j < 9 else KA[:, j - 9, :]

        CQ, CK, CV = AR[:, 0:8, :], AR[:, 8:16, :], AR[:, 16:24, :]
        CL, CN, CR, CPR, CPT = (AR[:, a:a + 2, :] for a in (24, 26, 28, 30, 32))
        CSQ, CRS = AR[:, 34:36, :], AR[:, 36:38, :]
        def PT_of(name):
            return {"diff": PT, "mem": MPT, "A": APT, "C": CPT}[name]

        block = ctx.enter_context(nc.Block())

        @block.sync
        def _(sp):
            sp.dma_start(C[:, :], c_d).then_inc(sems["c_in"], 16)
            for j in range(RING):
                sp.dma_start(W[:, j, :], w_d[j, :, :]).then_inc(slot_loaded[j], 16)
            with sp.Fori(1, STREAM_UNITS // RING) as i:
                for j in range(RING):
                    sp.wait_ge(sems["w_used"], i * RING + (j - RING + 1))
                    sp.dma_start(W[:, j, :], w_d[bass.ds(i * RING + j, 1), :, :].rearrange("a p n -> p (a n)"))\
                        .then_inc(slot_loaded[j], 16)
            for k in range(KT):
                sp.wait_ge(sems["norm_h"], RES[None] + k + 1)
                sp.dma_start(out_d[:, k, :], H[:, k, :]).then_inc(sems["stored"], 16)
            sp.wait_ge(sems["stored"], 16 * KT)

        @block.gpsimd
        def _(pool):
            def rel(l, dst):
                s = LEVELS[l]
                g = GB.rearrange("p a (g n) -> p (a g) n", n=2 * s)
                return pool.tensor_tensor(dst.rearrange("p a (g n) -> p (a g) n", n=2 * s), g,
                                          g[:, :, s - 1:s].to_broadcast([P, 1024 // (2 * s), 2 * s]), ALU.subtract)
            pool.wait_ge(sems["gb_ready"], 1)
            rel(1, GE[1]).then_inc(sems["lv_d"], 1)
            for l in range(1, 8):
                if l < 7:
                    if l >= 2:
                        pool.wait_ge(sems["lv_in"], 2 * (l - 1))
                    rel(l + 1, GE[(l + 1) % 2]).then_inc(sems["lv_d"], 1)
                pool.wait_ge(sems["lv_e"], l)
                if l >= 2:
                    pool.wait_ge(sems["lvl_mm"], 4 * l)
                pool.tensor_tensor(GQE, GQ, GE[l % 2], ALU.mult).then_inc(sems["lv_in"], 1)
                pool.tensor_tensor(GKE, GK, GE[l % 2], ALU.mult).then_inc(sems["lv_in"], 1)
            b3 = GB.rearrange("p a (t n) -> p (a t) n", n=P)
            pool.wait_ge(sems["idx_mm"], 24)
            pool.tensor_tensor(GED.rearrange("p a (t n) -> p (a t) n", n=P), b3[:, :, P - 1:P].to_broadcast([P, 8, P]), b3,
                               ALU.subtract).then_inc(sems["g_ed"], 1)
            pool.wait_ge(sems["lvl_mm"], 32)
            pool.wait_ge(sems["g_ede"], 1)
            pool.tensor_tensor(GKE, GK, GED, ALU.mult).then_inc(sems["ke_in"], 1)
            pool.wait_ge(sems["g_eb"], 1)
            pool.tensor_tensor(GQE, GQ, GEB, ALU.mult).then_inc(sems["ke_in"], 1)

        @block.scalar
        def _(act):
            A = Count(sems, "act_step")
            ends = [0]

            def end_stage():
                ends[0] += 1
                act.drain().then_inc(sems["stage"], 1)
                act.wait_ge(sems["stage"], 3 * ends[0])

            def f(out, in_, func, **k):
                return act.activation(out, in_, func, **k)

            def rstd(n, eps, w=S):
                act.wait_ge(sems["norm_ms"], n + 1)
                f(LN[:, 0:w], PB[4][:, 0:w], ACT.Ln, scale=1.0 / 1024, bias=sc(eps)).then_inc(*A.inc())
                act.wait_ge(*A.latest)
                f(RS[:, 0:w], LN[:, 0:w], ACT.Exp, scale=-0.5).then_inc(*A.inc("norm_rs"))

            def used(name, i):
                act.wait_ge(sems["w_used"], UNIT[name] + i + 1)

            act.dma_start(H[:, :, :], x_d).then_inc(sems["x_in"], 16)
            act.dma_start(V[:, :], v_d).then_inc(sems["v_in"], 16)
            act.wait_ge(sems["c_in"], 16)
            act.wait_ge(sems["v_in"], 16)
            act.wait_ge(sems["x_in"], 16)
            for k in range(KT):
                f(SQ[:, k, :], H[:, k, :], ACT.Square).then_inc(*A.inc("norm_sq"))
            act.wait_ge(sems["lam_mm"], 1)
            f(LAME, PB[7][:, 0:2], ACT.Exp).then_inc(*A.inc("lam_exp"))
            rstd(N_MIX, "eps1")

            for m in range(14):
                used("rwkv_lora", m)
                f(PX[:, m, 1:PW], PB[m % 4][:, :], ACT.Copy).then_inc(*A.inc("ev_act"))
                if m == 5:
                    act.wait_ge(sems["lora_in"], 2)
                    f(PX[0:64, LORA, 1:PW], PX[0:64, LORA, 1:PW], ACT.Tanh).then_inc(*A.inc())
                    f(PX[:, GD, 1:PW], PX[:, GD, 1:PW], ACT.Sigmoid).then_inc(*A.inc("sig_ready"))
            for p in range(4):
                act.wait_ge(sems["prep_mm"], p + 1)
                f(SIG[:, p, :], PB[4 + p][:, :], ACT.Sigmoid, bias=vec("w0", p, p + 1)).then_inc(*A.inc("prep_act"))
            for p in range(4):
                act.wait_ge(sems["prep_mm"], 4 + p + 1)
                f(AG[:, p, :], PB[4 + p][:, :], ACT.Sigmoid, bias=vec("a0", p, p + 1)).then_inc(*A.inc("prep_act"))
            for p in range(4):
                act.wait_ge(sems["prep_mm"], 8 + p + 1)
                f(GT[:, p, :], PB[4 + p][:, :], ACT.Copy).then_inc(*A.inc("prep_act"))
            for m in range(4):
                used("diff_q", m)
                f(DQ[:, m, :], PB[(14 + m) % 4][:, :], ACT.Copy, scale=0.125).then_inc(*A.inc("ev_act"))
            for p in range(4):
                act.wait_ge(sems["kkln_in"], p + 1)
                f(CS[:, p, :], CS[:, p, :], ACT.Ln).then_inc(*A.inc())
                act.wait_ge(*A.latest)
                f(CS[:, p, :], CS[:, p, :], ACT.Exp, scale=-0.5, bias=sc("kkb")).then_inc(*A.inc("kk_rs"))
            for m in range(4):
                used("diff_k", m)
                f(DK[:, m, :], PB[(18 + m) % 4][:, :], ACT.Copy).then_inc(*A.inc("ev_act"))
            for p in range(4):
                act.wait_ge(sems["cs_ready"], p + 1)
                f(SIG[:, p, :], SIG[:, p, :], ACT.Exp, scale=-DEC).then_inc(*A.inc("exp_ready"))
                if p >= 2:
                    act.wait_ge(sems["exp_used"], p - 1)
                f(TMP[:, p % 2, :], CS[:, p, :], ACT.Exp, scale=DEC).then_inc(*A.inc("exp_ready"))
                f(CS[:, p, :], CS[:, p, :], ACT.Exp, scale=-DEC).then_inc(*A.inc("exp_ready"))
            for m in range(4):
                used("diff_v", m)
                f(DV[:, m, :], PB[(22 + m) % 4][:, :], ACT.Copy).then_inc(*A.inc("ev_act"))

            def tr_evac(name, j, n):
                b = BASE[name]
                act.wait_ge(sems["tr_mm"], b + j + 1)
                if j >= 2:
                    act.wait_ge(sems["pv_mm"], b + j - 1)
                f(PT_of(name)[:, j % 2, 0:n * P], PB[0][:, 0:n * P], ACT.Copy).then_inc(*A.inc("tr_ev"))

            steps = STEPS["diff"]
            for i in range(len(steps) + PIPE + 2):
                if i < len(steps):
                    w = (steps[i][1] + 1) * P
                    act.wait_ge(sems["sc_max"], i + 1)
                    if i >= 2:
                        act.wait_ge(sems["tr_mm"], i - 1)
                    f(PR1[:, i % 2, 0:w], PB[4 + 2 * (i % 2)][:, 0:w], ACT.Exp, bias=nmax(i, 0), accum_out=psum_of(i, 0))\
                        .then_inc(*A.inc("sc_exp"))
                    f(PR2[:, i % 2, 0:w], PB[5 + 2 * (i % 2)][:, 0:w], ACT.Exp, bias=nmax(i, 1), accum_out=psum_of(i, 1))\
                        .then_inc(*A.inc("sc_exp"))
                if 2 <= i < len(steps) + 2:
                    tr_evac("diff", i - 2, steps[i - 2][1] + 1)
                j = i - PIPE
                if 0 <= j < len(steps) and steps[j][1] == TT - 1:
                    h = steps[j][0]
                    act.wait_ge(sems["pv_mm"], j + 1)
                    if h:
                        act.wait_ge(sems["on_mm"], h)
                    f(OSQ, PB[2 + h % 2][:, :], ACT.Square).then_inc(*A.inc("on_sq"))
                j = i - PIPE - 1
                if 0 <= j < len(steps) and steps[j][1] == TT - 1:
                    h = steps[j][0]
                    act.wait_ge(sems["on_mm"], h + 1)
                    if h:
                        act.wait_ge(sems["on_out"], h)
                    f(OLN, PB[1][:, :], ACT.Ln, scale=1.0 / P, bias=sc("eps1")).then_inc(*A.inc())
                    act.wait_ge(*A.latest)
                    f(OLN, OLN, ACT.Exp, scale=-0.5).then_inc(*A.inc("on_rs"))
            end_stage()

            for t in range(TT):
                for n, dst in enumerate((TOKA, TOKV, TOKB, TOKK)):
                    act.wait_ge(sems["ch_tr"], 4 * t + n + 1)
                    f(dst, PB[4 + n][:, :].rearrange("p (a n) -> p a n", n=P), ACT.Copy).then_inc(*A.inc("ch_trev"))
                act.wait_ge(sems["w1_mm"], 3 * t + 1)
                f(P1, PB[4][:, :].rearrange("p (a n) -> p a n", n=P), ACT.Copy).then_inc(*A.inc("w1_ev"))
                act.wait_ge(sems["w1_mm"], 3 * t + 2)
                f(TA, PB[5][:, :].rearrange("p (a n) -> p a n", n=P), ACT.Copy).then_inc(*A.inc("w1_ev"))
                act.wait_ge(sems["w1_mm"], 3 * t + 3)
                f(W1, PB[6][:, :].rearrange("p (a n) -> p a n", n=P), ACT.Copy, scale=-1.0).then_inc(*A.inc("w1_ev"))
                act.wait_ge(sems["y_mm"], t + 1)
                f(HN[:, 0:4, tile(t)], PB[7][:, :].rearrange("p (a n) -> p a n", n=P), ACT.Copy).then_inc(*A.inc("y_ev"))
                end_stage()
            for p in range(4):
                act.wait_ge(sems["gn_c"], p + 1)
                f(SIG[:, p, :], HN[:, p, :], ACT.Square).then_inc(*A.inc("gn_sq"))
            for p in range(4):
                act.wait_ge(sems["gn_mm"], 4 + p + 1)
                f(SIG[:, p, :], PB[4 + p][:, :], ACT.Ln, scale=1.0 / 64, bias=sc("gn")).then_inc(*A.inc())
                act.wait_ge(*A.latest)
                f(SIG[:, p, :], SIG[:, p, :], ACT.Exp, scale=-0.5).then_inc(*A.inc("gn_rs"))
            end_stage()

            act.dma_start(MT, mem_d).then_inc(sems["mem_in"], 16)
            act.wait_ge(sems["mem_in"], 16)
            for k in range(KT):
                f(SQ[:, k, 0:MEM], MT[:, k, :], ACT.Square).then_inc(*A.inc("norm_sq"))
            rstd(N_SRC, "eps1", MEM)
            for k in range(KT):
                act.wait_ge(sems["norm_h"], RES[N_MEM] + k + 1)
                f(SQ[:, k, :], H[:, k, :], ACT.Square).then_inc(*A.inc("norm_sq"))
            rstd(N_MEM, "eps1")
            for m in range(8):
                used("mem_k", m)
                f(MK[:, m, :], PB[m % 4][:, 0:MEM], ACT.Copy).then_inc(*A.inc("ev_act"))
            for m in range(8):
                used("mem_v", m)
                f(MV[:, :, tile(m)], PB[m % 4][:, 0:MEM].rearrange("p (t n) -> p t n", t=2), ACT.Copy)\
                    .then_inc(*A.inc("ev_act"))
            for m in range(8):
                used("mem_q", m)
                f(MQ[:, m, :], PB[m % 4][:, :], ACT.Copy, scale=1.0 / 16).then_inc(*A.inc("ev_act"))
            steps = STEPS["mem"]
            b = BASE["mem"]
            for i in range(len(steps) + PIPE):
                if i < len(steps):
                    act.wait_ge(sems["sc_max"], b + i + 1)
                    if i >= 2:
                        act.wait_ge(sems["tr_mm"], b + i - 1)
                    f(MPR[:, i % 2, 0:MEM], PB[4 + i % 2][:, 0:MEM], ACT.Exp, bias=nmax(i), accum_out=psum_of(i))\
                        .then_inc(*A.inc("sc_exp"))
                if 2 <= i < len(steps) + 2:
                    tr_evac("mem", i - 2, 2)
                if i >= PIPE:
                    h, t = steps[i - PIPE]
                    act.wait_ge(sems["pv_mm"], b + i - PIPE + 1)
                    f(MO[:, 2 * h:2 * h + 2, tile(t)], PB[2 + (i - PIPE) % 2][:, 0:MEM].rearrange("p (j n) -> p j n", j=2), ACT.Copy)\
                        .then_inc(*A.inc("o_ev"))
            for k in range(KT):
                act.wait_ge(sems["norm_h"], RES[N_MLP] + k + 1)
                f(SQ[:, k, :], H[:, k, :], ACT.Square).then_inc(*A.inc("norm_sq"))
            rstd(N_MLP, "eps1")
            end_stage()

            def mlp(n, up, nxt, eps):
                def tile_pair(i, j):
                    m = i * RING + j
                    act.wait_ge(sems["w_used"], UNIT[up] + 1 + m)
                    act.activation(RL[:, j % 2, :], PB[j % 4][:, :], ACT.Relu).then_inc(sems["relu"], 1)
                    act.wait_ge(sems["relu"], 32 * n + 1 + m)
                    act.activation(MA[:, m, :] if isinstance(m, int) else MA[:, bass.ds(m, 1), :].rearrange("p a n -> p (a n)"),
                                   RL[:, j % 2, :], ACT.Square).then_inc(sems["mlp_a"], 1)
                with act.Fori(0, 32 // RING) as i:
                    for j in range(RING):
                        tile_pair(i, j)
                if nxt is None:
                    return
                for k in range(KT):
                    act.wait_ge(sems["norm_h"], RES[nxt] + k + 1)
                    f(SQ[:, k, :], H[:, k, :], ACT.Square).then_inc(*A.inc("norm_sq"))
                rstd(nxt, eps)
            mlp(0, "up", N_FINAL, "eps1")

            for k in range(KT):
                act.wait_ge(sems["norm_out"], N_FINAL * KT + k + 1)
                f(SQ[:, k, :], H[:, k, :], ACT.Square).then_inc(*A.inc("norm_sq"))
            rstd(N_MIX0, "eps2")
            end_stage()

            def ev2(i, out, scale=1.0, func=ACT.Copy):
                act.wait_ge(sems["w_used"], UNIT["i_q"] + i + 1)
                f(out, PB[i % 2][:, :], func, scale=scale).then_inc(*A.inc("ev_act"))

            def head_rstd(j, bank, out, done, nm, nr):
                act.wait_ge(sems[nm], j + 1)
                if j >= 2:
                    act.wait_ge(sems[done], j - 1)
                f(out, PB[bank][:, :], ACT.Ln, scale=1.0 / P, bias=sc("eps2")).then_inc(*A.inc())
                act.wait_ge(*A.latest)
                f(out, out, ACT.Exp, scale=-0.5).then_inc(*A.inc(nr))
            for i in range(30):
                dst, s_ = ((IQ[:, i, :], 1.0) if i < 4 else (IK, 1.0) if i == 4 else (MISC, 1.0) if i == 5 else
                           (GQ[:, i - 6, :], 0.125) if i < 8 else (GK[:, i - 8, :], 1.0) if i < 10 else
                           (QA[:, i - 10, :], 1.0) if i < 14 else (KA[:, i - 14, :], 1.0) if i < 18 else
                           (VA[:, i - 18, :], 1.0) if i < 22 else (GV[:, i - 22, :], 1.0) if i < 26 else
                           (OG[:, i - 26, :], 1.0))
                if i < 26:
                    ev2(i, dst, s_)
                else:
                    ev2(i, dst, 1.0, ACT.Silu)
                if i == 9:
                    for p in range(2):
                        act.wait_ge(sems["gate_in"], p + 1)
                        f(GE[1][:, p, :], GE[0][:, p, :], ACT.Abs).then_inc(*A.inc())
                    act.wait_ge(*A.latest)
                    f(GE[1], GE[1], ACT.Exp, scale=-1.0).then_inc(*A.inc())
                    act.wait_ge(*A.latest)
                    f(GE[1], GE[1], ACT.Ln, bias=sc("one")).then_inc(*A.inc("gate_ln"))
                if 10 <= i < 18:
                    j = i - 10
                    if j >= 2:
                        act.wait_ge(sems["a_mm"], j - 1)
                    act.wait_ge(*A.latest)
                    f(SQA[:, j % 2, :], dst, ACT.Square).then_inc(*A.inc("a_sq"))
                    for n in range(3 * j, 3 * j + 3):
                        w = (INDEX_STEPS[n][0] + 1) * P
                        act.wait_ge(sems["idx_mm"], n + 1)
                        if n >= 2:
                            act.wait_ge(sems["idx_acc"], n - 1)
                        f(RLU[:, n % 2, 0:w], PB[6 + n % 2][:, 0:w], ACT.Relu, scale=0.125).then_inc(*A.inc("idx_r"))
                if 11 <= i < 19:
                    head_rstd(i - 11, 2, RA[:, (i - 11) % 2, :], "a_sc", "a_mm", "a_rs")
                if 18 <= i < 25:
                    l = i - 17
                    act.wait_ge(sems["lv_d"], l)
                    f(GE[l % 2], GE[l % 2], ACT.Abs).then_inc(*A.inc())
                    act.wait_ge(*A.latest)
                    f(GE[l % 2], GE[l % 2], ACT.Exp, scale=-1.0 / 16).then_inc(*A.inc("lv_e"))
            f(GEB, GB, ACT.Exp, scale=1.0 / 16).then_inc(*A.inc("g_eb"))
            act.wait_ge(sems["g_ed"], 1)
            f(GED, GED, ACT.Exp, scale=1.0 / 16).then_inc(*A.inc("g_ede"))
            for n in range(2):
                act.wait_ge(sems["ke_tr"], n + 1)
                f(GKT[:, 2 * n:2 * n + 2, :], PB[n][:, :].rearrange("p (t n) -> p t n", n=256), ACT.Copy)\
                    .then_inc(*A.inc("ke_ev"))
            for h in range(4):
                act.wait_ge(sems["go_mm"], h + 1)
                f(GSQ[:, h, :], PB[4 + h][:, :], ACT.Square).then_inc(*A.inc("go_sq"))
            for h in range(4):
                act.wait_ge(sems["go_nm"], h + 1)
                f(GSQ[:, h, :], PB[h][:, :], ACT.Ln, scale=1.0 / P, bias=sc("eps2")).then_inc(*A.inc())
            act.wait_ge(*A.latest)
            for h in range(4):
                f(GSQ[:, h, :], GSQ[:, h, :], ACT.Exp, scale=-0.5).then_inc(*A.inc("go_rs"))

            steps = STEPS["A"]
            b = BASE["A"]
            for i in range(len(steps) + PIPE):
                if i < len(steps):
                    w = (steps[i][1] + 1) * P
                    act.wait_ge(sems["sc_max"], b + i + 1)
                    if i >= 2:
                        act.wait_ge(sems["tr_mm"], b + i - 1)
                    f(APR[:, i % 2, 0:w], PB[4 + i % 2][:, 0:w], ACT.Exp, bias=nmax(i), accum_out=psum_of(i))\
                        .then_inc(*A.inc("sc_exp"))
                if 2 <= i < len(steps) + 2:
                    tr_evac("A", i - 2, steps[i - 2][1] + 1)
                if i >= PIPE:
                    h, t = steps[i - PIPE]
                    act.wait_ge(sems["pv_mm"], b + i - PIPE + 1)
                    f(HN[:, h, tile(t)], PB[2 + (i - PIPE) % 2][:, 0:P], ACT.Copy).then_inc(*A.inc("o_ev"))
            for k in range(KT):
                act.wait_ge(sems["norm_h"], RES[N_FFN0] + k + 1)
                f(SQ[:, k, :], H[:, k, :], ACT.Square).then_inc(*A.inc("norm_sq"))
            rstd(N_FFN0, "eps2")
            end_stage()
            mlp(1, "up_0", N_MIX1, "eps2")
            end_stage()

            for i in range(25):
                if i < 24:
                    act.wait_ge(sems["w_used"], UNIT["c_q"] + i + 1)
                    dst = CQ[:, i, :] if i < 8 else CK[:, i - 8, :] if i < 16 else CV[:, i - 16, :]
                    f(dst, PB[i % 4][:, :], ACT.Copy).then_inc(*A.inc("ev_act"))
                    if i < 16:
                        if i >= 2:
                            act.wait_ge(sems["c_nm"], i - 1)
                        act.wait_ge(*A.latest)
                        f(CSQ[:, i % 2, :], dst, ACT.Square).then_inc(*A.inc("c_sq"))
                if 1 <= i < 17:
                    head_rstd(i - 1, 4, CRS[:, (i - 1) % 2, :], "c_sc", "c_nm", "c_rs")
            steps = STEPS["C"]
            b = BASE["C"]
            for i in range(len(steps) + PIPE + 1):
                if i < len(steps):
                    w = (steps[i][1] + 1) * P
                    act.wait_ge(sems["sc_mm"], b + i + 1)
                    if i >= 2:
                        act.wait_ge(sems["c_nl"], i - 1)
                    f(CL[:, i % 2, 0:w], PB[4 + i % 4][:, 0:w], ACT.Abs).then_inc(*A.inc())
                    act.wait_ge(*A.latest)
                    f(CL[:, i % 2, 0:w], CL[:, i % 2, 0:w], ACT.Exp, scale=-1.0).then_inc(*A.inc())
                    act.wait_ge(*A.latest)
                    f(CL[:, i % 2, 0:w], CL[:, i % 2, 0:w], ACT.Ln, bias=sc("one")).then_inc(*A.inc("c_l"))
                if 1 <= i <= len(steps):
                    j = i - 1
                    w = (steps[j][1] + 1) * P
                    act.wait_ge(sems["c_la"], j + 1)
                    if j >= 2:
                        act.wait_ge(sems["tr_mm"], b + j - 1)
                    f(CPR[:, j % 2, 0:w], CN[:, j % 2, 0:w], ACT.Exp).then_inc(*A.inc("c_prob"))
                if 3 <= i < len(steps) + 3:
                    tr_evac("C", i - 3, steps[i - 3][1] + 1)
                j = i - PIPE - 1
                if j >= 0:
                    h, t = steps[j]
                    act.wait_ge(sems["pv_mm"], b + j + 1)
                    f(HN[:, h, tile(t)], PB[2 + j % 2][:, 0:P], ACT.Copy).then_inc(*A.inc("o_ev"))
            for k in range(KT):
                act.wait_ge(sems["norm_h"], RES[N_FFN1] + k + 1)
                f(SQ[:, k, :], H[:, k, :], ACT.Square).then_inc(*A.inc("norm_sq"))
            rstd(N_FFN1, "eps2")
            end_stage()
            mlp(2, "up_1", None, None)

        @block.vector
        def _(dve):
            D = Count(sems, "dve_step")
            ends = [0]

            def end_stage():
                ends[0] += 1
                dve.drain().then_inc(sems["stage"], 1)
                dve.wait_ge(sems["stage"], 3 * ends[0])

            def tt(out, a, b, op):
                return dve.tensor_tensor(out, a, b, op)

            def stt(out, a, scalar, b, op0, op1):
                return dve.scalar_tensor_tensor(out, a, scalar, b, op0, op1)

            def ts(out, a, s1, s2, op0, op1=None):
                if op1 is None:
                    return dve.tensor_scalar(out, a, s1, None, op0)
                return dve.tensor_scalar(out, a, s1, s2, op0, op1)

            def add_squares(n, k, w=S):
                dve.wait_ge(sems["norm_sq"], n * KT + k + 1)
                if k:
                    dve.wait_ge(*D.latest)
                    tt(ACC[:, 0:w], SQ[:, 0, 0:w] if k == 1 else ACC[:, 0:w], SQ[:, k, 0:w], ALU.add)\
                        .then_inc(*D.inc("norm_acc" if k == KT - 1 else None))

            def scale_out(n, src, dst, w, width=S):
                dve.wait_ge(sems["norm_rs"], n + 1)
                for k in range(KT):
                    stt(dst(k), src(k), vec(w, k, k + 1), RS[:, 0:width], ALU.mult, ALU.mult).then_inc(*D.inc("norm_out"))

            def residual(n, unit, bank, per=1):
                for k in range(KT):
                    dve.wait_ge(sems["w_used"], UNIT[unit] + per * (k + 1))
                    tt(H[:, k, :], H[:, k, :], PB[bank(k)][:, :], ALU.add).then_inc(*D.inc("norm_h"))
                    if k:
                        add_squares(n, k - 1)
                add_squares(n, KT - 1)

            def rd(out, in_, op, negate=False):
                return dve.tensor_reduce(out, in_, AX.X, op, negate=negate)

            dve.memset(PX[:, :, 0:1], 0.0).then_inc(*D.inc())
            dve.wait_ge(sems["v_in"], 16)
            dve.wait_ge(sems["c_in"], 16)
            tt(LAMP, vec("lam", 0, 2), vec("lam", 2, 4), ALU.mult).then_inc(*D.inc("lam_in"))
            ts(SUBW, vec("subln"), 0.8, None, ALU.mult).then_inc(*D.inc())
            ts(KA1, vec("k_a"), -1.0, 1.0, ALU.mult, ALU.add).then_inc(*D.inc())
            for k in range(KT):
                add_squares(N_MIX, k)
            dve.wait_ge(sems["x_in"], 16)
            scale_out(N_MIX, lambda k: H[:, k, :], lambda k: HN[:, k, :], "norm_mix")
            dve.wait_ge(sems["lam_exp"], 1)
            tt(NLAM, LAME[:, 1:2], LAME[:, 0:1], ALU.subtract).then_inc(*D.inc())
            dve.wait_ge(*D.latest)
            ts(NLAM, NLAM, 0.2, None, ALU.subtract).then_inc(*D.inc())

            def shift(m, name=None):
                dve.wait_ge(sems["ev_act"], m + 1)
                cur = PX[:, m, 1:PW]
                tt(TMP[:, m % 2, :], PX[:, m, 0:S], cur, ALU.subtract).then_inc(*D.inc())
                dve.wait_ge(*D.latest)
                stt(cur, TMP[:, m % 2, :], vec("mu", m, m + 1), cur, ALU.mult, ALU.add).then_inc(*D.inc(name))
            shift(LORA, "lora_in")
            shift(GD, "lora_in")
            for p in range(4):
                shift(K0 + p)
            dve.wait_ge(*D.latest)
            for p in range(4):
                ts(KK[:, p, :], PX[:, K0 + p, 1:PW], vec("k_k", p, p + 1), None, ALU.mult).then_inc(*D.inc())
            dve.wait_ge(*D.latest)
            for p in range(4):
                tt(CS[:, p, :], KK[:, p, :], KK[:, p, :], ALU.mult).then_inc(*D.inc("kk_sq"))
            for m in range(R0, 14):
                shift(m)
            for p in range(4):
                dve.wait_ge(sems["prep_act"], 4 + p + 1)
                ts(TMP[:, p % 2, :], AG[:, p, :], vec("k_a", p, p + 1), KA1[:, p:p + 1], ALU.mult, ALU.add).then_inc(*D.inc())
                dve.wait_ge(*D.latest)
                tt(PX[:, K0 + p, 1:PW], PX[:, K0 + p, 1:PW], TMP[:, p % 2, :], ALU.mult).then_inc(*D.inc())
                dve.wait_ge(*D.latest)
                stt(BON[:, p, :], PX[:, R0 + p, 1:PW], vec("r_k", p, p + 1), PX[:, K0 + p, 1:PW], ALU.mult, ALU.mult)\
                    .then_inc(*D.inc("bonus_in"))
            for p in range(4):
                dve.wait_ge(sems["prep_mm"], 12 + p + 1)
                ts(CS[:, p, :], PB[4 + p][:, :], 1e-24, KK_SCALE, ALU.max, ALU.mult).then_inc(*D.inc("kkln_in"))
            for p in range(4):
                dve.wait_ge(sems["kk_rs"], p + 1)
                tt(KK[:, p, :], KK[:, p, :], CS[:, p, :], ALU.mult).then_inc(*D.inc())
                dve.wait_ge(*D.latest)
                tt(AG[:, p, :], AG[:, p, :], KK[:, p, :], ALU.mult).then_inc(*D.inc())
            for p in range(4):
                dve.tensor_tensor_scan(CS[:, p, :], cst("reset64"), SIG[:, p, :], 0.0, ALU.mult, ALU.add).then_inc(*D.inc())
                dve.wait_ge(*D.latest)
                tt(SIG[:, p, :], CS[:, p, :], SIG[:, p, :], ALU.subtract).then_inc(*D.inc("cs_ready"))
            for p in range(4):
                dve.wait_ge(sems["prep_mm"], 16 + p + 1)
                tt(BON[:, p, :], PB[4 + p][:, :], PX[:, V0 + p, 1:PW], ALU.mult).then_inc(*D.inc("prep_dve"))
            for p in range(4):
                dve.wait_ge(sems["exp_ready"], 3 * p + 3)
                tt(KK[:, p, :], KK[:, p, :], SIG[:, p, :], ALU.mult).then_inc(*D.inc())
                tt(AG[:, p, :], AG[:, p, :], TMP[:, p % 2, :], ALU.mult).then_inc(*D.inc())
                tt(PX[:, K0 + p, 1:PW], PX[:, K0 + p, 1:PW], TMP[:, p % 2, :], ALU.mult).then_inc(*D.inc("exp_used"))
                tt(PX[:, R0 + p, 1:PW], PX[:, R0 + p, 1:PW], CS[:, p, :], ALU.mult).then_inc(*D.inc())
            dve.tensor_copy(ECH, CS[:, :, 63::64]).then_inc(*D.inc())
            dve.wait_ge(*D.latest)

            steps = STEPS["diff"]
            for i in range(len(steps) + PIPE + 2):
                if i < len(steps):
                    w = (steps[i][1] + 1) * P
                    dve.wait_ge(sems["sc_mm"], i + 1)
                    banks = [PB[4 + 2 * (i % 2)], PB[5 + 2 * (i % 2)]]
                    for pb in banks:
                        tt(pb[:, w - 64:w], pb[:, w - 64:w], cst("chunk_bias"), ALU.add).then_inc(*D.inc())
                    dve.wait_ge(*D.latest)
                    for m, pb in enumerate(banks):
                        rd(nmax(i, m), pb[:, 0:w], ALU.max, negate=True).then_inc(*D.inc("sc_max" if m else None))
                j = i - 1
                if 0 <= j < len(steps):
                    w = (steps[j][1] + 1) * P
                    dve.wait_ge(sems["sc_exp"], 2 * (j + 1))
                    dve.reciprocal(recip(j, 0, 2), psum_of(j, 0, 2)).then_inc(*D.inc())
                    dve.wait_ge(*D.latest)
                    tt(recip(j, 1), recip(j, 1), NLAM, ALU.mult).then_inc(*D.inc())
                    dve.wait_ge(*D.latest)
                    ts(PR2[:, j % 2, 0:w], PR2[:, j % 2, 0:w], recip(j, 1), None, ALU.mult).then_inc(*D.inc())
                    dve.wait_ge(*D.latest)
                    stt(PR1[:, j % 2, 0:w], PR1[:, j % 2, 0:w], recip(j, 0), PR2[:, j % 2, 0:w], ALU.mult, ALU.add)\
                        .then_inc(*D.inc("prob"))
                j = i - PIPE - 1
                if 0 <= j < len(steps) and steps[j][1] == TT - 1:
                    h = steps[j][0]
                    dve.wait_ge(sems["on_rs"], h + 1)
                    stt(HN[:, 4 + h, :], PB[2 + h % 2][:, :], SUBW, OLN, ALU.mult, ALU.mult).then_inc(*D.inc("on_out"))
            end_stage()

            for g in GS:
                dve.memset(g, 0.0).then_inc(*D.inc())
            dve.wait_ge(*D.latest)

            def two(bank):
                return PB[bank][:, :].rearrange("p (a n) -> p a n", n=256)

            def four(bank):
                return PB[bank][:, :].rearrange("p (a n) -> p a n", n=P)

            def heads4(x, q):
                return x[:, q::2, :]
            masks = cst("bd_strict", 0, 256).unsqueeze(1).to_broadcast([P, 2, 256])
            pairm = cst("low_mask", 0, 128).unsqueeze(1).to_broadcast([P, 4, P])
            pairt = cst("gla_mask", 0, 128).unsqueeze(1).to_broadcast([P, 4, P])
            eye = cst("ident").unsqueeze(1).to_broadcast([P, 4, P])
            for t in range(TT):
                ech = ECH[:, :, 2 * t:2 * t + 2].unsqueeze(3).to_broadcast([P, 4, 2, 64])
                for src, dst in ((AG[:, :, tile(t)], BP), (PX[:, K0:K0 + 4, 1 + t * P:1 + (t + 1) * P], KP)):
                    tt(dst.rearrange("p a (c n) -> p a c n", n=64), src.rearrange("p a (c n) -> p a c n", n=64), ech, ALU.mult)\
                        .then_inc(*D.inc("ch_in"))
                for n in range(8):
                    dve.wait_ge(sems["ch_aq"], 10 * t + n + 1)
                    h = 4 * (n % 4 // 2) + n % 2
                    dst = AQ if n < 4 else BQ
                    tt(dst[:, h:h + 3:2, :], two(n % 4), masks, ALU.mult).then_inc(*D.inc("ch_aqev"))
                for q in range(2):
                    dve.wait_ge(sems["ch_aq"], 10 * t + 8 + q + 1)
                    tt(heads4(TI, q), four(q), pairm, ALU.mult).then_inc(*D.inc("ch_aqev"))
                dve.wait_ge(*D.latest)
                for q in range(2):
                    tt(heads4(TI, q), eye, heads4(TI, q), ALU.subtract).then_inc(*D.inc("ch_t0ev"))
                for q in range(2):
                    tt(heads4(UI, q), AQ[:, q::2, 0:P], pairt, ALU.mult).then_inc(*D.inc())
                dve.wait_ge(*D.latest)
                for q in range(2):
                    tt(heads4(UI, q), eye, heads4(UI, q), ALU.subtract).then_inc(*D.inc("ch_t0ev"))
                for l in range(5):
                    m = cst("low_mask", (l + 1) * P, (l + 2) * P).unsqueeze(1).to_broadcast([P, 4, P])
                    for q in range(2):
                        dve.wait_ge(sems["lv_x"], 10 * t + 2 * l + q + 1)
                        tt(heads4(XI, q), four(q), m, ALU.mult).then_inc(*D.inc("lv_xev"))
                    for q in range(2):
                        dve.wait_ge(sems["lv_y"], 20 * t + 4 * l + 2 * q + 1)
                        tt(heads4(TI, q), heads4(TI, q), four(2 + q), ALU.subtract).then_inc(*D.inc("lv_yev"))
                        dve.wait_ge(sems["lv_y"], 20 * t + 4 * l + 2 * q + 2)
                        tt(heads4(UI, q), heads4(UI, q), four(4 + q), ALU.subtract).then_inc(*D.inc("lv_yev"))
                for c in (2 * t, 2 * t + 1):
                    r = slice(64 * (c % 2), 64 * (c % 2) + 64)
                    g, g1 = GS[c % 3], GS[(c + 1) % 3]
                    tt(TG, g, ECH[:, :, c:c + 1].to_broadcast([P, 4, P]), ALU.mult).then_inc(*D.inc())
                    dve.wait_ge(sems["sa_mm"], c + 1)
                    tt(SA[r], W1[r], four(0)[r], ALU.subtract).then_inc(*D.inc("sa_ev"))
                    dve.wait_ge(sems["gu_mm"], c + 1)
                    tt(g1[0:64, :, 0:64], TG[0:64, :, 0:64], four(1)[0:64, :, 0:64], ALU.add).then_inc(*D.inc())
                    tt(g1[64:128, :, 64:128], TG[64:128, :, 64:128], four(1)[64:128, :, 64:128], ALU.add)\
                        .then_inc(*D.inc("g_ev"))
                    dve.wait_ge(*D.latest)
                end_stage()

            for p in range(4):
                dve.wait_ge(sems["gn_mm"], p + 1)
                stt(HN[:, p, :], PB[p][:, :], -1.0 / 64, HN[:, p, :], ALU.mult, ALU.add).then_inc(*D.inc("gn_c"))
            for p in range(4):
                dve.wait_ge(sems["gn_rs"], p + 1)
                stt(HN[:, p, :], HN[:, p, :], vec("lnx_w", p, p + 1), SIG[:, p, :], ALU.mult, ALU.mult).then_inc(*D.inc())
                dve.wait_ge(*D.latest)
                stt(HN[:, p, :], HN[:, p, :], vec("lnx_b", p, p + 1), BON[:, p, :], ALU.add, ALU.add).then_inc(*D.inc())
                dve.wait_ge(*D.latest)
                tt(HN[:, p, :], HN[:, p, :], GT[:, p, :], ALU.mult).then_inc(*D.inc("mix_out"))
            end_stage()

            for k in range(KT):
                add_squares(N_SRC, k, MEM)
            dve.wait_ge(sems["mem_in"], 16)
            scale_out(N_SRC, lambda k: MT[:, k, :], lambda k: MN[:, k, :], "norm_src", MEM)
            residual(N_MEM, "out", lambda k: k % 4)
            scale_out(N_MEM, lambda k: H[:, k, :], lambda k: HN[:, k, :], "norm_mem")
            steps = STEPS["mem"]
            for i in range(len(steps) + 1):
                if i < len(steps):
                    dve.wait_ge(sems["sc_mm"], BASE["mem"] + i + 1)
                    rd(nmax(i), PB[4 + i % 2][:, 0:MEM], ALU.max, negate=True).then_inc(*D.inc("sc_max"))
                if i:
                    j = i - 1
                    dve.wait_ge(sems["sc_exp"], EXPB["mem"] + j + 1)
                    dve.reciprocal(recip(j), psum_of(j)).then_inc(*D.inc())
                    dve.wait_ge(*D.latest)
                    ts(MPR[:, j % 2, 0:MEM], MPR[:, j % 2, 0:MEM], recip(j), None, ALU.mult).then_inc(*D.inc("prob"))
            residual(N_MLP, "mem_o", lambda k: k % 4)
            scale_out(N_MLP, lambda k: H[:, k, :], lambda k: HN[:, k, :], "norm_mlp")
            end_stage()
            residual(N_FINAL, "down", lambda k: k % 2, 4)
            scale_out(N_FINAL, lambda k: H[:, k, :], lambda k: H[:, k, :], "norm_final")

            for k in range(KT):
                add_squares(N_MIX0, k)
            scale_out(N_MIX0, lambda k: H[:, k, :], lambda k: HN[:, k, :], "g_mix0")
            ts(GQS, vec("gq_a"), P ** -0.5, None, ALU.mult).then_inc(*D.inc())
            ts(GCS, vec("gq_c"), P ** -0.5, None, ALU.mult).then_inc(*D.inc())
            end_stage()

            def rope(j):
                kind = "i" if j < 5 else "a"
                x = rope_plane(j)
                dve.wait_ge(sems["rope_mm"], j + 1)
                tt(T1, PB[3][:, :], cst("sin_" + kind), ALU.mult).then_inc(*D.inc())
                tt(x, x, cst("cos_" + kind), ALU.mult).then_inc(*D.inc())
                dve.wait_ge(*D.latest)
                tt(x, x, T1, ALU.add).then_inc(*D.inc("rope_ev"))
            for j in range(5):
                rope(j)
                if j == 4:
                    dve.wait_ge(sems["iw_tr"], 1)
                    ts(IW, PB[2][:, :].rearrange("p (t n) -> p t n", n=P)[:, :, 32:40], 8 ** -0.5, None, ALU.mult, None)\
                        .then_inc(*D.inc("iw_ev"))
            for p in range(2):
                dve.wait_ge(sems["gate_mm"], p + 1)
                ts(GE[0][:, p, :], PB[4 + p][:, :], vec("b_gate", p, p + 1), None, ALU.add).then_inc(*D.inc("gate_in"))
            dve.wait_ge(sems["gate_ln"], 1)
            stt(GB, GE[0], 0.0, GE[1], ALU.min, ALU.subtract).then_inc(*D.inc())
            dve.wait_ge(*D.latest)
            for p in range(2):
                dve.tensor_tensor_scan(GE[0][:, p, :], cst("reset128"), GB[:, p, :], 0.0, ALU.mult, ALU.add).then_inc(*D.inc())
            dve.wait_ge(*D.latest)
            dve.tensor_copy(GB, GE[0]).then_inc(*D.inc("gb_ready"))

            def a_scale(j):
                x = rope_plane(5 + j)
                dve.wait_ge(sems["a_rs"], j + 1)
                stt(x, x, GQS if j < 4 else vec("gk_a"), RA[:, j % 2, :], ALU.mult, ALU.mult).then_inc(*D.inc("a_sc"))

            for j in range(9):
                if j < 8:
                    for n in range(3 * j, 3 * j + 3):
                        t, h = INDEX_STEPS[n]
                        w = (t + 1) * P
                        dve.wait_ge(sems["idx_r"], n + 1)
                        if h == 0:
                            ts(SCORE[:, t, 0:w], RLU[:, n % 2, 0:w], IW[:, t, h:h + 1], None, ALU.mult, None)\
                                .then_inc(*D.inc("idx_acc"))
                        else:
                            dve.wait_ge(*D.latest)
                            stt(SCORE[:, t, 0:w], RLU[:, n % 2, 0:w], IW[:, t, h:h + 1], SCORE[:, t, 0:w], ALU.mult, ALU.add)\
                                .then_inc(*D.inc("idx_acc"))
                if j:
                    a_scale(j - 1)
            dve.wait_ge(*D.latest)
            for t in range(1, TT):
                w = (t + 1) * P
                tt(SCORE[:, t, w - 64:w], SCORE[:, t, w - 64:w], cst("chunk_bias"), ALU.add).then_inc(*D.inc())

            def topk(t):
                w = (t + 1) * P
                s = SCORE[:, t, 0:w]
                for n in range(16):
                    src = s if n == 0 else WORK[:, 0:w]
                    dve.max(TOP, src).then_inc(*D.inc())
                    dve.wait_ge(*D.latest)
                    if n < 15:
                        dve.match_replace(WORK[:, 0:w], TOP, src, -3.0e38).then_inc(*D.inc())
                        dve.wait_ge(*D.latest)
                thr = TOP[:, 7:8]
                ts(EQ[:, 0:w], s, thr, None, ALU.is_equal).then_inc(*D.inc())
                ts(s, s, thr, None, ALU.is_gt).then_inc(*D.inc())
                dve.wait_ge(*D.latest)
                dve.tensor_reduce(NGT, s, AX.X, ALU.add).then_inc(*D.inc())
                dve.tensor_tensor_scan(PRE[:, 0:w], cst("ones", 0, 1).to_broadcast([P, w]), EQ[:, 0:w], 0.0, ALU.mult, ALU.add)\
                    .then_inc(*D.inc())
                dve.wait_ge(*D.latest)
                ts(NGT, NGT, -1.0, 128.0, ALU.mult, ALU.add).then_inc(*D.inc())
                dve.wait_ge(*D.latest)
                stt(EQ[:, 0:w], PRE[:, 0:w], NGT, EQ[:, 0:w], ALU.is_le, ALU.mult).then_inc(*D.inc())
                dve.wait_ge(*D.latest)
                tt(s, s, EQ[:, 0:w], ALU.add).then_inc(*D.inc())
                dve.wait_ge(*D.latest)
                ts(s, s, -1.0, -NEG, ALU.add, ALU.mult).then_inc(*D.inc())
                dve.wait_ge(*D.latest)
            for l in range(8):
                mask = cst("gla_mask", 7 * P, 8 * P) if l == 0 else cst("gla_mask", (l - 1) * P, l * P)
                mask = mask.unsqueeze(1).to_broadcast([P, 4, P])
                for n in range(4):
                    dve.wait_ge(sems["lvl_mm"], 4 * l + n + 1)
                    dst = (ATT if l == 0 else LV)[:, n, :].rearrange("p (a n) -> p a n", n=P)
                    tt(dst, PB[4 + n][:, :].rearrange("p (a n) -> p a n", n=P), mask, ALU.mult).then_inc(*D.inc("lvl_ev"))
                if l:
                    dve.wait_ge(*D.latest)
                    for n in range(4):
                        tt(ATT[:, n, :], ATT[:, n, :], LV[:, n, :], ALU.add).then_inc(*D.inc("att"))
                if 1 <= l:
                    rope(4 + l)
            rope(12)
            topk(1)
            for t in range(3):
                dve.wait_ge(sems["kv2_mm"], max(t + 1, 2))
                bank, o = (2, 256 * t) if t < 2 else (3, 0)
                dve.wait_ge(sems["g_eb"], 1)
                if t == 0:
                    dve.tensor_copy(GSH[:, 1, :], PB[bank][:, o:o + 256]).then_inc(*D.inc("sh_ev"))
                else:
                    dve.wait_ge(*D.latest)
                    for p in range(2):
                        e = t * P + P - 1
                        stt(GSH[:, t + 1, p * P:(p + 1) * P], GSH[:, t, p * P:(p + 1) * P], GEB[:, p, e:e + 1], PB[bank][:, o + p * P:o + (p + 1) * P], ALU.mult, ALU.add)\
                            .then_inc(*D.inc("sh_ev" if p else None))
            for h in range(4):
                dve.wait_ge(sems["go_rs"], h + 1)
                stt(HN[:, 4 + h, :], PB[4 + h][:, :], vec("g_gla"), GSQ[:, h, :], ALU.mult, ALU.mult).then_inc(*D.inc("go_ev"))
            dve.wait_ge(*D.latest)
            for h in range(4):
                tt(HN[:, 4 + h, :], HN[:, 4 + h, :], OG[:, h, :], ALU.mult).then_inc(*D.inc())

            steps = STEPS["A"]
            for i in range(len(steps) + 1):
                if i < len(steps):
                    h, t = steps[i]
                    w = (t + 1) * P
                    if h == 0 and t >= 2:
                        topk(t)
                    dve.wait_ge(sems["sc_mm"], BASE["A"] + i + 1)
                    pb = PB[4 + i % 2]
                    if t == 0:
                        tt(pb[:, 64:P], pb[:, 64:P], cst("chunk_bias"), ALU.add).then_inc(*D.inc())
                    else:
                        tt(pb[:, 0:w], pb[:, 0:w], SCORE[:, t, 0:w], ALU.add).then_inc(*D.inc())
                    dve.wait_ge(*D.latest)
                    rd(nmax(i), pb[:, 0:w], ALU.max, negate=True).then_inc(*D.inc("sc_max"))
                if i:
                    j = i - 1
                    w = (steps[j][1] + 1) * P
                    dve.wait_ge(sems["sc_exp"], EXPB["A"] + j + 1)
                    dve.reciprocal(recip(j), psum_of(j)).then_inc(*D.inc())
                    dve.wait_ge(*D.latest)
                    ts(APR[:, j % 2, 0:w], APR[:, j % 2, 0:w], recip(j), None, ALU.mult).then_inc(*D.inc("prob"))
            residual(N_FFN0, "out_ab", lambda k: k % 4)
            scale_out(N_FFN0, lambda k: H[:, k, :], lambda k: HN[:, k, :], "g_ffn0")
            end_stage()
            residual(N_MIX1, "down_0", lambda k: k % 2, 4)
            scale_out(N_MIX1, lambda k: H[:, k, :], lambda k: HN[:, k, :], "g_mix1")
            end_stage()

            for j in range(16):
                x = CQ[:, j, :] if j < 8 else CK[:, j - 8, :]
                dve.wait_ge(sems["c_rs"], j + 1)
                stt(x, x, GCS if j < 8 else vec("gk_c"), CRS[:, j % 2, :], ALU.mult, ALU.mult).then_inc(*D.inc("c_sc"))
            steps = STEPS["C"]
            for i in range(len(steps)):
                t = steps[i][1]
                w = (t + 1) * P
                z = PB[4 + i % 4]
                nl, rc, la = CL[:, i % 2, 0:w], CR[:, i % 2, 0:w], CN[:, i % 2, 0:w]
                dve.wait_ge(sems["c_l"], i + 1)
                if i >= 2:
                    dve.wait_ge(sems["c_prob"], i - 1)
                stt(la, z[:, 0:w], 0.0, nl, ALU.max, ALU.add).then_inc(*D.inc("c_nl"))
                dve.wait_ge(*D.latest)
                tt(la[:, w - P:w], la[:, w - P:w], cst("strict"), ALU.mult).then_inc(*D.inc())
                dve.wait_ge(*D.latest)
                dve.tensor_tensor_scan(rc[:, ::-1], cst("ones", 0, 1).to_broadcast([P, w]), la[:, ::-1], 0.0, ALU.mult, ALU.add)\
                    .then_inc(*D.inc())
                dve.wait_ge(*D.latest)
                tt(la, z[:, 0:w], rc, ALU.subtract).then_inc(*D.inc())
                dve.wait_ge(*D.latest)
                tt(la[:, w - P:w], la[:, w - P:w], cst("strict_bias"), ALU.add).then_inc(*D.inc("c_la"))
            residual(N_FFN1, "out_c", lambda k: k % 4)
            scale_out(N_FFN1, lambda k: H[:, k, :], lambda k: HN[:, k, :], "g_ffn1")
            end_stage()
            for k in range(KT):
                dve.wait_ge(sems["w_used"], UNIT["down_1"] + 4 * (k + 1))
                tt(H[:, k, :], H[:, k, :], PB[k % 2][:, :], ALU.add).then_inc(*D.inc("norm_h"))

        @block.tensor
        def _(pe):
            T = Count(sems, None)
            ends = [0]
            unit = [0]
            free = [None] * 8

            def end_stage():
                ends[0] += 1
                pe.drain().then_inc(sems["stage"], 1)
                pe.wait_ge(sems["stage"], 3 * ends[0])
                for b in range(8):
                    free[b] = None

            def take(b):
                if free[b] is not None:
                    pe.wait_ge(sems[free[b][0]], free[b][1])
                    free[b] = None

            def mm(out, lhsT, rhs, start=True, stop=True, **k):
                return pe.matmul(out, lhsT, rhs, start=start, stop=stop, **k)

            def tr(out, in_):
                return pe.transpose(out, in_, cst("ident"))

            def weights(u):
                pe.wait_ge(slot_loaded[u % RING], 16 * (u // RING + 1))
                return W[:, u % RING, :].rearrange("p (k n) -> p k n", n=P)

            def project(n, bank0, ev, rhs, ready=None, width=S, banks=4, evbase=0):
                for m in range(n):
                    u = unit[0]
                    b = (bank0 + m) % banks
                    take(b)
                    w = weights(u)
                    for k in range(KT):
                        if m == 0 and ready is not None:
                            pe.wait_ge(sems["norm_out"], ready + k + 1)
                        ins = pe.matmul(PB[b][:, 0:width], w[:, k, :], rhs(k), start=k == 0, stop=k == KT - 1)
                    ins.then_inc(*T.inc("w_used"))
                    unit[0] += 1
                    free[b] = (ev, evbase + m + 1)

            def project_tok(n, bank0, ev, lhs, tiles=TT, evbase=0, ready=None, banks=4):
                for m in range(n):
                    u = unit[0]
                    b = (bank0 + m) % banks
                    take(b)
                    w = weights(u)
                    for t in range(tiles):
                        for k in range(KT):
                            if m == 0 and t == 0 and ready is not None:
                                pe.wait_ge(sems["norm_out"], ready + k + 1)
                            ins = pe.matmul(PB[b][:, tile(t)], lhs(k, t), w[:, k, :], start=k == 0, stop=k == KT - 1)
                    ins.then_inc(*T.inc("w_used"))
                    unit[0] += 1
                    free[b] = (ev, evbase + m + 1)

            def norm_sum(n, width=S):
                pe.wait_ge(sems["norm_acc"], n + 1)
                mm(PB[4][:, 0:width], cst("ones"), ACC[:, 0:width]).then_inc(*T.inc("norm_ms"))
                free[4] = ("norm_rs", n + 1)

            def hn(k):
                return HN[:, k, :]

            pe.wait_ge(sems["c_in"], 16)
            pe.wait_ge(sems["lam_in"], 1)
            mm(PB[7][:, 0:2], cst("ones"), LAMP).then_inc(*T.inc("lam_mm"))
            free[7] = ("lam_exp", 1)
            norm_sum(N_MIX)

            def prep(n, lhsT, rhs, w=S):
                b = 4 + n % 4
                take(b)
                mm(PB[b][:, :], lhsT, rhs).then_inc(*T.inc("prep_mm"))
                free[b] = ("prep_act", n + 1) if n < 12 else ("kkln_in", n - 11) if n < 16 else ("prep_dve", n - 15)
            project(14, 0, "ev_act", hn, ready=0)
            pe.wait_ge(sems["sig_ready"], 1)
            for p in range(4):
                prep(p, vec("dec_aaa_up", p * P, (p + 1) * P)[0:64], PX[0:64, LORA, 1:PW])
            for p in range(4):
                prep(4 + p, vec("dec_aaa_up", p * P, (p + 1) * P)[64:128], PX[64:128, LORA, 1:PW])
            for p in range(4):
                prep(8 + p, vec("g_up", p * P, (p + 1) * P), PX[:, GD, 1:PW])
            project(4, 14, "ev_act", hn, evbase=14)
            for p in range(4):
                pe.wait_ge(sems["kk_sq"], p + 1)
                prep(12 + p, cst("bd_ones"), CS[:, p, :])
            project(4, 18, "ev_act", hn, evbase=18)
            for p in range(4):
                pe.wait_ge(sems["bonus_in"], p + 1)
                prep(16 + p, cst("bd_ones"), BON[:, p, :])
            project_tok(4, 22, "ev_act", lambda k, t: HN[:, k, tile(t)], evbase=22)

            steps = STEPS["diff"]
            for i in range(len(steps) + PIPE + 1):
                j = i - PIPE - 1
                if 0 <= j < len(steps) and steps[j][1] == TT - 1:
                    h = steps[j][0]
                    pe.wait_ge(sems["on_sq"], h + 1)
                    take(1)
                    mm(PB[1][:, :], cst("ones"), OSQ).then_inc(*T.inc("on_mm"))
                    free[1] = ("on_rs", h + 1)
                if i < len(steps):
                    h, t = steps[i]
                    w = (t + 1) * P
                    if i == 0:
                        pe.wait_ge(sems["ev_act"], 26)
                    for m in range(2):
                        b = 4 + 2 * (i % 2) + m
                        take(b)
                        r = slice(64 * m, 64 * m + 64)
                        last = mm(PB[b][:, 0:w], DQ[r, h, tile(t)], DK[r, h, 0:w])
                        if m:
                            last.then_inc(*T.inc("sc_mm"))
                        free[b] = ("sc_exp", 2 * (i + 1))
                if 2 <= i < len(steps) + 2:
                    j = i - 2
                    pe.wait_ge(sems["prob"], j + 1)
                    take(0)
                    for k in range(steps[j][1] + 1):
                        last = tr(PB[0][:, tile(k)], PR1[:, j % 2, tile(k)])
                        if k == steps[j][1]:
                            last.then_inc(*T.inc("tr_mm"))
                    free[0] = ("tr_ev", j + 1)
                j = i - PIPE
                if 0 <= j < len(steps):
                    h, t = steps[j]
                    pe.wait_ge(sems["tr_ev"], j + 1)
                    b = 2 + h % 2
                    if t == 0:
                        take(b)
                    for k in range(t + 1):
                        last = mm(PB[b][:, tile(t)], DV[:, h, tile(k)], PT[:, j % 2, tile(k)], start=k == 0, stop=k == t)
                        if k == t:
                            last.then_inc(*T.inc("pv_mm"))
                    if t == TT - 1:
                        free[b] = ("on_out", h + 1)
            end_stage()

            def bank4(b, p):
                return PB[b][:, p * P:(p + 1) * P]
            alpha, beta = (lambda p, t: KK[:, p, tile(t)]), (lambda p, t: AG[:, p, tile(t)])

            def px(m, t, lo=0, n=P):
                return PX[:, m, 1 + t * P + lo:1 + t * P + lo + n]
            for t in range(TT):
                for n, src in enumerate((alpha, lambda p, t: px(V0 + p, t), lambda p, t: BP[:, p, :], lambda p, t: KP[:, p, :])):
                    if n >= 2:
                        pe.wait_ge(sems["ch_in"], 2 * t + n - 1)
                    for p in range(4):
                        last = tr(bank4(4 + n, p), src(p, t))
                        if p == 3:
                            last.then_inc(*T.inc("ch_tr"))
                for n in range(8):
                    if n >= 4:
                        pe.wait_ge(sems["ch_aqev"], 10 * t + n - 3)
                    for e in range(2):
                        h = 4 * (n % 4 // 2) + n % 2 + 2 * e
                        p, r = h // 2, slice(64 * (h % 2), 64 * (h % 2) + 64)
                        lhsT = (beta(p, t) if n < 4 else px(K0 + p, t))[r]
                        o = 256 * e
                        mm(PB[n % 4][:, o:o + P], lhsT, alpha(p, t)[r])
                        last = mm(PB[n % 4][:, o + P:o + 256], lhsT, px(R0 + p, t)[r])
                        if e:
                            last.then_inc(*T.inc("ch_aq"))
                for q in range(2):
                    pe.wait_ge(sems["ch_aqev"], 10 * t + 5 + q)
                    for e in range(4):
                        r = slice(64 * q, 64 * q + 64)
                        last = mm(bank4(q, e), alpha(e, t)[r], beta(e, t)[r])
                        if e == 3:
                            last.then_inc(*T.inc("ch_aq"))
                for l in range(5):
                    for q in range(2):
                        if l == 0:
                            pe.wait_ge(sems["ch_t0ev"], 4 * t + 4)
                        else:
                            pe.wait_ge(sems["lv_yev"], 20 * t + 4 * (l - 1) + 2 * q + 2)
                        for e in range(4):
                            h = 2 * e + q
                            last = mm(bank4(q, e), AQ[:, h, 0:P], TI[:, h, :])
                            if e == 3:
                                last.then_inc(*T.inc("lv_x"))
                    for q in range(2):
                        pe.wait_ge(sems["lv_xev"], 10 * t + 2 * l + q + 1)
                        for e in range(4):
                            h = 2 * e + q
                            last = mm(bank4(2 + q, e), UI[:, h, :], XI[:, h, :])
                            if e == 3:
                                last.then_inc(*T.inc("lv_y"))
                        if l == 0 and q == 0:
                            pe.wait_ge(sems["ch_trev"], 4 * t + 4)
                        for e in range(4):
                            h = 2 * e + q
                            last = mm(bank4(4 + q, e), XI[:, h, :], UI[:, h, :])
                            if e == 3:
                                last.then_inc(*T.inc("lv_y"))
                pe.wait_ge(sems["lv_yev"], 20 * t + 20)
                for h in range(8):
                    last = mm(PB[4][:, h * 64:h * 64 + 64], BQ[:, h, 0:P], TOKV[:, h // 2, 64 * (h % 2):64 * (h % 2) + 64])
                    if h == 7:
                        last.then_inc(*T.inc("w1_mm"))
                for h in range(8):
                    r = slice(64 * (h % 2), 64 * (h % 2) + 64)
                    last = mm(PB[5][r, tile(h // 2)], TOKA[:, h // 2, r], UI[:, h, :])
                    if h == 7:
                        last.then_inc(*T.inc("w1_mm"))
                pe.wait_ge(sems["w1_ev"], 3 * t + 1)
                for h in range(8):
                    last = mm(PB[6][:, h * 64:h * 64 + 64], UI[:, h, :], P1[:, h // 2, 64 * (h % 2):64 * (h % 2) + 64])
                    if h == 7:
                        last.then_inc(*T.inc("w1_mm"))
                pe.wait_ge(sems["w1_ev"], 3 * t + 3)
                for c in (2 * t, 2 * t + 1):
                    r = slice(64 * (c % 2), 64 * (c % 2) + 64)
                    if c:
                        pe.wait_ge(sems["g_ev"], c)
                    for p in range(4):
                        last = mm(PB[0][r, tile(p)], TA[:, p, r], GS[c % 3][:, p, :])
                        if p == 3:
                            last.then_inc(*T.inc("sa_mm"))
                    for p in range(4):
                        mm(PB[1][:, tile(p)], TOKK[r, p, :], TOKV[r, p, :], start=p == 0, stop=False, skip_group_check=True)
                    pe.wait_ge(sems["sa_ev"], c + 1)
                    for p in range(4):
                        last = mm(PB[1][:, tile(p)], TOKB[r, p, :], SA[r, p, :], start=False, stop=True, skip_group_check=True)
                        if p == 3:
                            last.then_inc(*T.inc("gu_mm"))
                for p in range(4):
                    for q in range(2):
                        r = slice(64 * q, 64 * q + 64)
                        mm(PB[7][r, tile(p)], SA[:, p, r], AQ[:, 2 * p + q, P:2 * P], start=True, stop=False, skip_group_check=True)
                        mm(PB[7][r, tile(p)], TOKV[:, p, r], BQ[:, 2 * p + q, P:2 * P], start=False, stop=False, skip_group_check=True)
                    for e in range(2):
                        o = p * P + 64 * e
                        last = mm(PB[7][:, o:o + 64], GS[(2 * t + e) % 3][:, p, :], px(R0 + p, t, 64 * e, 64), start=False, stop=e == 1, skip_group_check=True)
                        if p == 3 and e == 1:
                            last.then_inc(*T.inc("y_mm"))
                end_stage()
            for p in range(4):
                mm(PB[p][:, :], cst("bd_ones"), HN[:, p, :]).then_inc(*T.inc("gn_mm"))
            for p in range(4):
                pe.wait_ge(sems["gn_sq"], p + 1)
                mm(PB[4 + p][:, :], cst("bd_ones"), SIG[:, p, :]).then_inc(*T.inc("gn_mm"))
            end_stage()

            project(4, 0, "norm_h", hn, evbase=RES[N_MEM])
            norm_sum(N_SRC, MEM)
            project(4, 4, "norm_h", hn, evbase=RES[N_MEM] + 4)
            take(4)
            norm_sum(N_MEM)
            evb = 26
            project(8, 0, "ev_act", lambda k: MN[:, k, :], ready=N_SRC * KT, width=MEM, evbase=evb)
            project_tok(8, 0, "ev_act", lambda k, t: MN[:, k, tile(t)], tiles=2, evbase=evb + 8)
            project(8, 0, "ev_act", hn, ready=N_MEM * KT, evbase=evb + 16)
            steps = STEPS["mem"]
            b0 = BASE["mem"]
            pe.wait_ge(sems["ev_act"], evb + 24)
            for i in range(len(steps) + PIPE):
                if i < len(steps):
                    h, t = steps[i]
                    b = 4 + i % 2
                    take(b)
                    for j in range(2):
                        last = mm(PB[b][:, 0:MEM], MQ[:, 2 * h + j, tile(t)], MK[:, 2 * h + j, :], start=j == 0, stop=j == 1)
                        if j:
                            last.then_inc(*T.inc("sc_mm"))
                    free[b] = ("sc_exp", EXPB["mem"] + i + 1)
                if 2 <= i < len(steps) + 2:
                    j = i - 2
                    pe.wait_ge(sems["prob"], b0 + j + 1)
                    take(0)
                    for k in range(2):
                        last = tr(PB[0][:, tile(k)], MPR[:, j % 2, tile(k)])
                        if k:
                            last.then_inc(*T.inc("tr_mm"))
                    free[0] = ("tr_ev", b0 + j + 1)
                j = i - PIPE
                if j >= 0:
                    h, t = steps[j]
                    pe.wait_ge(sems["tr_ev"], b0 + j + 1)
                    b = 2 + j % 2
                    take(b)
                    for d in range(2):
                        for k in range(2):
                            last = mm(PB[b][:, tile(d)], MV[:, k, h * MEM + d * P:h * MEM + (d + 1) * P], MPT[:, j % 2, tile(k)], start=k == 0, stop=k == 1)
                            if d and k:
                                last.then_inc(*T.inc("pv_mm"))
                    free[b] = ("o_ev", j + 1)
            pe.wait_ge(sems["o_ev"], 16)
            take(0)
            project(8, 0, "norm_h", lambda k: MO[:, k, :], evbase=RES[N_MLP])
            take(4)
            norm_sum(N_MLP)
            for k in range(KT):
                pe.wait_ge(sems["norm_out"], N_MLP * KT + k + 1)
            end_stage()

            def mlp(n, up, down, nxt):
                def up_unit(i, j):
                    pe.wait_ge(slot_loaded[(UNIT[up] + j) % RING], 16 * ((UNIT[up] + j) // RING + 1 + i))
                    if not isinstance(i, int) or j >= 4:
                        pe.wait_ge(sems["relu"], 32 * n + i * RING + (j - 3))
                    w = W[:, (UNIT[up] + j) % RING, :].rearrange("p (k n) -> p k n", n=P)
                    for k in range(KT):
                        ins = pe.matmul(PB[j % 4][:, :], w[:, k, :], HN[:, k, :], start=k == 0, stop=k == KT - 1)
                    ins.then_inc(sems["w_used"], 1)
                for j in range(RING):
                    up_unit(0, j)
                with pe.Fori(1, 32 // RING) as i:
                    for j in range(RING):
                        up_unit(i, j)
                pe.wait_ge(sems["mlp_a"], 32 * (n + 1))

                def down_unit(i, m, g):
                    v = 4 * m + g
                    pe.wait_ge(slot_loaded[(UNIT[down] + v) % RING], 16 * ((UNIT[down] + v) // RING + 1 + i))
                    if g == 0 and not isinstance(i, int):
                        pe.wait_ge(sems["norm_h"], RES[nxt] + 2 * i + (m - 1))
                    w = W[:, (UNIT[down] + v) % RING, :].rearrange("p (k n) -> p k n", n=P)
                    for k in range(KT):
                        ins = pe.matmul(PB[m][:, :], w[:, k, :], MA[:, g * KT + k, :],
                                        start=g == 0 and k == 0, stop=g == 3 and k == KT - 1)
                    ins.then_inc(sems["w_used"], 1)
                for m in range(2):
                    for g in range(4):
                        down_unit(0, m, g)
                with pe.Fori(1, 4) as i:
                    for m in range(2):
                        for g in range(4):
                            down_unit(i, m, g)
                unit[0] += 64
                if nxt is not None:
                    norm_sum(nxt)
            mlp(0, "up", "down", N_FINAL)

            norm_sum(N_MIX0)
            end_stage()

            def rope_mm(j):
                if j < 5:
                    pe.wait_ge(sems["ev_act"], EV2 + j + 1)
                else:
                    pe.wait_ge(sems["a_sc"], j - 4)
                take(3)
                mm(PB[3][:, :], cst("rope_i" if j < 5 else "rope_a"), rope_plane(j)).then_inc(*T.inc("rope_mm"))
                free[3] = ("rope_ev", j + 1)
            for i in range(30):
                kind = project_tok if 18 <= i < 26 else None
                if kind:
                    project_tok(1, i, "ev_act", lambda k, t: HN[:, k, tile(t)], evbase=EV2 + i, banks=2)
                else:
                    project(1, i, "ev_act", hn, evbase=EV2 + i, banks=2, ready=N_MIX0 * KT if i == 0 else None)
                if 2 <= i < 7:
                    rope_mm(i - 2)
                if i == 7:
                    pe.wait_ge(sems["ev_act"], EV2 + 6)
                    for t in range(TT):
                        last = tr(PB[2][:, tile(t)], MISC[:, tile(t)])
                        if t == TT - 1:
                            last.then_inc(*T.inc("iw_tr"))
                    free[2] = ("iw_ev", 1)
                    for p in range(2):
                        take(4 + p)
                        mm(PB[4 + p][:, :], vec("gate_up", p * P, (p + 1) * P)[0:16], MISC[0:16, :]).then_inc(*T.inc("gate_mm"))
                        free[4 + p] = ("gate_in", p + 1)
                if 10 <= i < 18:
                    for n in range(3 * (i - 10), 3 * (i - 10) + 3):
                        t, h = INDEX_STEPS[n]
                        if n == 0:
                            pe.wait_ge(sems["rope_ev"], 5)
                        b = 6 + n % 2
                        r = slice(64 * (h % 2), 64 * (h % 2) + 64)
                        take(b)
                        mm(PB[b][:, 0:(t + 1) * P], IQ[r, h // 2, tile(t)], IK[r, 0:(t + 1) * P]).then_inc(*T.inc("idx_mm"))
                        free[b] = ("idx_r", n + 1)
                if 11 <= i < 19:
                    j = i - 11
                    pe.wait_ge(sems["a_sq"], j + 1)
                    take(2)
                    mm(PB[2][:, :], cst("ones"), SQA[:, j % 2, :]).then_inc(*T.inc("a_mm"))
                    free[2] = ("a_rs", j + 1)
                if 18 <= i < 26:
                    l = i - 18
                    if l:
                        pe.wait_ge(sems["lv_in"], 2 * l)
                    for n in range(4):
                        q, th = n // 2, n % 2
                        r = slice(64 * q, 64 * q + 64)
                        take(4 + n)
                        for e in range(4):
                            t, p = 2 * th + e // 2, e % 2
                            k_, q_ = (GK, GQ) if l == 0 else (GKE, GQE)
                            last = mm(PB[4 + n][:, tile(e)], k_[r, p, tile(t)], q_[r, p, tile(t)])
                            if e == 3:
                                last.then_inc(*T.inc("lvl_mm"))
                        free[4 + n] = ("lvl_ev", 4 * l + n + 1)
                if 19 <= i < 27:
                    rope_mm(5 + i - 19)

            pe.wait_ge(sems["ke_in"], 2)
            for n in range(2):
                take(n)
                for e in range(4):
                    t, p = 2 * n + e // 2, e % 2
                    last = tr(PB[n][:, tile(e)], GKE[:, p, tile(t)])
                    if e == 3:
                        last.then_inc(*T.inc("ke_tr"))
                free[n] = ("ke_ev", n + 1)
            pe.wait_ge(sems["ev_act"], EV2 + 30)
            for t in range(3):
                if t == 0 or t == 2:
                    take(2 + t // 2)
                pe.wait_ge(sems["ke_ev"], t // 2 + 1)
                for h in range(4):
                    r = slice(64 * (h % 2), 64 * (h % 2) + 64)
                    o = (256 * t if t < 2 else 0) + P * (h // 2)
                    last = mm(PB[2 + t // 2][r, o:o + P], GKT[:, t, h * 64:h * 64 + 64], GV[:, h, tile(t)])
                    if h == 3:
                        last.then_inc(*T.inc("kv2_mm"))
            pe.wait_ge(sems["att"], 28)
            for h in range(4):
                take(4 + h)
                for t in range(TT):
                    th, e = t // 2, 2 * (t % 2) + h // 2
                    mm(PB[4 + h][:, tile(t)], GV[:, h, tile(t)], ATT[:, 2 * (h % 2) + th, tile(e)], start=t == 0, stop=t == 0, skip_group_check=True)
            pe.wait_ge(sems["sh_ev"], 3)
            for h in range(4):
                r = slice(64 * (h % 2), 64 * (h % 2) + 64)
                for t in range(1, TT):
                    last = mm(PB[4 + h][:, tile(t)], GSH[r, t, P * (h // 2):P * (h // 2) + P], GQE[r, h // 2, tile(t)], start=False, stop=True, skip_group_check=True)
                    if t == 3:
                        last.then_inc(*T.inc("go_mm"))
                free[4 + h] = ("go_ev", h + 1)
            for h in range(4):
                pe.wait_ge(sems["go_sq"], h + 1)
                take(h)
                mm(PB[h][:, :], cst("ones"), GSQ[:, h, :]).then_inc(*T.inc("go_nm"))
                free[h] = ("go_rs", h + 1)

            pe.wait_ge(sems["rope_ev"], 13)
            steps = STEPS["A"]
            b0 = BASE["A"]
            for i in range(len(steps) + PIPE):
                if i < len(steps):
                    h, t = steps[i]
                    w = (t + 1) * P
                    b = 4 + i % 2
                    take(b)
                    mm(PB[b][:, 0:w], QA[:, h, tile(t)], KA[:, h, 0:w]).then_inc(*T.inc("sc_mm"))
                    free[b] = ("sc_exp", EXPB["A"] + i + 1)
                if 2 <= i < len(steps) + 2:
                    j = i - 2
                    pe.wait_ge(sems["prob"], b0 + j + 1)
                    take(0)
                    for k in range(steps[j][1] + 1):
                        last = tr(PB[0][:, tile(k)], APR[:, j % 2, tile(k)])
                        if k == steps[j][1]:
                            last.then_inc(*T.inc("tr_mm"))
                    free[0] = ("tr_ev", b0 + j + 1)
                j = i - PIPE
                if j >= 0:
                    h, t = steps[j]
                    pe.wait_ge(sems["tr_ev"], b0 + j + 1)
                    b = 2 + j % 2
                    take(b)
                    for k in range(t + 1):
                        last = mm(PB[b][:, 0:P], VA[:, h, tile(k)], APT[:, j % 2, tile(k)], start=k == 0, stop=k == t)
                        if k == t:
                            last.then_inc(*T.inc("pv_mm"))
                    free[b] = ("o_ev", 16 + j + 1)
            pe.wait_ge(sems["o_ev"], 32)
            take(0)
            project(8, 0, "norm_h", hn, evbase=RES[N_FFN0])
            take(4)
            norm_sum(N_FFN0)
            for k in range(KT):
                pe.wait_ge(sems["norm_out"], N_FFN0 * KT + k + 1)
            end_stage()
            mlp(1, "up_0", "down_0", N_MIX1)
            end_stage()

            for i in range(24):
                if i < 16:
                    project(1, i, "ev_act", hn, evbase=EV3 + i, ready=N_MIX1 * KT if i == 0 else None)
                else:
                    project_tok(1, i, "ev_act", lambda k, t: HN[:, k, tile(t)], evbase=EV3 + i)
                if 1 <= i < 17:
                    pe.wait_ge(sems["c_sq"], i)
                    take(4)
                    mm(PB[4][:, :], cst("ones"), CSQ[:, (i - 1) % 2, :]).then_inc(*T.inc("c_nm"))
                    free[4] = ("c_rs", i)
            pe.wait_ge(sems["c_sc"], 16)
            pe.wait_ge(sems["ev_act"], EV3 + 24)
            steps = STEPS["C"]
            b0 = BASE["C"]
            for i in range(len(steps) + PIPE + 1):
                if i < len(steps):
                    h, t = steps[i]
                    w = (t + 1) * P
                    b = 4 + i % 4
                    take(b)
                    mm(PB[b][:, 0:w], CQ[:, h, tile(t)], CK[:, h, 0:w]).then_inc(*T.inc("sc_mm"))
                    free[b] = ("c_la", i + 1)
                if 3 <= i < len(steps) + 3:
                    j = i - 3
                    pe.wait_ge(sems["c_prob"], j + 1)
                    take(0)
                    for k in range(steps[j][1] + 1):
                        last = tr(PB[0][:, tile(k)], CPR[:, j % 2, tile(k)])
                        if k == steps[j][1]:
                            last.then_inc(*T.inc("tr_mm"))
                    free[0] = ("tr_ev", b0 + j + 1)
                j = i - PIPE - 1
                if j >= 0:
                    h, t = steps[j]
                    pe.wait_ge(sems["tr_ev"], b0 + j + 1)
                    b = 2 + j % 2
                    take(b)
                    for k in range(t + 1):
                        last = mm(PB[b][:, 0:P], CV[:, h, tile(k)], CPT[:, j % 2, tile(k)], start=k == 0, stop=k == t)
                        if k == t:
                            last.then_inc(*T.inc("pv_mm"))
                    free[b] = ("o_ev", 32 + j + 1)
            pe.wait_ge(sems["o_ev"], 64)
            take(0)
            project(8, 0, "norm_h", hn, evbase=RES[N_FFN1])
            take(4)
            norm_sum(N_FFN1)
            for k in range(KT):
                pe.wait_ge(sems["norm_out"], N_FFN1 * KT + k + 1)
            end_stage()
            mlp(2, "up_1", "down_1", None)


def planes(a):
    a = np.ascontiguousarray(np.asarray(a).T)
    return np.ascontiguousarray(a.reshape(a.shape[0] // P, P, a.shape[1]).transpose(1, 0, 2))


def units(w):
    k, n = w.shape
    a = w.reshape(k // (KT * P), KT, P, n // P, P).transpose(3, 0, 2, 1, 4)
    return a.reshape(-1, P, KT * P)


def stream(i):
    w_in, w_ab, w_c = i["w_in"][0], i["w_in_ab_2"][0], i["w_in_c_2"][0]
    r = 512
    ab = {}
    o = 0
    for name, n in (("qa", 512), ("ka", 512), ("va", 512), ("iq", 512), ("ik", 64), ("iw", 8),
                    ("qb", 256), ("kb", 256), ("vb", 512), ("g", 16), ("og", 512)):
        ab[name] = w_ab[:, o:o + n]
        o += n
    misc = np.zeros((w_ab.shape[0], P), w_ab.dtype)
    misc[:, 0:16], misc[:, 32:40] = ab["g"], ab["iw"]
    parts = {
        "rwkv_lora": w_in[:, 3 * r:3 * r + 256], "rwkv_k": w_in[:, r:2 * r], "rwkv_r": w_in[:, 0:r],
        "rwkv_v": w_in[:, 2 * r:3 * r], "diff_q": w_in[:, 1792:1792 + r], "diff_k": w_in[:, 1792 + r:1792 + 2 * r],
        "diff_v": w_in[:, 1792 + 2 * r:1792 + 3 * r], "out": i["w_out"][0], "mem_k": i["w_mk"][0], "mem_v": i["w_mv"][0],
        "mem_q": i["w_mq"][0], "mem_o": i["w_mo"][0], "up": i["w_up"][0], "down": i["w_down"][0],
        "a_q": ab["qa"], "a_k": ab["ka"], "a_v": ab["va"], "i_q": ab["iq"],
        "i_k": np.concatenate([ab["ik"], ab["ik"]], 1), "misc": misc, "b_q": ab["qb"], "b_k": ab["kb"],
        "b_v": ab["vb"], "b_og": ab["og"], "out_ab": i["w_out_ab_2"][0],
        "up_0": i["w_up_2"][0], "down_0": i["w_down_2"][0],
        "c_q": w_c[:, 0:1024], "c_k": w_c[:, 1024:2048], "c_v": w_c[:, 2048:3072], "out_c": i["w_out_c_2"][0],
        "up_1": i["w_up_2"][1], "down_1": i["w_down_2"][1]}
    out = np.zeros((STREAM_UNITS, P, KT * P), np.float32)
    for name, n in STREAM:
        out[UNIT[name]:UNIT[name] + n] = units(parts[name])
    return out


def vectors(i):
    v = np.zeros((P, N_VEC), np.float32)

    def put(name, a):
        o, n = VO[name]
        v[:, o:o + n] = a.reshape(n, P).T
    put("norm_mix", i["norm_mix_w"][0])
    put("norm_mem", i["norm_mem_w"][0])
    put("norm_src", i["norm_src_w"][0])
    put("norm_mlp", i["norm_mlp_w"][0])
    put("norm_final", i["norm_final_w"])
    for l in range(2):
        put(f"g_mix{l}", i["g_mix_2"][l])
        put(f"g_ffn{l}", i["g_ffn_2"][l])
    mu = i["mu_shift"][0]
    put("mu", np.concatenate([mu[1536:1792], mu[512:1024], mu[0:512], mu[1024:1536]]))
    for name, key in (("w0", "w_decay0"), ("a0", "a0"), ("k_k", "k_k"), ("k_a", "k_a"), ("r_k", "r_k"),
                      ("lnx_w", "lnx_w"), ("lnx_b", "lnx_b"), ("subln", "subln_w"), ("gq_a", "gq_a_2"), ("gk_a", "gk_a_2"),
                      ("gq_c", "gq_c_2"), ("gk_c", "gk_c_2"), ("g_gla", "g_gla_2"), ("b_gate", "b_gate_2")):
        put(name, i[key][0].reshape(-1))
    o = VO["lam"][0]
    for n, key in enumerate(("lam_q1", "lam_q2", "lam_k1", "lam_k2")):
        v[0:64, o + n] = i[key][0]
    o = VO["dec_aaa_up"][0]
    v[0:64, o:o + 512] = i["w_decay_up"][0]
    v[64:128, o:o + 512] = i["a_up"][0]
    o = VO["g_up"][0]
    v[:, o:o + 512] = i["g_up"][0]
    o = VO["gate_up"][0]
    v[0:16, o:o + 256] = i["w_gate_up_2"][0]
    return v


def kernel(**inputs):
    from concourse import bacc
    from concourse.bass_utils import run_bass_kernel_spmd
    i = {k: np.asarray(v) for k, v in inputs.items()}
    nc = bacc.Bacc("TRN2", target_bir_lowering=False, num_devices=1, dynamic_dma_scratch_size=1024)
    arrays = {"x_in": planes(i["x"][0]), "mem_in": planes(i["mem"][0]), "weights_in": stream(i),
              "constants_in": constants(), "vectors_in": vectors(i)}
    aps = [nc.dram_tensor(n, a.shape, F32, kind="ExternalInput").ap() for n, a in arrays.items()]
    out = nc.dram_tensor("h_out", (P, KT, S), F32, kind="ExternalOutput").ap()
    build(nc, *aps, out)
    r = run_bass_kernel_spmd(nc, [arrays], core_ids=[0])
    h = r.results[0]["h_out"]
    return np.ascontiguousarray(h.transpose(2, 1, 0).reshape(1, S, KT * P))
```

```python
from contextlib import ExitStack
import math
import numpy as np
import concourse.bass as bass
from concourse import mybir

F32 = mybir.dt.float32
F32R = mybir.dt.float32r
ACT = mybir.ActivationFunctionType
ALU = mybir.AluOpType
AX = mybir.AxisListType

P = 128
S = 512
KT = 8
TT = S // P
MEM = 256
RING = 4
BODY = 8
DEC = math.exp(-0.5)
NEG = -1.0e30

STREAM = [("rwkv_lora", 2), ("rwkv_k", 4), ("rwkv_r", 4), ("rwkv_v", 4),
          ("diff_q", 4), ("diff_k", 4), ("diff_v", 4), ("out", 8),
          ("mem_k", 8), ("mem_v", 8), ("mem_q", 8), ("mem_o", 8),
          ("up0a", 16), ("down0a", 16), ("up0b", 16), ("down0b", 16),
          ("i_q", 4), ("i_k", 1), ("misc", 1), ("b_q", 2), ("b_k", 2),
          ("a_q", 4), ("a_k", 4), ("a_v", 4), ("b_v", 4), ("b_og", 4), ("out_ab", 8),
          ("up1a", 16), ("down1a", 16), ("up1b", 16), ("down1b", 16),
          ("c_q", 8), ("c_k", 8), ("c_v", 8), ("out_c", 8),
          ("up2a", 16), ("down2a", 16), ("up2b", 16), ("down2b", 16)]
UNIT = {}
UNITS = 0
for _name, _n in STREAM:
    UNIT[_name] = UNITS
    UNITS += _n
STREAM_UNITS = -(-UNITS // BODY) * BODY

CONSTS = [("ident", 128), ("ones", 128), ("bd_ones", 128), ("rope_a", 128), ("rope_i", 128),
          ("cos_a", 512), ("sin_a", 512), ("cos_i", 512), ("sin_i", 512),
          ("reset64", 512), ("reset128", 512),
          ("bd_strict", 128), ("bd_incl", 128), ("low_mask", 6 * 128), ("gla_mask", 8 * 128),
          ("chunk_bias", 64), ("strict", 128), ("strict_bias", 128), ("scalars", 8)]
CO = {}
N_CONST = 0
for _name, _n in CONSTS:
    CO[_name] = (N_CONST, _n)
    N_CONST += _n

VECS = [("norm_mix", 8), ("norm_mem", 8), ("norm_src", 8), ("norm_mlp", 8), ("norm_final", 8),
        ("g_mix0", 8), ("g_ffn0", 8), ("g_mix1", 8), ("g_ffn1", 8),
        ("mu", 14), ("w0", 4), ("a0", 4), ("k_k", 4), ("k_a", 4), ("r_k", 4), ("lnx_w", 4), ("lnx_b", 4),
        ("lam", 4), ("subln", 1), ("gq_a", 1), ("gk_a", 1), ("gq_c", 1), ("gk_c", 1), ("g_gla", 1),
        ("b_gate", 2), ("dec_aaa_up", 512), ("g_up", 512), ("gate_up", 256)]
VO = {}
N_VEC = 0
for _name, _n in VECS:
    VO[_name] = (N_VEC, _n)
    N_VEC += _n

RMS_EPS, EPS2, GN_EPS = 1e-5, 1e-6, 64e-5
SC = {"eps1": 0, "eps2": 1, "gn": 2, "kkb": 3, "one": 4}
KK_SCALE = 65536.0


def constants():
    c = np.zeros((P, N_CONST), np.float32)

    def put(name, a):
        o, n = CO[name]
        c[:, o:o + n] = a.reshape(P, n)
    i = np.arange(P)
    row, col = i[:, None], i[None, :]
    put("ident", np.eye(P))
    put("ones", np.ones((P, P)))
    put("bd_ones", (row // 64 == col // 64) * 1.0)
    t = np.arange(S)

    def rope(name, head, width):
        rot = width // 4
        half = rot // 2
        inv = np.power(500000.0, -np.arange(half, dtype=np.float32) * 2.0 / rot).astype(np.float32)
        ang = t.astype(np.float32)[None, :] * inv[:, None]
        cos, sin, m = np.ones((P, S)), np.zeros((P, S)), np.zeros((P, P))
        for base in range(0, P, width):
            for j in range(half):
                cos[base + j] = cos[base + half + j] = np.cos(ang[j])
                sin[base + j] = sin[base + half + j] = np.sin(ang[j])
                m[base + half + j, base + j] = -1.0
                m[base + j, base + half + j] = 1.0
        put("cos_" + name, cos)
        put("sin_" + name, sin)
        put("rope_" + name, m)
    rope("a", 0, 128)
    rope("i", 0, 64)
    put("reset64", np.broadcast_to((t % 64 != 0) * 1.0, (P, S)))
    put("reset128", np.broadcast_to((t % 128 != 0) * 1.0, (P, S)))
    same = row // 64 == col // 64
    put("bd_strict", (same & (row < col)) * 1.0)
    put("bd_incl", (same & (row <= col)) * 1.0)
    low = [((row // (2 * s) == col // (2 * s)) & (row % (2 * s) >= s) & (col % (2 * s) < s)) * 1.0
           for s in (1, 2, 4, 8, 16, 32)]
    put("low_mask", np.concatenate(low, 1))
    gla = [((row // (2 * s) == col // (2 * s)) & (col % (2 * s) >= s) & (row % (2 * s) < s)) * 1.0
           for s in (1, 2, 4, 8, 16, 32, 64)] + [(row == col) * 1.0]
    put("gla_mask", np.concatenate(gla, 1))
    put("chunk_bias", np.broadcast_to(np.where(row < 64, NEG, 0.0), (P, 64)))
    put("strict", (col < row) * 1.0)
    put("strict_bias", np.where(col < row, 0.0, NEG))
    s = np.zeros((P, 8))
    s[:, SC["eps1"]], s[:, SC["eps2"]], s[:, SC["gn"]] = RMS_EPS, EPS2, GN_EPS
    s[:, SC["kkb"]] = 0.5 * math.log(KK_SCALE)
    s[:, SC["one"]] = 1.0
    put("scalars", s)
    return c


class Count:

    def __init__(self, sems, own):
        self.sems, self.own, self.n, self.latest = sems, own, {}, None

    def inc(self, name=None):
        name = name or self.own
        self.n[name] = self.n.get(name, 0) + 1
        self.latest = (self.sems[name], self.n[name])
        return self.sems[name], 1


def build(nc, x_d, mem_d, w_d, c_d, v_d, out_d, stop=None):
    ctx = ExitStack()
    with ctx:
        def sb(name, shape):
            return ctx.enter_context(nc.sbuf_tensor(name, shape, F32))

        PART = 16

        def sb_both(name, shape):
            offset = nc.sbuf_base
            t = sb(name, shape)
            return t, [nc.alloc_sbuf_tensor_at(f"{name}_r{a}", [P, min(PART, shape[1] - a), S], F32R, offset=offset + a * S * 4)
                       for a in range(0, shape[1], PART)]
        H = sb("H", [P, KT, S])
        HN, (HNR,) = sb_both("HN", [P, KT, S])
        W = sb("W", [P, RING, KT * P])
        WH = ctx.enter_context(nc.sbuf_tensor("WH", [P, 2, KT * P], F32R))
        WL = ctx.enter_context(nc.sbuf_tensor("WL", [P, 2, KT * P], F32R))
        NA = 61
        AR, AR_PARTS = sb_both("AR", [P, NA, S])
        C = sb("C", [P, N_CONST])
        V = sb("V", [P, N_VEC])
        SM = sb("SM", [P, 192])
        PB = [ctx.enter_context(nc.psum_tensor(f"PB{i}", [P, S], F32)) for i in range(8)]

        names = ["w_used", "w_round", "w_split", "x_hi", "x_lo", "hid_sq", "hid_hi", "half_h", "act_step", "dve_step", "pool_step", "stage", "x_in", "mem_in", "c_in", "v_in", "stored",
                 "norm_h", "norm_sq", "norm_acc", "norm_ms", "norm_rs", "norm_out",
                 "ev_act", "ev_dve", "lora_in", "kk_sq", "bonus_in", "prep_mm", "prep_act", "prep_dve",
                 "sig_ready", "a_ready", "kkln_in", "kk_rs", "cs_ready", "exp_ready", "exp_used", "lam_in", "lam_mm", "lam_exp",
                 "sc_mm", "sc_max", "sc_exp", "prob", "tr_mm", "tr_ev", "pv_mm", "o_ev",
                 "on_sq", "on_mm", "on_rs", "on_out",
                 "ch_in", "ch_tr", "ch_trev", "ch_aq", "ch_aqev", "ch_t0", "ch_t0ev", "lv_x", "lv_xev", "lv_y", "lv_yev",
                 "w1_mm", "w1_ev", "kv_mm", "g_ev", "sa_mm", "sa_ev", "gu_mm", "y_mm", "y_ev",
                 "gn_in", "gn_mm", "gn_c", "gn_sq", "gn_rs", "mix_out",
                 "relu", "mlp_a",
                 "rope_mm", "rope_ev", "iw_tr", "iw_ev", "gate_mm", "gate_in", "gate_ln", "gb_ready", "idx_mm", "idx_r", "idx_acc",
                 "a_sq", "a_mm", "a_rs", "a_sc", "lv_d", "lv_e", "lv_in", "lvl_mm", "lvl_ev", "att",
                 "g_eb", "g_ed", "gla_out", "g_ede", "ke_in", "ke_tr", "ke_ev", "kv2_mm", "sh_ev", "go_mm", "go_sq", "go_nm", "go_rs", "go_ev",
                 "c_sq", "c_nm", "c_rs", "c_sc", "c_l", "c_nl", "c_la", "c_prob"]
        sems = {n: ctx.enter_context(nc.semaphore(n)) for n in names}
        slot_loaded = [ctx.enter_context(nc.semaphore(f"slot_loaded{i}")) for i in range(RING)]

        def cst(name, a=0, b=None):
            o, n = CO[name]
            return C[:, o + a:o + (n if b is None else b)]

        def vec(name, a=0, b=None):
            o, n = VO[name]
            return V[:, o + a:o + (n if b is None else b)]

        def sc(name):
            return cst("scalars", SC[name], SC[name] + 1)

        flat = AR[:, :, :].rearrange("p a n -> p (a n)")
        PW = S + 1
        PX = flat[:, 0:14 * PW].rearrange("p (m n) -> p m n", n=PW)
        LORA, GD, K0, R0, V0 = 0, 1, 2, 6, 10
        SIG, CS, AG, KK, BON, GT = (AR[:, a:a + 4, :] for a in (15, 19, 23, 27, 31, 35))
        TMP = AR[:, 39:41, :]
        DQ, DK, DV = (AR[:, a:a + 4, :] for a in (41, 45, 49))
        SQ, ACC, LN, RS = AR[:, 48:56, :], AR[:, 56, :], AR[:, 57, :], AR[:, 58, :]
        PR1, PR2, PT, OSQ, OLN = AR[:, 53:55, :], AR[:, 55:57, :], AR[:, 57:59, :], AR[:, 59, :], AR[:, 60, :]
        def arr(a, b):
            return AR_PARTS[a // PART][:, a % PART:a % PART + b - a, :]
        MAH, MAL, RL = arr(0, 16), arr(16, 32), AR[:, 59:61, :]

        STEPS = {"diff": [(h, t) for h in range(4) for t in range(TT)],
                 "mem": [(h, t) for h in range(4) for t in range(TT)],
                 "A": [(h, t) for t in range(TT) for h in range(4)],
                 "C": [(h, t) for h in range(8) for t in range(TT)]}
        MAPS = {"diff": 2, "mem": 1, "A": 1, "C": 0}
        BASE, EXPB, s0, e0 = {}, {}, 0, 0
        for a in STEPS:
            BASE[a], EXPB[a] = s0, e0
            s0 += len(STEPS[a])
            e0 += len(STEPS[a]) * MAPS[a]
        PIPE = 3
        N_MIX, N_SRC, N_MEM, N_MLP, N_FINAL, N_MIX0, N_FFN0, N_MIX1, N_FFN1 = range(9)
        RES = {N_MEM: 0, N_MLP: 8, N_FINAL: 16, N_FFN0: 24, N_MIX1: 32, N_FFN1: 40, None: 48}

        LAMP, LAME, NLAM, SUBW, KA1 = SM[:, 0:2], SM[:, 2:4], SM[:, 4:5], SM[:, 5:6], SM[:, 6:10]
        ECH = SM[:, 16:48].rearrange("p (a c) -> p a c", c=8)

        def nmax(i, m=0, n=1):
            return SM[:, 48 + 2 * (i % 4) + m:48 + 2 * (i % 4) + m + n]

        def psum_of(i, m=0, n=1):
            return SM[:, 56 + 2 * (i % 4) + m:56 + 2 * (i % 4) + m + n]

        def recip(i, m=0, n=1):
            return SM[:, 64 + 2 * (i % 4) + m:64 + 2 * (i % 4) + m + n]

        def tile(t):
            return slice(t * P, (t + 1) * P)

        def pk(a, n=1, w=None):
            return AR[:, a:a + n, :].rearrange("p a (h n) -> p (a h) n", n=w)
        AQ, BQ = pk(41, 4, 256), pk(45, 4, 256)
        TI, UI, XI = pk(49, 2, 128), pk(51, 2, 128), pk(53, 2, 128)
        TOKA, TOKB, TOKK, TOKV = (pk(a, 1, 128) for a in (55, 56, 57, 58))
        BP, KP = pk(59, 1, 128), pk(60, 1, 128)
        TA, W1, SA, P1 = pk(39, 1, 128), pk(40, 1, 128), pk(18, 1, 128), pk(14 + 7, 1, 128)
        GS = [pk(a, 1, 128) for a in (15, 16, 17)]
        TG = pk(19, 1, 128)

        mview = AR[:, 0:8, :].rearrange("p a (b m) -> p (a b) m", m=MEM)
        MT, MN = mview[:, 0:8, :], mview[:, 8:16, :]
        MK = AR[:, 8:12, :].rearrange("p a (b m) -> p (a b) m", m=MEM)
        MV = AR[:, 12:16, :].rearrange("p (t a) n -> p t (a n)", t=2)
        MNH = arr(36, 40).rearrange("p a (b m) -> p (a b) m", m=MEM)
        MNL = arr(4, 8).rearrange("p a (b m) -> p (a b) m", m=MEM)
        MQ, MO = AR[:, 16:24, :], AR[:, 24:32, :]
        MPR, MPT = AR[:, 32:34, :], AR[:, 34:36, :]


        SPLITS = {"mix": [53, 54, 55, 56, 57, 59, 60, 58], "out": range(24, 32), "src": None, "mem": range(24, 32),
                  "mo": range(16, 24), "mlp0": range(40, 48), "ab": [5, 30, 34, 56, 57, 59, 60, 58],
                  "oab": range(18, 26), "mlp1": range(40, 48), "c": range(24, 32), "oc": range(0, 8),
                  "mlp2": range(40, 48)}
        SPLIT_NO = {name: n for n, name in enumerate(SPLITS)}

        def x_full(x, k):
            return MN[:, k, :] if x == "src" else MO[:, k, :] if x == "mo" else HN[:, k, :]

        def x_hi(x, k):
            return MNH[:, k, :] if x == "src" else arr(SPLITS[x][k], SPLITS[x][k] + 1)[:, 0, :]

        def x_lo(x, k):
            return MNL[:, k, :] if x == "src" else arr(24 + k, 25 + k)[:, 0, :] if x == "mo" else HNR[:, k, :]

        IQ, IK, MISC = AR[:, 0:4, :], AR[:, 4, :], AR[:, 47, :]
        QA, KA, VA = AR[:, 6:10, :], AR[:, 10:14, :], AR[:, 14:18, :]
        GQ, GK, GV, OG = AR[:, 18:20, :], AR[:, 20:22, :], AR[:, 22:26, :], AR[:, 26:30, :]
        SCORE, WORK, RLU, T1 = AR[:, 30:34, :], AR[:, 41, :], AR[:, 35:37, :], AR[:, 37, :]
        SQA, RA, GB = AR[:, 38:40, :], AR[:, 40:42, :], AR[:, 42:44, :]
        GE = [AR[:, 44:46, :], AR[:, 46:48, :]]
        GQE, GKE, ATT, LV = AR[:, 48:50, :], AR[:, 50:52, :], AR[:, 52:56, :], AR[:, 35:37, :]
        GEB, GED = AR[:, 0:2, :], AR[:, 2:4, :]
        GKT = AR[:, 56:58, :].rearrange("p a (t n) -> p (a t) n", n=256)
        GSH = AR[:, 58:60, :].rearrange("p a (t n) -> p (a t) n", n=256)
        GSQ = AR[:, 44:48, :]
        APR, APT = AR[:, 35:37, :], AR[:, 38:40, :]
        EQ, PRE = AR[:, 37, :], AR[:, 40, :]
        IW = SM[:, 80:112].rearrange("p (t h) -> p t h", h=8)
        TOP = SM[:, 112:120]
        NGT = SM[:, 120:121]
        GQS, GCS = SM[:, 121:122], SM[:, 122:123]
        EV2 = 50
        EV3 = EV2 + 30
        LEVELS = [None, 1, 2, 4, 8, 16, 32, 64]
        INDEX_STEPS = [(t, h) for t in range(1, TT) for h in range(8)]

        def rope_plane(j):
            return IQ[:, j, :] if j < 4 else IK if j == 4 else QA[:, j - 5, :] if j < 9 else KA[:, j - 9, :]

        CQ, CK, CV = AR[:, 0:8, :], AR[:, 8:16, :], AR[:, 16:24, :]
        CL, CN, CR, CPR, CPT = (AR[:, a:a + 2, :] for a in (24, 26, 28, 30, 32))
        CSQ, CRS = AR[:, 34:36, :], AR[:, 36:38, :]
        def PT_of(name):
            return {"diff": PT, "mem": MPT, "A": APT, "C": CPT}[name]

        block = ctx.enter_context(nc.Block())

        @block.sync
        def _(sp):
            sp.dma_start(C[:, :], c_d).then_inc(sems["c_in"], 16)
            for j in range(RING):
                sp.dma_start(W[:, j, :], w_d[j, :, :]).then_inc(slot_loaded[j], 16)
            with sp.Fori(1, STREAM_UNITS // RING) as i:
                for j in range(RING):
                    sp.wait_ge(sems["w_split"], i * RING + (j - RING + 1))
                    sp.dma_start(W[:, j, :], w_d[bass.ds(i * RING + j, 1), :, :].rearrange("a p n -> p (a n)"))\
                        .then_inc(slot_loaded[j], 16)
            for k in range(KT):
                sp.wait_ge(sems["norm_h"], RES[None] + k + 1)
                sp.dma_start(out_d[:, k, :], H[:, k, :]).then_inc(sems["stored"], 16)
            sp.wait_ge(sems["stored"], 16 * KT)

        @block.gpsimd
        def _(pool):
            def split_unit(i, j):
                pool.wait_ge(slot_loaded[j % RING], 16 * (BODY // RING * i + (j // RING + 1)))
                if not isinstance(i, int) or j >= 2:
                    pool.wait_ge(sems["w_used"], BODY * i + (j - 1))
                w = W[:, j % RING, :]
                pool.tensor_tensor(WH[:, j % 2, :], w, ones, ALU.mult).then_inc(sems["w_round"], 1)
                pool.wait_ge(sems["w_round"], BODY * i + (j + 1))
                pool.tensor_tensor(WL[:, j % 2, :], w, WH[:, j % 2, :].bitcast(F32), ALU.subtract)\
                    .then_inc(sems["w_split"], 1)
            ones = cst("ones", 0, 1).to_broadcast([P, KT * P])
            pool.wait_ge(sems["c_in"], 16)
            for j in range(BODY):
                split_unit(0, j)
            with pool.Fori(1, STREAM_UNITS // BODY) as i:
                for j in range(BODY):
                    split_unit(i, j)

        @block.scalar
        def _(act):
            A = Count(sems, "act_step")
            ends = [0]

            def end_stage():
                ends[0] += 1
                act.drain().then_inc(sems["stage"], 1)
                act.wait_ge(sems["stage"], 3 * ends[0])

            def f(out, in_, func, **k):
                return act.activation(out, in_, func, **k)

            def rstd(n, eps, w=S):
                act.wait_ge(sems["norm_ms"], n + 1)
                f(LN[:, 0:w], PB[4][:, 0:w], ACT.Ln, scale=1.0 / 1024, bias=sc(eps)).then_inc(*A.inc())
                act.wait_ge(*A.latest)
                f(RS[:, 0:w], LN[:, 0:w], ACT.Exp, scale=-0.5).then_inc(*A.inc("norm_rs"))

            def round_x(x, norm=None):
                for k in range(KT):
                    if norm is not None:
                        act.wait_ge(sems["norm_out"], norm * KT + k + 1)
                    f(x_hi(x, k), x_full(x, k), ACT.Copy).then_inc(*A.inc("x_hi"))

            def used(name, i):
                act.wait_ge(sems["w_used"], UNIT[name] + i + 1)

            act.preload_act_table_set("natural_log_exp_and_others")
            act.dma_start(H[:, :, :], x_d).then_inc(sems["x_in"], 16)
            act.dma_start(V[:, :], v_d).then_inc(sems["v_in"], 16)
            act.wait_ge(sems["c_in"], 16)
            act.wait_ge(sems["v_in"], 16)
            act.wait_ge(sems["x_in"], 16)
            for k in range(KT):
                f(SQ[:, k, :], H[:, k, :], ACT.Square).then_inc(*A.inc("norm_sq"))
            act.wait_ge(sems["lam_mm"], 1)
            f(LAME, PB[7][:, 0:2], ACT.Exp).then_inc(*A.inc("lam_exp"))
            rstd(N_MIX, "eps1")
            round_x("mix", N_MIX)

            for m in range(14):
                used("rwkv_lora", m)
                f(PX[:, m, 1:PW], PB[m % 4][:, :], ACT.Copy).then_inc(*A.inc("ev_act"))
                if m == 5:
                    act.wait_ge(sems["lora_in"], 2)
                    f(PX[0:64, LORA, 1:PW], PX[0:64, LORA, 1:PW], ACT.Tanh).then_inc(*A.inc())
                    f(PX[:, GD, 1:PW], PX[:, GD, 1:PW], ACT.Sigmoid).then_inc(*A.inc("sig_ready"))
            for p in range(4):
                act.wait_ge(sems["prep_mm"], p + 1)
                f(SIG[:, p, :], PB[4 + p][:, :], ACT.Sigmoid, bias=vec("w0", p, p + 1)).then_inc(*A.inc("prep_act"))
            for p in range(4):
                act.wait_ge(sems["prep_mm"], 4 + p + 1)
                f(AG[:, p, :], PB[4 + p][:, :], ACT.Sigmoid, bias=vec("a0", p, p + 1)).then_inc(*A.inc("prep_act"))
            for p in range(4):
                act.wait_ge(sems["prep_mm"], 8 + p + 1)
                f(GT[:, p, :], PB[4 + p][:, :], ACT.Copy).then_inc(*A.inc("prep_act"))
            act.preload_act_table_set("natural_log_exp_and_others")
            for m in range(4):
                used("diff_q", m)
                f(DQ[:, m, :], PB[(14 + m) % 4][:, :], ACT.Copy, scale=0.125).then_inc(*A.inc("ev_act"))
            for p in range(4):
                act.wait_ge(sems["kkln_in"], p + 1)
                f(CS[:, p, :], CS[:, p, :], ACT.Ln).then_inc(*A.inc())
                act.wait_ge(*A.latest)
                f(CS[:, p, :], CS[:, p, :], ACT.Exp, scale=-0.5, bias=sc("kkb")).then_inc(*A.inc("kk_rs"))
            for m in range(4):
                used("diff_k", m)
                f(DK[:, m, :], PB[(18 + m) % 4][:, :], ACT.Copy).then_inc(*A.inc("ev_act"))
            for p in range(4):
                act.wait_ge(sems["cs_ready"], p + 1)
                f(SIG[:, p, :], SIG[:, p, :], ACT.Exp, scale=-DEC).then_inc(*A.inc("exp_ready"))
                if p >= 2:
                    act.wait_ge(sems["exp_used"], p - 1)
                f(TMP[:, p % 2, :], CS[:, p, :], ACT.Exp, scale=DEC).then_inc(*A.inc("exp_ready"))
                f(CS[:, p, :], CS[:, p, :], ACT.Exp, scale=-DEC).then_inc(*A.inc("exp_ready"))
            for m in range(4):
                used("diff_v", m)
                f(DV[:, m, :], PB[(22 + m) % 4][:, :], ACT.Copy).then_inc(*A.inc("ev_act"))

            def tr_evac(name, j, n):
                b = BASE[name]
                act.wait_ge(sems["tr_mm"], b + j + 1)
                if j >= 2:
                    act.wait_ge(sems["pv_mm"], b + j - 1)
                f(PT_of(name)[:, j % 2, 0:n * P], PB[0][:, 0:n * P], ACT.Copy).then_inc(*A.inc("tr_ev"))

            steps = STEPS["diff"]
            for i in range(len(steps) + PIPE + 2):
                if i < len(steps):
                    w = (steps[i][1] + 1) * P
                    act.wait_ge(sems["sc_max"], i + 1)
                    if i >= 2:
                        act.wait_ge(sems["tr_mm"], i - 1)
                    f(PR1[:, i % 2, 0:w], PB[4 + 2 * (i % 2)][:, 0:w], ACT.Exp, bias=nmax(i, 0), accum_out=psum_of(i, 0))\
                        .then_inc(*A.inc("sc_exp"))
                    f(PR2[:, i % 2, 0:w], PB[5 + 2 * (i % 2)][:, 0:w], ACT.Exp, bias=nmax(i, 1), accum_out=psum_of(i, 1))\
                        .then_inc(*A.inc("sc_exp"))
                if 2 <= i < len(steps) + 2:
                    tr_evac("diff", i - 2, steps[i - 2][1] + 1)
                j = i - PIPE
                if 0 <= j < len(steps) and steps[j][1] == TT - 1:
                    h = steps[j][0]
                    act.wait_ge(sems["pv_mm"], j + 1)
                    if h:
                        act.wait_ge(sems["on_mm"], h)
                    f(OSQ, PB[2 + h % 2][:, :], ACT.Square).then_inc(*A.inc("on_sq"))
                j = i - PIPE - 1
                if 0 <= j < len(steps) and steps[j][1] == TT - 1:
                    h = steps[j][0]
                    act.wait_ge(sems["on_mm"], h + 1)
                    if h:
                        act.wait_ge(sems["on_out"], h)
                    f(OLN, PB[1][:, :], ACT.Ln, scale=1.0 / P, bias=sc("eps1")).then_inc(*A.inc())
                    act.wait_ge(*A.latest)
                    f(OLN, OLN, ACT.Exp, scale=-0.5).then_inc(*A.inc("on_rs"))
            end_stage()

            for t in range(TT):
                for n, dst in enumerate((TOKA, TOKV, TOKB, TOKK)):
                    act.wait_ge(sems["ch_tr"], 4 * t + n + 1)
                    f(dst, PB[4 + n][:, :].rearrange("p (a n) -> p a n", n=P), ACT.Copy).then_inc(*A.inc("ch_trev"))
                act.wait_ge(sems["w1_mm"], 3 * t + 1)
                f(P1, PB[4][:, :].rearrange("p (a n) -> p a n", n=P), ACT.Copy).then_inc(*A.inc("w1_ev"))
                act.wait_ge(sems["w1_mm"], 3 * t + 2)
                f(TA, PB[5][:, :].rearrange("p (a n) -> p a n", n=P), ACT.Copy).then_inc(*A.inc("w1_ev"))
                act.wait_ge(sems["w1_mm"], 3 * t + 3)
                f(W1, PB[6][:, :].rearrange("p (a n) -> p a n", n=P), ACT.Copy, scale=-1.0).then_inc(*A.inc("w1_ev"))
                act.wait_ge(sems["y_mm"], t + 1)
                f(HN[:, 0:4, tile(t)], PB[7][:, :].rearrange("p (a n) -> p a n", n=P), ACT.Copy).then_inc(*A.inc("y_ev"))
                end_stage()
            for p in range(4):
                act.wait_ge(sems["gn_c"], p + 1)
                f(SIG[:, p, :], HN[:, p, :], ACT.Square).then_inc(*A.inc("gn_sq"))
            for p in range(4):
                act.wait_ge(sems["gn_mm"], 4 + p + 1)
                f(SIG[:, p, :], PB[4 + p][:, :], ACT.Ln, scale=1.0 / 64, bias=sc("gn")).then_inc(*A.inc())
                act.wait_ge(*A.latest)
                f(SIG[:, p, :], SIG[:, p, :], ACT.Exp, scale=-0.5).then_inc(*A.inc("gn_rs"))
            end_stage()

            act.dma_start(MT, mem_d).then_inc(sems["mem_in"], 16)
            round_x("out")
            act.wait_ge(sems["mem_in"], 16)
            for k in range(KT):
                f(SQ[:, k, 0:MEM], MT[:, k, :], ACT.Square).then_inc(*A.inc("norm_sq"))
            rstd(N_SRC, "eps1", MEM)
            round_x("src", N_SRC)
            for k in range(KT):
                act.wait_ge(sems["norm_h"], RES[N_MEM] + k + 1)
                f(SQ[:, k, :], H[:, k, :], ACT.Square).then_inc(*A.inc("norm_sq"))
            rstd(N_MEM, "eps1")
            round_x("mem", N_MEM)
            for m in range(8):
                used("mem_k", m)
                f(MK[:, m, :], PB[m % 4][:, 0:MEM], ACT.Copy).then_inc(*A.inc("ev_act"))
            for m in range(8):
                used("mem_v", m)
                f(MV[:, :, tile(m)], PB[m % 4][:, 0:MEM].rearrange("p (t n) -> p t n", t=2), ACT.Copy)\
                    .then_inc(*A.inc("ev_act"))
            for m in range(8):
                used("mem_q", m)
                f(MQ[:, m, :], PB[m % 4][:, :], ACT.Copy, scale=1.0 / 16).then_inc(*A.inc("ev_act"))
            steps = STEPS["mem"]
            b = BASE["mem"]
            for i in range(len(steps) + PIPE):
                if i < len(steps):
                    act.wait_ge(sems["sc_max"], b + i + 1)
                    if i >= 2:
                        act.wait_ge(sems["tr_mm"], b + i - 1)
                    f(MPR[:, i % 2, 0:MEM], PB[4 + i % 2][:, 0:MEM], ACT.Exp, bias=nmax(i), accum_out=psum_of(i))\
                        .then_inc(*A.inc("sc_exp"))
                if 2 <= i < len(steps) + 2:
                    tr_evac("mem", i - 2, 2)
                if i >= PIPE:
                    h, t = steps[i - PIPE]
                    act.wait_ge(sems["pv_mm"], b + i - PIPE + 1)
                    f(MO[:, 2 * h:2 * h + 2, tile(t)], PB[2 + (i - PIPE) % 2][:, 0:MEM].rearrange("p (j n) -> p j n", j=2), ACT.Copy)\
                        .then_inc(*A.inc("o_ev"))
            act.wait_ge(*A.latest)
            round_x("mo")
            for k in range(KT):
                act.wait_ge(sems["norm_h"], RES[N_MLP] + k + 1)
                f(SQ[:, k, :], H[:, k, :], ACT.Square).then_inc(*A.inc("norm_sq"))
            rstd(N_MLP, "eps1")
            round_x("mlp0", N_MLP)
            end_stage()

            def mlp(n, nxt, eps):
                for half in range(2):
                    done = 32 * n + 16 * half
                    up = UNIT[f"up{n}{'ab'[half]}"]

                    def hidden_tile(i, j):
                        act.wait_ge(sems["w_used"], i * 4 + (up + j + 1))
                        if not isinstance(i, int) or j >= 2:
                            act.wait_ge(sems["mlp_a"], i * 4 + (done + j - 1))
                        act.activation(RL[:, j % 2, :], PB[j][:, :], ACT.Relu).then_inc(sems["relu"], 1)
                        act.wait_ge(sems["relu"], i * 4 + (done + j + 1))
                        act.activation(RL[:, j % 2, :], RL[:, j % 2, :], ACT.Square).then_inc(sems["hid_sq"], 1)
                        act.wait_ge(sems["hid_sq"], i * 4 + (done + j + 1))
                        hi = MAH[:, i * 4 + j, :] if isinstance(i, int) else MAH[:, bass.ds(i * 4 + j, 1), :].rearrange("p a n -> p (a n)")
                        act.activation(hi, RL[:, j % 2, :], ACT.Copy).then_inc(sems["hid_hi"], 1)
                    for j in range(4):
                        hidden_tile(0, j)
                    with act.Fori(1, 4) as i:
                        for j in range(4):
                            hidden_tile(i, j)
                if nxt is None:
                    return
                for k in range(KT):
                    act.wait_ge(sems["norm_h"], RES[nxt] + k + 1)
                    f(SQ[:, k, :], H[:, k, :], ACT.Square).then_inc(*A.inc("norm_sq"))
                rstd(nxt, eps)
            mlp(0, N_FINAL, "eps1")

            for k in range(KT):
                act.wait_ge(sems["norm_out"], N_FINAL * KT + k + 1)
                f(SQ[:, k, :], H[:, k, :], ACT.Square).then_inc(*A.inc("norm_sq"))
            rstd(N_MIX0, "eps2")
            round_x("ab", N_MIX0)
            end_stage()

            def ev2(i, out, scale=1.0, func=ACT.Copy):
                act.wait_ge(sems["w_used"], UNIT["i_q"] + i + 1)
                f(out, PB[i % 2][:, :], func, scale=scale).then_inc(*A.inc("ev_act"))

            def head_rstd(j, bank, out, done, nm, nr):
                act.wait_ge(sems[nm], j + 1)
                if j >= 2:
                    act.wait_ge(sems[done], j - 1)
                f(out, PB[bank][:, :], ACT.Ln, scale=1.0 / P, bias=sc("eps2")).then_inc(*A.inc())
                act.wait_ge(*A.latest)
                f(out, out, ACT.Exp, scale=-0.5).then_inc(*A.inc(nr))
            for i in range(30):
                dst, s_ = ((IQ[:, i, :], 1.0) if i < 4 else (IK, 1.0) if i == 4 else (MISC, 1.0) if i == 5 else
                           (GQ[:, i - 6, :], 0.125) if i < 8 else (GK[:, i - 8, :], 1.0) if i < 10 else
                           (QA[:, i - 10, :], 1.0) if i < 14 else (KA[:, i - 14, :], 1.0) if i < 18 else
                           (VA[:, i - 18, :], 1.0) if i < 22 else (GV[:, i - 22, :], 1.0) if i < 26 else
                           (OG[:, i - 26, :], 1.0))
                if i < 26:
                    ev2(i, dst, s_)
                else:
                    ev2(i, dst, 1.0, ACT.Silu)
                if i == 9:
                    for p in range(2):
                        act.wait_ge(sems["gate_in"], p + 1)
                        f(GE[1][:, p, :], GE[0][:, p, :], ACT.Abs).then_inc(*A.inc())
                    act.wait_ge(*A.latest)
                    f(GE[1], GE[1], ACT.Exp, scale=-1.0).then_inc(*A.inc())
                    act.wait_ge(*A.latest)
                    f(GE[1], GE[1], ACT.Ln, bias=sc("one")).then_inc(*A.inc("gate_ln"))
                if 10 <= i < 18:
                    j = i - 10
                    if j >= 2:
                        act.wait_ge(sems["a_mm"], j - 1)
                    act.wait_ge(*A.latest)
                    f(SQA[:, j % 2, :], dst, ACT.Square).then_inc(*A.inc("a_sq"))
                    for n in range(3 * j, 3 * j + 3):
                        w = (INDEX_STEPS[n][0] + 1) * P
                        act.wait_ge(sems["idx_mm"], n + 1)
                        if n >= 2:
                            act.wait_ge(sems["idx_acc"], n - 1)
                        f(RLU[:, n % 2, 0:w], PB[6 + n % 2][:, 0:w], ACT.Relu, scale=0.125).then_inc(*A.inc("idx_r"))
                if 11 <= i < 19:
                    head_rstd(i - 11, 2, RA[:, (i - 11) % 2, :], "a_sc", "a_mm", "a_rs")
                if 18 <= i < 25:
                    l = i - 17
                    act.wait_ge(sems["lv_d"], l)
                    f(GE[l % 2], GE[l % 2], ACT.Abs).then_inc(*A.inc())
                    act.wait_ge(*A.latest)
                    f(GE[l % 2], GE[l % 2], ACT.Exp, scale=-1.0 / 16).then_inc(*A.inc("lv_e"))
            act.preload_act_table_set("natural_log_exp_and_others")
            f(GEB, GB, ACT.Exp, scale=1.0 / 16).then_inc(*A.inc("g_eb"))
            act.wait_ge(sems["g_ed"], 1)
            f(GED, GED, ACT.Exp, scale=1.0 / 16).then_inc(*A.inc("g_ede"))
            for n in range(2):
                act.wait_ge(sems["ke_tr"], n + 1)
                f(GKT[:, 2 * n:2 * n + 2, :], PB[n][:, :].rearrange("p (t n) -> p t n", n=256), ACT.Copy)\
                    .then_inc(*A.inc("ke_ev"))
            for h in range(4):
                act.wait_ge(sems["go_mm"], h + 1)
                f(GSQ[:, h, :], PB[4 + h][:, :], ACT.Square).then_inc(*A.inc("go_sq"))
            for h in range(4):
                act.wait_ge(sems["go_nm"], h + 1)
                f(GSQ[:, h, :], PB[h][:, :], ACT.Ln, scale=1.0 / P, bias=sc("eps2")).then_inc(*A.inc())
            act.wait_ge(*A.latest)
            for h in range(4):
                f(GSQ[:, h, :], GSQ[:, h, :], ACT.Exp, scale=-0.5).then_inc(*A.inc("go_rs"))

            steps = STEPS["A"]
            b = BASE["A"]
            for i in range(len(steps) + PIPE):
                if i < len(steps):
                    w = (steps[i][1] + 1) * P
                    act.wait_ge(sems["sc_max"], b + i + 1)
                    if i >= 2:
                        act.wait_ge(sems["tr_mm"], b + i - 1)
                    f(APR[:, i % 2, 0:w], PB[4 + i % 2][:, 0:w], ACT.Exp, bias=nmax(i), accum_out=psum_of(i))\
                        .then_inc(*A.inc("sc_exp"))
                if 2 <= i < len(steps) + 2:
                    tr_evac("A", i - 2, steps[i - 2][1] + 1)
                if i >= PIPE:
                    h, t = steps[i - PIPE]
                    act.wait_ge(sems["pv_mm"], b + i - PIPE + 1)
                    f(HN[:, h, tile(t)], PB[2 + (i - PIPE) % 2][:, 0:P], ACT.Copy).then_inc(*A.inc("o_ev"))
            act.wait_ge(*A.latest)
            act.wait_ge(sems["gla_out"], 4)
            round_x("oab")
            for k in range(KT):
                act.wait_ge(sems["norm_h"], RES[N_FFN0] + k + 1)
                f(SQ[:, k, :], H[:, k, :], ACT.Square).then_inc(*A.inc("norm_sq"))
            rstd(N_FFN0, "eps2")
            round_x("mlp1", N_FFN0)
            end_stage()
            mlp(1, N_MIX1, "eps2")
            round_x("c", N_MIX1)
            end_stage()

            for i in range(25):
                if i < 24:
                    act.wait_ge(sems["w_used"], UNIT["c_q"] + i + 1)
                    dst = CQ[:, i, :] if i < 8 else CK[:, i - 8, :] if i < 16 else CV[:, i - 16, :]
                    f(dst, PB[i % 4][:, :], ACT.Copy).then_inc(*A.inc("ev_act"))
                    if i < 16:
                        if i >= 2:
                            act.wait_ge(sems["c_nm"], i - 1)
                        act.wait_ge(*A.latest)
                        f(CSQ[:, i % 2, :], dst, ACT.Square).then_inc(*A.inc("c_sq"))
                if 1 <= i < 17:
                    head_rstd(i - 1, 4, CRS[:, (i - 1) % 2, :], "c_sc", "c_nm", "c_rs")
            steps = STEPS["C"]
            b = BASE["C"]
            for i in range(len(steps) + PIPE + 1):
                if i < len(steps):
                    w = (steps[i][1] + 1) * P
                    act.wait_ge(sems["sc_mm"], b + i + 1)
                    if i >= 2:
                        act.wait_ge(sems["c_nl"], i - 1)
                    f(CL[:, i % 2, 0:w], PB[4 + i % 4][:, 0:w], ACT.Abs).then_inc(*A.inc())
                    act.wait_ge(*A.latest)
                    f(CL[:, i % 2, 0:w], CL[:, i % 2, 0:w], ACT.Exp, scale=-1.0).then_inc(*A.inc())
                    act.wait_ge(*A.latest)
                    f(CL[:, i % 2, 0:w], CL[:, i % 2, 0:w], ACT.Ln, bias=sc("one")).then_inc(*A.inc("c_l"))
                if 1 <= i <= len(steps):
                    j = i - 1
                    w = (steps[j][1] + 1) * P
                    act.wait_ge(sems["c_la"], j + 1)
                    if j >= 2:
                        act.wait_ge(sems["tr_mm"], b + j - 1)
                    f(CPR[:, j % 2, 0:w], CN[:, j % 2, 0:w], ACT.Exp).then_inc(*A.inc("c_prob"))
                if 3 <= i < len(steps) + 3:
                    tr_evac("C", i - 3, steps[i - 3][1] + 1)
                j = i - PIPE - 1
                if j >= 0:
                    h, t = steps[j]
                    act.wait_ge(sems["pv_mm"], b + j + 1)
                    f(HN[:, h, tile(t)], PB[2 + j % 2][:, 0:P], ACT.Copy).then_inc(*A.inc("o_ev"))
            act.wait_ge(*A.latest)
            round_x("oc")
            for k in range(KT):
                act.wait_ge(sems["norm_h"], RES[N_FFN1] + k + 1)
                f(SQ[:, k, :], H[:, k, :], ACT.Square).then_inc(*A.inc("norm_sq"))
            rstd(N_FFN1, "eps2")
            round_x("mlp2", N_FFN1)
            end_stage()
            mlp(2, None, None)

        @block.vector
        def _(dve):
            D = Count(sems, "dve_step")
            ends = [0]

            def end_stage():
                ends[0] += 1
                dve.drain().then_inc(sems["stage"], 1)
                dve.wait_ge(sems["stage"], 3 * ends[0])

            def tt(out, a, b, op):
                return dve.tensor_tensor(out, a, b, op)

            def stt(out, a, scalar, b, op0, op1):
                return dve.scalar_tensor_tensor(out, a, scalar, b, op0, op1)

            def ts(out, a, s1, s2, op0, op1=None):
                if op1 is None:
                    return dve.tensor_scalar(out, a, s1, None, op0)
                return dve.tensor_scalar(out, a, s1, s2, op0, op1)

            def add_squares(n, k, w=S):
                dve.wait_ge(sems["norm_sq"], n * KT + k + 1)
                if k:
                    dve.wait_ge(*D.latest)
                    tt(ACC[:, 0:w], SQ[:, 0, 0:w] if k == 1 else ACC[:, 0:w], SQ[:, k, 0:w], ALU.add)\
                        .then_inc(*D.inc("norm_acc" if k == KT - 1 else None))

            def rest(x, k):
                dve.wait_ge(sems["x_hi"], SPLIT_NO[x] * KT + k + 1)
                tt(x_lo(x, k), x_full(x, k), x_hi(x, k).bitcast(F32), ALU.subtract).then_inc(*D.inc("x_lo"))

            def scale_out(n, src, w, width=S, x=None):
                dve.wait_ge(sems["norm_rs"], n + 1)
                for k in range(KT + 1):
                    if k < KT:
                        stt(x_full(x, k) if x else src(k), src(k), vec(w, k, k + 1), RS[:, 0:width], ALU.mult, ALU.mult)\
                            .then_inc(*D.inc("norm_out"))
                    if k and x:
                        rest(x, k - 1)

            def residual(n, unit, bank, per=1):
                for k in range(KT):
                    dve.wait_ge(sems["w_used"], UNIT[unit] + per * (k + 1))
                    tt(H[:, k, :], H[:, k, :], PB[bank(k)][:, :], ALU.add).then_inc(*D.inc("norm_h"))
                    if k:
                        add_squares(n, k - 1)
                add_squares(n, KT - 1)

            def rd(out, in_, op, negate=False):
                return dve.tensor_reduce(out, in_, AX.X, op, negate=negate)

            def mlp(n):
                for half in range(2):
                    done = 32 * n + 16 * half
                    with dve.Fori(0, 4) as i:
                        for j in range(4):
                            dve.wait_ge(sems["hid_hi"], i * 4 + (done + j + 1))
                            lo, hi = (a[:, bass.ds(i * 4 + j, 1), :].rearrange("p a n -> p (a n)") for a in (MAL, MAH))
                            tt(lo, RL[:, j % 2, :], hi.bitcast(F32), ALU.subtract).then_inc(sems["mlp_a"], 1)
                    if half == 0:
                        for k in range(KT):
                            dve.wait_ge(sems["w_used"], UNIT[f"down{n}a"] + 2 * (k + 1))
                            tt(H[:, k, :], H[:, k, :], PB[6 + k % 2][:, :], ALU.add).then_inc(*D.inc("half_h"))
                dve.wait_ge(sems["half_h"], KT * (n + 1))

            dve.memset(PX[:, :, 0:1], 0.0).then_inc(*D.inc())
            dve.wait_ge(sems["v_in"], 16)
            dve.wait_ge(sems["c_in"], 16)
            tt(LAMP, vec("lam", 0, 2), vec("lam", 2, 4), ALU.mult).then_inc(*D.inc("lam_in"))
            ts(SUBW, vec("subln"), 0.8, None, ALU.mult).then_inc(*D.inc())
            ts(KA1, vec("k_a"), -1.0, 1.0, ALU.mult, ALU.add).then_inc(*D.inc())
            for k in range(KT):
                add_squares(N_MIX, k)
            dve.wait_ge(sems["x_in"], 16)
            scale_out(N_MIX, lambda k: H[:, k, :], "norm_mix", x="mix")
            dve.wait_ge(sems["lam_exp"], 1)
            tt(NLAM, LAME[:, 1:2], LAME[:, 0:1], ALU.subtract).then_inc(*D.inc())
            dve.wait_ge(*D.latest)
            ts(NLAM, NLAM, 0.2, None, ALU.subtract).then_inc(*D.inc())

            def shift(m, name=None):
                dve.wait_ge(sems["ev_act"], m + 1)
                cur = PX[:, m, 1:PW]
                tt(TMP[:, m % 2, :], PX[:, m, 0:S], cur, ALU.subtract).then_inc(*D.inc())
                dve.wait_ge(*D.latest)
                stt(cur, TMP[:, m % 2, :], vec("mu", m, m + 1), cur, ALU.mult, ALU.add).then_inc(*D.inc(name))
            shift(LORA, "lora_in")
            shift(GD, "lora_in")
            for p in range(4):
                shift(K0 + p)
            dve.wait_ge(*D.latest)
            for p in range(4):
                ts(KK[:, p, :], PX[:, K0 + p, 1:PW], vec("k_k", p, p + 1), None, ALU.mult).then_inc(*D.inc())
            dve.wait_ge(*D.latest)
            for p in range(4):
                tt(CS[:, p, :], KK[:, p, :], KK[:, p, :], ALU.mult).then_inc(*D.inc("kk_sq"))
            for m in range(R0, 14):
                shift(m)
            for p in range(4):
                dve.wait_ge(sems["prep_act"], 4 + p + 1)
                ts(TMP[:, p % 2, :], AG[:, p, :], vec("k_a", p, p + 1), KA1[:, p:p + 1], ALU.mult, ALU.add).then_inc(*D.inc())
                dve.wait_ge(*D.latest)
                tt(PX[:, K0 + p, 1:PW], PX[:, K0 + p, 1:PW], TMP[:, p % 2, :], ALU.mult).then_inc(*D.inc())
                dve.wait_ge(*D.latest)
                stt(BON[:, p, :], PX[:, R0 + p, 1:PW], vec("r_k", p, p + 1), PX[:, K0 + p, 1:PW], ALU.mult, ALU.mult)\
                    .then_inc(*D.inc("bonus_in"))
            for p in range(4):
                dve.wait_ge(sems["prep_mm"], 12 + p + 1)
                ts(CS[:, p, :], PB[4 + p][:, :], 1e-24, KK_SCALE, ALU.max, ALU.mult).then_inc(*D.inc("kkln_in"))
            for p in range(4):
                dve.wait_ge(sems["kk_rs"], p + 1)
                tt(KK[:, p, :], KK[:, p, :], CS[:, p, :], ALU.mult).then_inc(*D.inc())
                dve.wait_ge(*D.latest)
                tt(AG[:, p, :], AG[:, p, :], KK[:, p, :], ALU.mult).then_inc(*D.inc())
            for p in range(4):
                dve.tensor_tensor_scan(CS[:, p, :], cst("reset64"), SIG[:, p, :], 0.0, ALU.mult, ALU.add).then_inc(*D.inc())
                dve.wait_ge(*D.latest)
                tt(SIG[:, p, :], CS[:, p, :], SIG[:, p, :], ALU.subtract).then_inc(*D.inc("cs_ready"))
            for p in range(4):
                dve.wait_ge(sems["prep_mm"], 16 + p + 1)
                tt(BON[:, p, :], PB[4 + p][:, :], PX[:, V0 + p, 1:PW], ALU.mult).then_inc(*D.inc("prep_dve"))
            for p in range(4):
                dve.wait_ge(sems["exp_ready"], 3 * p + 3)
                tt(KK[:, p, :], KK[:, p, :], SIG[:, p, :], ALU.mult).then_inc(*D.inc())
                tt(AG[:, p, :], AG[:, p, :], TMP[:, p % 2, :], ALU.mult).then_inc(*D.inc())
                tt(PX[:, K0 + p, 1:PW], PX[:, K0 + p, 1:PW], TMP[:, p % 2, :], ALU.mult).then_inc(*D.inc("exp_used"))
                tt(PX[:, R0 + p, 1:PW], PX[:, R0 + p, 1:PW], CS[:, p, :], ALU.mult).then_inc(*D.inc())
            dve.tensor_copy(ECH, CS[:, :, 63::64]).then_inc(*D.inc())
            dve.wait_ge(*D.latest)

            steps = STEPS["diff"]
            for i in range(len(steps) + PIPE + 2):
                if i < len(steps):
                    w = (steps[i][1] + 1) * P
                    dve.wait_ge(sems["sc_mm"], i + 1)
                    banks = [PB[4 + 2 * (i % 2)], PB[5 + 2 * (i % 2)]]
                    for pb in banks:
                        tt(pb[:, w - 64:w], pb[:, w - 64:w], cst("chunk_bias"), ALU.add).then_inc(*D.inc())
                    dve.wait_ge(*D.latest)
                    for m, pb in enumerate(banks):
                        rd(nmax(i, m), pb[:, 0:w], ALU.max, negate=True).then_inc(*D.inc("sc_max" if m else None))
                j = i - 1
                if 0 <= j < len(steps):
                    w = (steps[j][1] + 1) * P
                    dve.wait_ge(sems["sc_exp"], 2 * (j + 1))
                    dve.reciprocal(recip(j, 0, 2), psum_of(j, 0, 2)).then_inc(*D.inc())
                    dve.wait_ge(*D.latest)
                    tt(recip(j, 1), recip(j, 1), NLAM, ALU.mult).then_inc(*D.inc())
                    dve.wait_ge(*D.latest)
                    ts(PR2[:, j % 2, 0:w], PR2[:, j % 2, 0:w], recip(j, 1), None, ALU.mult).then_inc(*D.inc())
                    dve.wait_ge(*D.latest)
                    stt(PR1[:, j % 2, 0:w], PR1[:, j % 2, 0:w], recip(j, 0), PR2[:, j % 2, 0:w], ALU.mult, ALU.add)\
                        .then_inc(*D.inc("prob"))
                j = i - PIPE - 1
                if 0 <= j < len(steps) and steps[j][1] == TT - 1:
                    h = steps[j][0]
                    dve.wait_ge(sems["on_rs"], h + 1)
                    stt(HN[:, 4 + h, :], PB[2 + h % 2][:, :], SUBW, OLN, ALU.mult, ALU.mult).then_inc(*D.inc("on_out"))
            end_stage()

            for g in GS:
                dve.memset(g, 0.0).then_inc(*D.inc())
            dve.wait_ge(*D.latest)

            def two(bank):
                return PB[bank][:, :].rearrange("p (a n) -> p a n", n=256)

            def four(bank):
                return PB[bank][:, :].rearrange("p (a n) -> p a n", n=P)

            def heads4(x, q):
                return x[:, q::2, :]
            masks = cst("bd_strict", 0, 256).unsqueeze(1).to_broadcast([P, 2, 256])
            pairm = cst("low_mask", 0, 128).unsqueeze(1).to_broadcast([P, 4, P])
            pairt = cst("gla_mask", 0, 128).unsqueeze(1).to_broadcast([P, 4, P])
            eye = cst("ident").unsqueeze(1).to_broadcast([P, 4, P])
            for t in range(TT):
                ech = ECH[:, :, 2 * t:2 * t + 2].unsqueeze(3).to_broadcast([P, 4, 2, 64])
                for src, dst in ((AG[:, :, tile(t)], BP), (PX[:, K0:K0 + 4, 1 + t * P:1 + (t + 1) * P], KP)):
                    tt(dst.rearrange("p a (c n) -> p a c n", n=64), src.rearrange("p a (c n) -> p a c n", n=64), ech, ALU.mult)\
                        .then_inc(*D.inc("ch_in"))
                for n in range(8):
                    dve.wait_ge(sems["ch_aq"], 10 * t + n + 1)
                    h = 4 * (n % 4 // 2) + n % 2
                    dst = AQ if n < 4 else BQ
                    tt(dst[:, h:h + 3:2, :], two(n % 4), masks, ALU.mult).then_inc(*D.inc("ch_aqev"))
                for q in range(2):
                    dve.wait_ge(sems["ch_aq"], 10 * t + 8 + q + 1)
                    tt(heads4(TI, q), four(q), pairm, ALU.mult).then_inc(*D.inc("ch_aqev"))
                dve.wait_ge(*D.latest)
                for q in range(2):
                    tt(heads4(TI, q), eye, heads4(TI, q), ALU.subtract).then_inc(*D.inc("ch_t0ev"))
                for q in range(2):
                    tt(heads4(UI, q), AQ[:, q::2, 0:P], pairt, ALU.mult).then_inc(*D.inc())
                dve.wait_ge(*D.latest)
                for q in range(2):
                    tt(heads4(UI, q), eye, heads4(UI, q), ALU.subtract).then_inc(*D.inc("ch_t0ev"))
                for l in range(5):
                    m = cst("low_mask", (l + 1) * P, (l + 2) * P).unsqueeze(1).to_broadcast([P, 4, P])
                    for q in range(2):
                        dve.wait_ge(sems["lv_x"], 10 * t + 2 * l + q + 1)
                        tt(heads4(XI, q), four(q), m, ALU.mult).then_inc(*D.inc("lv_xev"))
                    for q in range(2):
                        dve.wait_ge(sems["lv_y"], 20 * t + 4 * l + 2 * q + 1)
                        tt(heads4(TI, q), heads4(TI, q), four(2 + q), ALU.subtract).then_inc(*D.inc("lv_yev"))
                        dve.wait_ge(sems["lv_y"], 20 * t + 4 * l + 2 * q + 2)
                        tt(heads4(UI, q), heads4(UI, q), four(4 + q), ALU.subtract).then_inc(*D.inc("lv_yev"))
                for c in (2 * t, 2 * t + 1):
                    r = slice(64 * (c % 2), 64 * (c % 2) + 64)
                    g, g1 = GS[c % 3], GS[(c + 1) % 3]
                    tt(TG, g, ECH[:, :, c:c + 1].to_broadcast([P, 4, P]), ALU.mult).then_inc(*D.inc())
                    dve.wait_ge(sems["sa_mm"], c + 1)
                    tt(SA[r], W1[r], four(0)[r], ALU.subtract).then_inc(*D.inc("sa_ev"))
                    dve.wait_ge(sems["gu_mm"], c + 1)
                    tt(g1[0:64, :, 0:64], TG[0:64, :, 0:64], four(1)[0:64, :, 0:64], ALU.add).then_inc(*D.inc())
                    tt(g1[64:128, :, 64:128], TG[64:128, :, 64:128], four(1)[64:128, :, 64:128], ALU.add)\
                        .then_inc(*D.inc("g_ev"))
                    dve.wait_ge(*D.latest)
                end_stage()

            for p in range(4):
                dve.wait_ge(sems["gn_mm"], p + 1)
                stt(HN[:, p, :], PB[p][:, :], -1.0 / 64, HN[:, p, :], ALU.mult, ALU.add).then_inc(*D.inc("gn_c"))
            for p in range(4):
                dve.wait_ge(sems["gn_rs"], p + 1)
                stt(HN[:, p, :], HN[:, p, :], vec("lnx_w", p, p + 1), SIG[:, p, :], ALU.mult, ALU.mult).then_inc(*D.inc())
                dve.wait_ge(*D.latest)
                stt(HN[:, p, :], HN[:, p, :], vec("lnx_b", p, p + 1), BON[:, p, :], ALU.add, ALU.add).then_inc(*D.inc())
                dve.wait_ge(*D.latest)
                tt(HN[:, p, :], HN[:, p, :], GT[:, p, :], ALU.mult).then_inc(*D.inc("mix_out"))
            end_stage()

            for k in range(KT):
                rest("out", k)
            for k in range(KT):
                add_squares(N_SRC, k, MEM)
            dve.wait_ge(sems["mem_in"], 16)
            scale_out(N_SRC, lambda k: MT[:, k, :], "norm_src", MEM, x="src")
            residual(N_MEM, "out", lambda k: k % 4)
            scale_out(N_MEM, lambda k: H[:, k, :], "norm_mem", x="mem")
            steps = STEPS["mem"]
            for i in range(len(steps) + 1):
                if i < len(steps):
                    dve.wait_ge(sems["sc_mm"], BASE["mem"] + i + 1)
                    rd(nmax(i), PB[4 + i % 2][:, 0:MEM], ALU.max, negate=True).then_inc(*D.inc("sc_max"))
                if i:
                    j = i - 1
                    dve.wait_ge(sems["sc_exp"], EXPB["mem"] + j + 1)
                    dve.reciprocal(recip(j), psum_of(j)).then_inc(*D.inc())
                    dve.wait_ge(*D.latest)
                    ts(MPR[:, j % 2, 0:MEM], MPR[:, j % 2, 0:MEM], recip(j), None, ALU.mult).then_inc(*D.inc("prob"))
            for k in range(KT):
                rest("mo", k)
            residual(N_MLP, "mem_o", lambda k: k % 4)
            scale_out(N_MLP, lambda k: H[:, k, :], "norm_mlp", x="mlp0")
            end_stage()
            mlp(0)
            residual(N_FINAL, "down0b", lambda k: 6 + k % 2, 2)
            scale_out(N_FINAL, lambda k: H[:, k, :], "norm_final")

            for k in range(KT):
                add_squares(N_MIX0, k)
            scale_out(N_MIX0, lambda k: H[:, k, :], "g_mix0", x="ab")
            ts(GQS, vec("gq_a"), P ** -0.5, None, ALU.mult).then_inc(*D.inc())
            ts(GCS, vec("gq_c"), P ** -0.5, None, ALU.mult).then_inc(*D.inc())
            end_stage()

            def rope(j):
                kind = "i" if j < 5 else "a"
                x = rope_plane(j)
                dve.wait_ge(sems["rope_mm"], j + 1)
                tt(T1, PB[3][:, :], cst("sin_" + kind), ALU.mult).then_inc(*D.inc())
                tt(x, x, cst("cos_" + kind), ALU.mult).then_inc(*D.inc())
                dve.wait_ge(*D.latest)
                tt(x, x, T1, ALU.add).then_inc(*D.inc("rope_ev"))
            for j in range(5):
                rope(j)
                if j == 4:
                    dve.wait_ge(sems["iw_tr"], 1)
                    ts(IW, PB[2][:, :].rearrange("p (t n) -> p t n", n=P)[:, :, 32:40], 8 ** -0.5, None, ALU.mult, None)\
                        .then_inc(*D.inc("iw_ev"))
            for p in range(2):
                dve.wait_ge(sems["gate_mm"], p + 1)
                ts(GE[0][:, p, :], PB[4 + p][:, :], vec("b_gate", p, p + 1), None, ALU.add).then_inc(*D.inc("gate_in"))
            dve.wait_ge(sems["gate_ln"], 1)
            stt(GB, GE[0], 0.0, GE[1], ALU.min, ALU.subtract).then_inc(*D.inc())
            dve.wait_ge(*D.latest)
            for p in range(2):
                dve.tensor_tensor_scan(GE[0][:, p, :], cst("reset128"), GB[:, p, :], 0.0, ALU.mult, ALU.add).then_inc(*D.inc())
            dve.wait_ge(*D.latest)
            dve.tensor_copy(GB, GE[0]).then_inc(*D.inc("gb_ready"))

            def a_scale(j):
                x = rope_plane(5 + j)
                dve.wait_ge(sems["a_rs"], j + 1)
                stt(x, x, GQS if j < 4 else vec("gk_a"), RA[:, j % 2, :], ALU.mult, ALU.mult).then_inc(*D.inc("a_sc"))

            for j in range(9):
                if j < 8:
                    for n in range(3 * j, 3 * j + 3):
                        t, h = INDEX_STEPS[n]
                        w = (t + 1) * P
                        dve.wait_ge(sems["idx_r"], n + 1)
                        if h == 0:
                            ts(SCORE[:, t, 0:w], RLU[:, n % 2, 0:w], IW[:, t, h:h + 1], None, ALU.mult, None)\
                                .then_inc(*D.inc("idx_acc"))
                        else:
                            dve.wait_ge(*D.latest)
                            stt(SCORE[:, t, 0:w], RLU[:, n % 2, 0:w], IW[:, t, h:h + 1], SCORE[:, t, 0:w], ALU.mult, ALU.add)\
                                .then_inc(*D.inc("idx_acc"))
                if j:
                    a_scale(j - 1)
            dve.wait_ge(*D.latest)
            for t in range(1, TT):
                w = (t + 1) * P
                tt(SCORE[:, t, w - 64:w], SCORE[:, t, w - 64:w], cst("chunk_bias"), ALU.add).then_inc(*D.inc())

            def topk(t):
                w = (t + 1) * P
                s = SCORE[:, t, 0:w]
                for n in range(16):
                    src = s if n == 0 else WORK[:, 0:w]
                    dve.max(TOP, src).then_inc(*D.inc())
                    dve.wait_ge(*D.latest)
                    if n < 15:
                        dve.match_replace(WORK[:, 0:w], TOP, src, -3.0e38).then_inc(*D.inc())
                        dve.wait_ge(*D.latest)
                thr = TOP[:, 7:8]
                ts(EQ[:, 0:w], s, thr, None, ALU.is_equal).then_inc(*D.inc())
                ts(s, s, thr, None, ALU.is_gt).then_inc(*D.inc())
                dve.wait_ge(*D.latest)
                dve.tensor_reduce(NGT, s, AX.X, ALU.add).then_inc(*D.inc())
                dve.tensor_tensor_scan(PRE[:, 0:w], cst("ones", 0, 1).to_broadcast([P, w]), EQ[:, 0:w], 0.0, ALU.mult, ALU.add)\
                    .then_inc(*D.inc())
                dve.wait_ge(*D.latest)
                ts(NGT, NGT, -1.0, 128.0, ALU.mult, ALU.add).then_inc(*D.inc())
                dve.wait_ge(*D.latest)
                stt(EQ[:, 0:w], PRE[:, 0:w], NGT, EQ[:, 0:w], ALU.is_le, ALU.mult).then_inc(*D.inc())
                dve.wait_ge(*D.latest)
                tt(s, s, EQ[:, 0:w], ALU.add).then_inc(*D.inc())
                dve.wait_ge(*D.latest)
                ts(s, s, -1.0, -NEG, ALU.add, ALU.mult).then_inc(*D.inc())
                dve.wait_ge(*D.latest)

            def rel(l, dst):
                s = LEVELS[l]
                g = GB.rearrange("p a (g n) -> p (a g) n", n=2 * s)
                tt(dst.rearrange("p a (g n) -> p (a g) n", n=2 * s), g, g[:, :, s - 1:s].to_broadcast([P, 1024 // (2 * s), 2 * s]),
                   ALU.subtract).then_inc(*D.inc("lv_d"))
            rel(1, GE[1])
            for l in range(8):
                mask = cst("gla_mask", 7 * P, 8 * P) if l == 0 else cst("gla_mask", (l - 1) * P, l * P)
                mask = mask.unsqueeze(1).to_broadcast([P, 4, P])
                if 1 <= l < 7:
                    dve.wait_ge(sems["lv_in"], 2 * l)
                    rel(l + 1, GE[(l + 1) % 2])
                for n in range(4):
                    dve.wait_ge(sems["lvl_mm"], 4 * l + n + 1)
                    if n >= 2:
                        dve.wait_ge(*D.latest)
                    dst = (ATT[:, n, :] if l == 0 else LV[:, n % 2, :]).rearrange("p (a n) -> p a n", n=P)
                    tt(dst, PB[4 + n][:, :].rearrange("p (a n) -> p a n", n=P), mask, ALU.mult).then_inc(*D.inc("lvl_ev"))
                    if l and n:
                        dve.wait_ge(sems["lvl_ev"], 4 * l + n)
                        tt(ATT[:, n - 1, :], ATT[:, n - 1, :], LV[:, (n - 1) % 2, :], ALU.add).then_inc(*D.inc("att"))
                if l:
                    dve.wait_ge(sems["lvl_ev"], 4 * l + 4)
                    tt(ATT[:, 3, :], ATT[:, 3, :], LV[:, 1, :], ALU.add).then_inc(*D.inc("att"))
                if l < 7:
                    dve.wait_ge(sems["lv_e"], l + 1)
                    tt(GQE, GQ, GE[(l + 1) % 2], ALU.mult).then_inc(*D.inc("lv_in"))
                    tt(GKE, GK, GE[(l + 1) % 2], ALU.mult).then_inc(*D.inc("lv_in"))
                if 1 <= l:
                    rope(4 + l)
            dve.wait_ge(sems["idx_mm"], 24)
            b3 = GB.rearrange("p a (t n) -> p (a t) n", n=P)
            tt(GED.rearrange("p a (t n) -> p (a t) n", n=P), b3[:, :, P - 1:P].to_broadcast([P, 8, P]), b3, ALU.subtract)\
                .then_inc(*D.inc("g_ed"))
            rope(12)
            dve.wait_ge(sems["lvl_mm"], 32)
            dve.wait_ge(sems["g_ede"], 1)
            tt(GKE, GK, GED, ALU.mult).then_inc(*D.inc("ke_in"))
            tt(GQE, GQ, GEB, ALU.mult).then_inc(*D.inc("ke_in"))
            topk(1)
            for t in range(3):
                dve.wait_ge(sems["kv2_mm"], max(t + 1, 2))
                bank, o = (2, 256 * t) if t < 2 else (3, 0)
                dve.wait_ge(sems["g_eb"], 1)
                if t == 0:
                    dve.tensor_copy(GSH[:, 1, :], PB[bank][:, o:o + 256]).then_inc(*D.inc("sh_ev"))
                else:
                    dve.wait_ge(*D.latest)
                    for p in range(2):
                        e = t * P + P - 1
                        stt(GSH[:, t + 1, p * P:(p + 1) * P], GSH[:, t, p * P:(p + 1) * P], GEB[:, p, e:e + 1], PB[bank][:, o + p * P:o + (p + 1) * P], ALU.mult, ALU.add)\
                            .then_inc(*D.inc("sh_ev" if p else None))
            for h in range(4):
                dve.wait_ge(sems["go_rs"], h + 1)
                stt(HN[:, 4 + h, :], PB[4 + h][:, :], vec("g_gla"), GSQ[:, h, :], ALU.mult, ALU.mult).then_inc(*D.inc("go_ev"))
            dve.wait_ge(*D.latest)
            for h in range(4):
                tt(HN[:, 4 + h, :], HN[:, 4 + h, :], OG[:, h, :], ALU.mult).then_inc(*D.inc("gla_out"))

            steps = STEPS["A"]
            for i in range(len(steps) + 1):
                if i < len(steps):
                    h, t = steps[i]
                    w = (t + 1) * P
                    if h == 0 and t >= 2:
                        topk(t)
                    dve.wait_ge(sems["sc_mm"], BASE["A"] + i + 1)
                    pb = PB[4 + i % 2]
                    if t == 0:
                        tt(pb[:, 64:P], pb[:, 64:P], cst("chunk_bias"), ALU.add).then_inc(*D.inc())
                    else:
                        tt(pb[:, 0:w], pb[:, 0:w], SCORE[:, t, 0:w], ALU.add).then_inc(*D.inc())
                    dve.wait_ge(*D.latest)
                    rd(nmax(i), pb[:, 0:w], ALU.max, negate=True).then_inc(*D.inc("sc_max"))
                if i:
                    j = i - 1
                    w = (steps[j][1] + 1) * P
                    dve.wait_ge(sems["sc_exp"], EXPB["A"] + j + 1)
                    dve.reciprocal(recip(j), psum_of(j)).then_inc(*D.inc())
                    dve.wait_ge(*D.latest)
                    ts(APR[:, j % 2, 0:w], APR[:, j % 2, 0:w], recip(j), None, ALU.mult).then_inc(*D.inc("prob"))
            for k in range(KT):
                rest("oab", k)
            residual(N_FFN0, "out_ab", lambda k: k % 4)
            scale_out(N_FFN0, lambda k: H[:, k, :], "g_ffn0", x="mlp1")
            end_stage()
            mlp(1)
            residual(N_MIX1, "down1b", lambda k: 6 + k % 2, 2)
            scale_out(N_MIX1, lambda k: H[:, k, :], "g_mix1", x="c")
            end_stage()

            for j in range(16):
                x = CQ[:, j, :] if j < 8 else CK[:, j - 8, :]
                dve.wait_ge(sems["c_rs"], j + 1)
                stt(x, x, GCS if j < 8 else vec("gk_c"), CRS[:, j % 2, :], ALU.mult, ALU.mult).then_inc(*D.inc("c_sc"))
            steps = STEPS["C"]
            for i in range(len(steps)):
                t = steps[i][1]
                w = (t + 1) * P
                z = PB[4 + i % 4]
                nl, rc, la = CL[:, i % 2, 0:w], CR[:, i % 2, 0:w], CN[:, i % 2, 0:w]
                dve.wait_ge(sems["c_l"], i + 1)
                if i >= 2:
                    dve.wait_ge(sems["c_prob"], i - 1)
                stt(la, z[:, 0:w], 0.0, nl, ALU.max, ALU.add).then_inc(*D.inc("c_nl"))
                dve.wait_ge(*D.latest)
                tt(la[:, w - P:w], la[:, w - P:w], cst("strict"), ALU.mult).then_inc(*D.inc())
                dve.wait_ge(*D.latest)
                dve.tensor_tensor_scan(rc[:, ::-1], cst("ones", 0, 1).to_broadcast([P, w]), la[:, ::-1], 0.0, ALU.mult, ALU.add)\
                    .then_inc(*D.inc())
                dve.wait_ge(*D.latest)
                tt(la, z[:, 0:w], rc, ALU.subtract).then_inc(*D.inc())
                dve.wait_ge(*D.latest)
                tt(la[:, w - P:w], la[:, w - P:w], cst("strict_bias"), ALU.add).then_inc(*D.inc("c_la"))
            for k in range(KT):
                rest("oc", k)
            residual(N_FFN1, "out_c", lambda k: k % 4)
            scale_out(N_FFN1, lambda k: H[:, k, :], "g_ffn1", x="mlp2")
            end_stage()
            mlp(2)
            for k in range(KT):
                dve.wait_ge(sems["w_used"], UNIT["down2b"] + 2 * (k + 1))
                tt(H[:, k, :], H[:, k, :], PB[6 + k % 2][:, :], ALU.add).then_inc(*D.inc("norm_h"))

        @block.tensor
        def _(pe):
            T = Count(sems, None)
            ends = [0]
            unit = [0]
            free = [None] * 8

            def end_stage():
                ends[0] += 1
                pe.drain().then_inc(sems["stage"], 1)
                pe.wait_ge(sems["stage"], 3 * ends[0])
                for b in range(8):
                    free[b] = None

            def take(b):
                if free[b] is not None:
                    pe.wait_ge(sems[free[b][0]], free[b][1])
                    free[b] = None

            def mm(out, lhsT, rhs, start=True, stop=True, **k):
                return pe.matmul(out, lhsT, rhs, start=start, stop=stop, **k)

            def tr(out, in_):
                return pe.transpose(out, in_, cst("ident"))

            def weights(u, j):
                pe.wait_ge(sems["w_split"], u + 1)
                return (w[:, j % 2, :].rearrange("p (k n) -> p k n", n=P) for w in (WH, WL))

            def product(out, lhs, rhs, start, stop):
                pe.matmul(out, lhs[0], rhs[0], start=start, stop=False)
                pe.matmul(out, lhs[0], rhs[1], start=False, stop=False)
                return pe.matmul(out, lhs[1], rhs[0], start=False, stop=stop)

            def project(n, bank0, ev, x, first=True, width=S, banks=4, evbase=0):
                for m in range(n):
                    u = unit[0]
                    b = (bank0 + m) % banks
                    take(b)
                    wh, wl = weights(u, u)
                    for k in range(KT):
                        if m == 0 and first:
                            pe.wait_ge(sems["x_lo"], SPLIT_NO[x] * KT + k + 1)
                        ins = product(PB[b][:, 0:width], (wh[:, k, :], wl[:, k, :]), (x_hi(x, k), x_lo(x, k)), k == 0, k == KT - 1)
                    ins.then_inc(*T.inc("w_used"))
                    unit[0] += 1
                    free[b] = (ev, evbase + m + 1)

            def project_tok(n, bank0, ev, x, tiles=TT, evbase=0, banks=4):
                for m in range(n):
                    u = unit[0]
                    b = (bank0 + m) % banks
                    take(b)
                    wh, wl = weights(u, u)
                    for t in range(tiles):
                        for k in range(KT):
                            ins = product(PB[b][:, tile(t)], (x_hi(x, k)[:, tile(t)], x_lo(x, k)[:, tile(t)]),
                                          (wh[:, k, :], wl[:, k, :]), k == 0, k == KT - 1)
                    ins.then_inc(*T.inc("w_used"))
                    unit[0] += 1
                    free[b] = (ev, evbase + m + 1)

            def norm_sum(n, width=S):
                pe.wait_ge(sems["norm_acc"], n + 1)
                mm(PB[4][:, 0:width], cst("ones"), ACC[:, 0:width]).then_inc(*T.inc("norm_ms"))
                free[4] = ("norm_rs", n + 1)

            pe.wait_ge(sems["c_in"], 16)
            pe.wait_ge(sems["lam_in"], 1)
            mm(PB[7][:, 0:2], cst("ones"), LAMP).then_inc(*T.inc("lam_mm"))
            free[7] = ("lam_exp", 1)
            norm_sum(N_MIX)

            def prep(n, lhsT, rhs, w=S):
                b = 4 + n % 4
                take(b)
                mm(PB[b][:, :], lhsT, rhs).then_inc(*T.inc("prep_mm"))
                free[b] = ("prep_act", n + 1) if n < 12 else ("kkln_in", n - 11) if n < 16 else ("prep_dve", n - 15)
            project(14, 0, "ev_act", "mix")
            pe.wait_ge(sems["sig_ready"], 1)
            for p in range(4):
                prep(p, vec("dec_aaa_up", p * P, (p + 1) * P)[0:64], PX[0:64, LORA, 1:PW])
            for p in range(4):
                prep(4 + p, vec("dec_aaa_up", p * P, (p + 1) * P)[64:128], PX[64:128, LORA, 1:PW])
            for p in range(4):
                prep(8 + p, vec("g_up", p * P, (p + 1) * P), PX[:, GD, 1:PW])
            project(4, 14, "ev_act", "mix", first=False, evbase=14)
            for p in range(4):
                pe.wait_ge(sems["kk_sq"], p + 1)
                prep(12 + p, cst("bd_ones"), CS[:, p, :])
            project(4, 18, "ev_act", "mix", first=False, evbase=18)
            for p in range(4):
                pe.wait_ge(sems["bonus_in"], p + 1)
                prep(16 + p, cst("bd_ones"), BON[:, p, :])
            project_tok(4, 22, "ev_act", "mix", evbase=22)

            steps = STEPS["diff"]
            for i in range(len(steps) + PIPE + 1):
                j = i - PIPE - 1
                if 0 <= j < len(steps) and steps[j][1] == TT - 1:
                    h = steps[j][0]
                    pe.wait_ge(sems["on_sq"], h + 1)
                    take(1)
                    mm(PB[1][:, :], cst("ones"), OSQ).then_inc(*T.inc("on_mm"))
                    free[1] = ("on_rs", h + 1)
                if i < len(steps):
                    h, t = steps[i]
                    w = (t + 1) * P
                    if i == 0:
                        pe.wait_ge(sems["ev_act"], 26)
                    for m in range(2):
                        b = 4 + 2 * (i % 2) + m
                        take(b)
                        r = slice(64 * m, 64 * m + 64)
                        last = mm(PB[b][:, 0:w], DQ[r, h, tile(t)], DK[r, h, 0:w])
                        if m:
                            last.then_inc(*T.inc("sc_mm"))
                        free[b] = ("sc_exp", 2 * (i + 1))
                if 2 <= i < len(steps) + 2:
                    j = i - 2
                    pe.wait_ge(sems["prob"], j + 1)
                    take(0)
                    for k in range(steps[j][1] + 1):
                        last = tr(PB[0][:, tile(k)], PR1[:, j % 2, tile(k)])
                        if k == steps[j][1]:
                            last.then_inc(*T.inc("tr_mm"))
                    free[0] = ("tr_ev", j + 1)
                j = i - PIPE
                if 0 <= j < len(steps):
                    h, t = steps[j]
                    pe.wait_ge(sems["tr_ev"], j + 1)
                    b = 2 + h % 2
                    if t == 0:
                        take(b)
                    for k in range(t + 1):
                        last = mm(PB[b][:, tile(t)], DV[:, h, tile(k)], PT[:, j % 2, tile(k)], start=k == 0, stop=k == t)
                        if k == t:
                            last.then_inc(*T.inc("pv_mm"))
                    if t == TT - 1:
                        free[b] = ("on_out", h + 1)
            end_stage()

            def bank4(b, p):
                return PB[b][:, p * P:(p + 1) * P]
            alpha, beta = (lambda p, t: KK[:, p, tile(t)]), (lambda p, t: AG[:, p, tile(t)])

            def px(m, t, lo=0, n=P):
                return PX[:, m, 1 + t * P + lo:1 + t * P + lo + n]
            for t in range(TT):
                for n, src in enumerate((alpha, lambda p, t: px(V0 + p, t), lambda p, t: BP[:, p, :], lambda p, t: KP[:, p, :])):
                    if n >= 2:
                        pe.wait_ge(sems["ch_in"], 2 * t + n - 1)
                    for p in range(4):
                        last = tr(bank4(4 + n, p), src(p, t))
                        if p == 3:
                            last.then_inc(*T.inc("ch_tr"))
                for n in range(8):
                    if n >= 4:
                        pe.wait_ge(sems["ch_aqev"], 10 * t + n - 3)
                    for e in range(2):
                        h = 4 * (n % 4 // 2) + n % 2 + 2 * e
                        p, r = h // 2, slice(64 * (h % 2), 64 * (h % 2) + 64)
                        lhsT = (beta(p, t) if n < 4 else px(K0 + p, t))[r]
                        o = 256 * e
                        mm(PB[n % 4][:, o:o + P], lhsT, alpha(p, t)[r])
                        last = mm(PB[n % 4][:, o + P:o + 256], lhsT, px(R0 + p, t)[r])
                        if e:
                            last.then_inc(*T.inc("ch_aq"))
                for q in range(2):
                    pe.wait_ge(sems["ch_aqev"], 10 * t + 5 + q)
                    for e in range(4):
                        r = slice(64 * q, 64 * q + 64)
                        last = mm(bank4(q, e), alpha(e, t)[r], beta(e, t)[r])
                        if e == 3:
                            last.then_inc(*T.inc("ch_aq"))
                for l in range(5):
                    for q in range(2):
                        if l == 0:
                            pe.wait_ge(sems["ch_t0ev"], 4 * t + 4)
                        else:
                            pe.wait_ge(sems["lv_yev"], 20 * t + 4 * (l - 1) + 2 * q + 2)
                        for e in range(4):
                            h = 2 * e + q
                            last = mm(bank4(q, e), AQ[:, h, 0:P], TI[:, h, :])
                            if e == 3:
                                last.then_inc(*T.inc("lv_x"))
                    for q in range(2):
                        pe.wait_ge(sems["lv_xev"], 10 * t + 2 * l + q + 1)
                        for e in range(4):
                            h = 2 * e + q
                            last = mm(bank4(2 + q, e), UI[:, h, :], XI[:, h, :])
                            if e == 3:
                                last.then_inc(*T.inc("lv_y"))
                        if l == 0 and q == 0:
                            pe.wait_ge(sems["ch_trev"], 4 * t + 4)
                        for e in range(4):
                            h = 2 * e + q
                            last = mm(bank4(4 + q, e), XI[:, h, :], UI[:, h, :])
                            if e == 3:
                                last.then_inc(*T.inc("lv_y"))
                pe.wait_ge(sems["lv_yev"], 20 * t + 20)
                for h in range(8):
                    last = mm(PB[4][:, h * 64:h * 64 + 64], BQ[:, h, 0:P], TOKV[:, h // 2, 64 * (h % 2):64 * (h % 2) + 64])
                    if h == 7:
                        last.then_inc(*T.inc("w1_mm"))
                for h in range(8):
                    r = slice(64 * (h % 2), 64 * (h % 2) + 64)
                    last = mm(PB[5][r, tile(h // 2)], TOKA[:, h // 2, r], UI[:, h, :])
                    if h == 7:
                        last.then_inc(*T.inc("w1_mm"))
                pe.wait_ge(sems["w1_ev"], 3 * t + 1)
                for h in range(8):
                    last = mm(PB[6][:, h * 64:h * 64 + 64], UI[:, h, :], P1[:, h // 2, 64 * (h % 2):64 * (h % 2) + 64])
                    if h == 7:
                        last.then_inc(*T.inc("w1_mm"))
                pe.wait_ge(sems["w1_ev"], 3 * t + 3)
                for c in (2 * t, 2 * t + 1):
                    r = slice(64 * (c % 2), 64 * (c % 2) + 64)
                    if c:
                        pe.wait_ge(sems["g_ev"], c)
                    for p in range(4):
                        last = mm(PB[0][r, tile(p)], TA[:, p, r], GS[c % 3][:, p, :])
                        if p == 3:
                            last.then_inc(*T.inc("sa_mm"))
                    for p in range(4):
                        mm(PB[1][:, tile(p)], TOKK[r, p, :], TOKV[r, p, :], start=p == 0, stop=False, skip_group_check=True)
                    pe.wait_ge(sems["sa_ev"], c + 1)
                    for p in range(4):
                        last = mm(PB[1][:, tile(p)], TOKB[r, p, :], SA[r, p, :], start=False, stop=True, skip_group_check=True)
                        if p == 3:
                            last.then_inc(*T.inc("gu_mm"))
                for p in range(4):
                    for q in range(2):
                        r = slice(64 * q, 64 * q + 64)
                        mm(PB[7][r, tile(p)], SA[:, p, r], AQ[:, 2 * p + q, P:2 * P], start=True, stop=False, skip_group_check=True)
                        mm(PB[7][r, tile(p)], TOKV[:, p, r], BQ[:, 2 * p + q, P:2 * P], start=False, stop=False, skip_group_check=True)
                    for e in range(2):
                        o = p * P + 64 * e
                        last = mm(PB[7][:, o:o + 64], GS[(2 * t + e) % 3][:, p, :], px(R0 + p, t, 64 * e, 64), start=False, stop=e == 1, skip_group_check=True)
                        if p == 3 and e == 1:
                            last.then_inc(*T.inc("y_mm"))
                end_stage()
            for p in range(4):
                mm(PB[p][:, :], cst("bd_ones"), HN[:, p, :]).then_inc(*T.inc("gn_mm"))
            for p in range(4):
                pe.wait_ge(sems["gn_sq"], p + 1)
                mm(PB[4 + p][:, :], cst("bd_ones"), SIG[:, p, :]).then_inc(*T.inc("gn_mm"))
            end_stage()

            project(4, 0, "norm_h", "out", evbase=RES[N_MEM])
            norm_sum(N_SRC, MEM)
            project(4, 4, "norm_h", "out", first=False, evbase=RES[N_MEM] + 4)
            take(4)
            norm_sum(N_MEM)
            evb = 26
            project(8, 0, "ev_act", "src", width=MEM, evbase=evb)
            project_tok(8, 0, "ev_act", "src", tiles=2, evbase=evb + 8)
            project(8, 0, "ev_act", "mem", evbase=evb + 16)
            steps = STEPS["mem"]
            b0 = BASE["mem"]
            pe.wait_ge(sems["ev_act"], evb + 24)
            for i in range(len(steps) + PIPE):
                if i < len(steps):
                    h, t = steps[i]
                    b = 4 + i % 2
                    take(b)
                    for j in range(2):
                        last = mm(PB[b][:, 0:MEM], MQ[:, 2 * h + j, tile(t)], MK[:, 2 * h + j, :], start=j == 0, stop=j == 1)
                        if j:
                            last.then_inc(*T.inc("sc_mm"))
                    free[b] = ("sc_exp", EXPB["mem"] + i + 1)
                if 2 <= i < len(steps) + 2:
                    j = i - 2
                    pe.wait_ge(sems["prob"], b0 + j + 1)
                    take(0)
                    for k in range(2):
                        last = tr(PB[0][:, tile(k)], MPR[:, j % 2, tile(k)])
                        if k:
                            last.then_inc(*T.inc("tr_mm"))
                    free[0] = ("tr_ev", b0 + j + 1)
                j = i - PIPE
                if j >= 0:
                    h, t = steps[j]
                    pe.wait_ge(sems["tr_ev"], b0 + j + 1)
                    b = 2 + j % 2
                    take(b)
                    for d in range(2):
                        for k in range(2):
                            last = mm(PB[b][:, tile(d)], MV[:, k, h * MEM + d * P:h * MEM + (d + 1) * P], MPT[:, j % 2, tile(k)], start=k == 0, stop=k == 1)
                            if d and k:
                                last.then_inc(*T.inc("pv_mm"))
                    free[b] = ("o_ev", j + 1)
            pe.wait_ge(sems["o_ev"], 16)
            take(0)
            project(8, 0, "norm_h", "mo", evbase=RES[N_MLP])
            take(4)
            norm_sum(N_MLP)
            end_stage()

            def mlp(n, nxt):
                x = f"mlp{n}"
                for half in range(2):
                    done = 32 * n + 16 * half
                    up, down = UNIT[f"up{n}{'ab'[half]}"], UNIT[f"down{n}{'ab'[half]}"]

                    def up_unit(i, j):
                        wh, wl = weights(i * 4 + (up + j), j)
                        if done or not isinstance(i, int):
                            pe.wait_ge(sems["relu"], i * 4 + (done + j - 3))
                        for k in range(KT):
                            if half == 0 and isinstance(i, int) and j == 0:
                                pe.wait_ge(sems["x_lo"], SPLIT_NO[x] * KT + k + 1)
                            ins = product(PB[j][:, :], (wh[:, k, :], wl[:, k, :]), (x_hi(x, k), x_lo(x, k)), k == 0, k == KT - 1)
                        ins.then_inc(sems["w_used"], 1)
                    for j in range(4):
                        up_unit(0, j)
                    with pe.Fori(1, 4) as i:
                        for j in range(4):
                            up_unit(i, j)

                    def down_unit(i, m, g):
                        wh, wl = weights(i * 4 + (down + 2 * m + g), g)
                        if g == 0 and not isinstance(i, int):
                            if half == 0:
                                pe.wait_ge(sems["half_h"], i * 2 + (KT * n + m - 1))
                            else:
                                pe.wait_ge(sems["norm_h"], i * 2 + (RES[nxt] + m - 1))
                        elif g == 0 and half:
                            pe.wait_ge(sems["half_h"], KT * n + KT - 1 + m)
                        if isinstance(i, int) and m == 0:
                            pe.wait_ge(sems["mlp_a"], done + 8 * (g + 1))
                        for k in range(KT):
                            h = g * KT + k
                            ins = product(PB[6 + m][:, :], (wh[:, k, :], wl[:, k, :]), (MAH[:, h, :], MAL[:, h, :]), h == 0, h == 15)
                        ins.then_inc(sems["w_used"], 1)
                    for m in range(2):
                        for g in range(2):
                            down_unit(0, m, g)
                    with pe.Fori(1, 4) as i:
                        for m in range(2):
                            for g in range(2):
                                down_unit(i, m, g)
                unit[0] += 64
                if nxt is not None:
                    norm_sum(nxt)
            mlp(0, N_FINAL)

            norm_sum(N_MIX0)
            end_stage()

            def rope_mm(j):
                if j < 5:
                    pe.wait_ge(sems["ev_act"], EV2 + j + 1)
                else:
                    pe.wait_ge(sems["a_sc"], j - 4)
                take(3)
                mm(PB[3][:, :], cst("rope_i" if j < 5 else "rope_a"), rope_plane(j)).then_inc(*T.inc("rope_mm"))
                free[3] = ("rope_ev", j + 1)
            for i in range(30):
                kind = project_tok if 18 <= i < 26 else None
                if kind:
                    project_tok(1, i, "ev_act", "ab", evbase=EV2 + i, banks=2)
                else:
                    project(1, i, "ev_act", "ab", evbase=EV2 + i, banks=2, first=i == 0)
                if 2 <= i < 7:
                    rope_mm(i - 2)
                if i == 7:
                    pe.wait_ge(sems["ev_act"], EV2 + 6)
                    for t in range(TT):
                        last = tr(PB[2][:, tile(t)], MISC[:, tile(t)])
                        if t == TT - 1:
                            last.then_inc(*T.inc("iw_tr"))
                    free[2] = ("iw_ev", 1)
                    for p in range(2):
                        take(4 + p)
                        mm(PB[4 + p][:, :], vec("gate_up", p * P, (p + 1) * P)[0:16], MISC[0:16, :]).then_inc(*T.inc("gate_mm"))
                        free[4 + p] = ("gate_in", p + 1)
                if 10 <= i < 18:
                    for n in range(3 * (i - 10), 3 * (i - 10) + 3):
                        t, h = INDEX_STEPS[n]
                        if n == 0:
                            pe.wait_ge(sems["rope_ev"], 5)
                        b = 6 + n % 2
                        r = slice(64 * (h % 2), 64 * (h % 2) + 64)
                        take(b)
                        mm(PB[b][:, 0:(t + 1) * P], IQ[r, h // 2, tile(t)], IK[r, 0:(t + 1) * P]).then_inc(*T.inc("idx_mm"))
                        free[b] = ("idx_r", n + 1)
                if 11 <= i < 19:
                    j = i - 11
                    pe.wait_ge(sems["a_sq"], j + 1)
                    take(2)
                    mm(PB[2][:, :], cst("ones"), SQA[:, j % 2, :]).then_inc(*T.inc("a_mm"))
                    free[2] = ("a_rs", j + 1)
                if 18 <= i < 26:
                    l = i - 18
                    if l:
                        pe.wait_ge(sems["lv_in"], 2 * l)
                    for n in range(4):
                        q, th = n // 2, n % 2
                        r = slice(64 * q, 64 * q + 64)
                        take(4 + n)
                        for e in range(4):
                            t, p = 2 * th + e // 2, e % 2
                            k_, q_ = (GK, GQ) if l == 0 else (GKE, GQE)
                            last = mm(PB[4 + n][:, tile(e)], k_[r, p, tile(t)], q_[r, p, tile(t)])
                            if e == 3:
                                last.then_inc(*T.inc("lvl_mm"))
                        free[4 + n] = ("lvl_ev", 4 * l + n + 1)
                if 19 <= i < 27:
                    rope_mm(5 + i - 19)

            pe.wait_ge(sems["ke_in"], 2)
            for n in range(2):
                take(n)
                for e in range(4):
                    t, p = 2 * n + e // 2, e % 2
                    last = tr(PB[n][:, tile(e)], GKE[:, p, tile(t)])
                    if e == 3:
                        last.then_inc(*T.inc("ke_tr"))
                free[n] = ("ke_ev", n + 1)
            pe.wait_ge(sems["ev_act"], EV2 + 30)
            for t in range(3):
                if t == 0 or t == 2:
                    take(2 + t // 2)
                pe.wait_ge(sems["ke_ev"], t // 2 + 1)
                for h in range(4):
                    r = slice(64 * (h % 2), 64 * (h % 2) + 64)
                    o = (256 * t if t < 2 else 0) + P * (h // 2)
                    last = mm(PB[2 + t // 2][r, o:o + P], GKT[:, t, h * 64:h * 64 + 64], GV[:, h, tile(t)])
                    if h == 3:
                        last.then_inc(*T.inc("kv2_mm"))
            pe.wait_ge(sems["att"], 28)
            for h in range(4):
                take(4 + h)
                for t in range(TT):
                    th, e = t // 2, 2 * (t % 2) + h // 2
                    mm(PB[4 + h][:, tile(t)], GV[:, h, tile(t)], ATT[:, 2 * (h % 2) + th, tile(e)], start=t == 0, stop=t == 0, skip_group_check=True)
            pe.wait_ge(sems["sh_ev"], 3)
            for h in range(4):
                r = slice(64 * (h % 2), 64 * (h % 2) + 64)
                for t in range(1, TT):
                    last = mm(PB[4 + h][:, tile(t)], GSH[r, t, P * (h // 2):P * (h // 2) + P], GQE[r, h // 2, tile(t)], start=False, stop=True, skip_group_check=True)
                    if t == 3:
                        last.then_inc(*T.inc("go_mm"))
                free[4 + h] = ("go_ev", h + 1)
            for h in range(4):
                pe.wait_ge(sems["go_sq"], h + 1)
                take(h)
                mm(PB[h][:, :], cst("ones"), GSQ[:, h, :]).then_inc(*T.inc("go_nm"))
                free[h] = ("go_rs", h + 1)

            pe.wait_ge(sems["rope_ev"], 13)
            steps = STEPS["A"]
            b0 = BASE["A"]
            for i in range(len(steps) + PIPE):
                if i < len(steps):
                    h, t = steps[i]
                    w = (t + 1) * P
                    b = 4 + i % 2
                    take(b)
                    mm(PB[b][:, 0:w], QA[:, h, tile(t)], KA[:, h, 0:w]).then_inc(*T.inc("sc_mm"))
                    free[b] = ("sc_exp", EXPB["A"] + i + 1)
                if 2 <= i < len(steps) + 2:
                    j = i - 2
                    pe.wait_ge(sems["prob"], b0 + j + 1)
                    take(0)
                    for k in range(steps[j][1] + 1):
                        last = tr(PB[0][:, tile(k)], APR[:, j % 2, tile(k)])
                        if k == steps[j][1]:
                            last.then_inc(*T.inc("tr_mm"))
                    free[0] = ("tr_ev", b0 + j + 1)
                j = i - PIPE
                if j >= 0:
                    h, t = steps[j]
                    pe.wait_ge(sems["tr_ev"], b0 + j + 1)
                    b = 2 + j % 2
                    take(b)
                    for k in range(t + 1):
                        last = mm(PB[b][:, 0:P], VA[:, h, tile(k)], APT[:, j % 2, tile(k)], start=k == 0, stop=k == t)
                        if k == t:
                            last.then_inc(*T.inc("pv_mm"))
                    free[b] = ("o_ev", 16 + j + 1)
            pe.wait_ge(sems["o_ev"], 32)
            take(0)
            project(8, 0, "norm_h", "oab", evbase=RES[N_FFN0])
            take(4)
            norm_sum(N_FFN0)
            end_stage()
            mlp(1, N_MIX1)
            end_stage()

            for i in range(24):
                if i < 16:
                    project(1, i, "ev_act", "c", evbase=EV3 + i, first=i == 0)
                else:
                    project_tok(1, i, "ev_act", "c", evbase=EV3 + i)
                if 1 <= i < 17:
                    pe.wait_ge(sems["c_sq"], i)
                    take(4)
                    mm(PB[4][:, :], cst("ones"), CSQ[:, (i - 1) % 2, :]).then_inc(*T.inc("c_nm"))
                    free[4] = ("c_rs", i)
            pe.wait_ge(sems["c_sc"], 16)
            pe.wait_ge(sems["ev_act"], EV3 + 24)
            steps = STEPS["C"]
            b0 = BASE["C"]
            for i in range(len(steps) + PIPE + 1):
                if i < len(steps):
                    h, t = steps[i]
                    w = (t + 1) * P
                    b = 4 + i % 4
                    take(b)
                    mm(PB[b][:, 0:w], CQ[:, h, tile(t)], CK[:, h, 0:w]).then_inc(*T.inc("sc_mm"))
                    free[b] = ("c_la", i + 1)
                if 3 <= i < len(steps) + 3:
                    j = i - 3
                    pe.wait_ge(sems["c_prob"], j + 1)
                    take(0)
                    for k in range(steps[j][1] + 1):
                        last = tr(PB[0][:, tile(k)], CPR[:, j % 2, tile(k)])
                        if k == steps[j][1]:
                            last.then_inc(*T.inc("tr_mm"))
                    free[0] = ("tr_ev", b0 + j + 1)
                j = i - PIPE - 1
                if j >= 0:
                    h, t = steps[j]
                    pe.wait_ge(sems["tr_ev"], b0 + j + 1)
                    b = 2 + j % 2
                    take(b)
                    for k in range(t + 1):
                        last = mm(PB[b][:, 0:P], CV[:, h, tile(k)], CPT[:, j % 2, tile(k)], start=k == 0, stop=k == t)
                        if k == t:
                            last.then_inc(*T.inc("pv_mm"))
                    free[b] = ("o_ev", 32 + j + 1)
            pe.wait_ge(sems["o_ev"], 64)
            take(0)
            project(8, 0, "norm_h", "oc", evbase=RES[N_FFN1])
            take(4)
            norm_sum(N_FFN1)
            end_stage()
            mlp(2, None)


def planes(a):
    a = np.ascontiguousarray(np.asarray(a).T)
    return np.ascontiguousarray(a.reshape(a.shape[0] // P, P, a.shape[1]).transpose(1, 0, 2))


def units(w):
    k, n = w.shape
    a = w.reshape(k // (KT * P), KT, P, n // P, P).transpose(3, 0, 2, 1, 4)
    return a.reshape(-1, P, KT * P)


def stream(i):
    w_in, w_ab, w_c = i["w_in"][0], i["w_in_ab_2"][0], i["w_in_c_2"][0]
    r = 512
    ab = {}
    o = 0
    for name, n in (("qa", 512), ("ka", 512), ("va", 512), ("iq", 512), ("ik", 64), ("iw", 8),
                    ("qb", 256), ("kb", 256), ("vb", 512), ("g", 16), ("og", 512)):
        ab[name] = w_ab[:, o:o + n]
        o += n
    misc = np.zeros((w_ab.shape[0], P), w_ab.dtype)
    misc[:, 0:16], misc[:, 32:40] = ab["g"], ab["iw"]
    parts = {
        "rwkv_lora": w_in[:, 3 * r:3 * r + 256], "rwkv_k": w_in[:, r:2 * r], "rwkv_r": w_in[:, 0:r],
        "rwkv_v": w_in[:, 2 * r:3 * r], "diff_q": w_in[:, 1792:1792 + r], "diff_k": w_in[:, 1792 + r:1792 + 2 * r],
        "diff_v": w_in[:, 1792 + 2 * r:1792 + 3 * r], "out": i["w_out"][0], "mem_k": i["w_mk"][0], "mem_v": i["w_mv"][0],
        "mem_q": i["w_mq"][0], "mem_o": i["w_mo"][0],
        "a_q": ab["qa"], "a_k": ab["ka"], "a_v": ab["va"], "i_q": ab["iq"],
        "i_k": np.concatenate([ab["ik"], ab["ik"]], 1), "misc": misc, "b_q": ab["qb"], "b_k": ab["kb"],
        "b_v": ab["vb"], "b_og": ab["og"], "out_ab": i["w_out_ab_2"][0],
        "c_q": w_c[:, 0:1024], "c_k": w_c[:, 1024:2048], "c_v": w_c[:, 2048:3072], "out_c": i["w_out_c_2"][0]}
    for n, (up, down) in enumerate(((i["w_up"][0], i["w_down"][0]), (i["w_up_2"][0], i["w_down_2"][0]),
                                    (i["w_up_2"][1], i["w_down_2"][1]))):
        f = up.shape[1] // 2
        for half in range(2):
            parts[f"up{n}{'ab'[half]}"] = up[:, half * f:(half + 1) * f]
            parts[f"down{n}{'ab'[half]}"] = down[half * f:(half + 1) * f]
    out = np.zeros((STREAM_UNITS, P, KT * P), np.float32)
    for name, n in STREAM:
        out[UNIT[name]:UNIT[name] + n] = units(parts[name])
    return out


def vectors(i):
    v = np.zeros((P, N_VEC), np.float32)

    def put(name, a):
        o, n = VO[name]
        v[:, o:o + n] = a.reshape(n, P).T
    put("norm_mix", i["norm_mix_w"][0])
    put("norm_mem", i["norm_mem_w"][0])
    put("norm_src", i["norm_src_w"][0])
    put("norm_mlp", i["norm_mlp_w"][0])
    put("norm_final", i["norm_final_w"])
    for l in range(2):
        put(f"g_mix{l}", i["g_mix_2"][l])
        put(f"g_ffn{l}", i["g_ffn_2"][l])
    mu = i["mu_shift"][0]
    put("mu", np.concatenate([mu[1536:1792], mu[512:1024], mu[0:512], mu[1024:1536]]))
    for name, key in (("w0", "w_decay0"), ("a0", "a0"), ("k_k", "k_k"), ("k_a", "k_a"), ("r_k", "r_k"),
                      ("lnx_w", "lnx_w"), ("lnx_b", "lnx_b"), ("subln", "subln_w"), ("gq_a", "gq_a_2"), ("gk_a", "gk_a_2"),
                      ("gq_c", "gq_c_2"), ("gk_c", "gk_c_2"), ("g_gla", "g_gla_2"), ("b_gate", "b_gate_2")):
        put(name, i[key][0].reshape(-1))
    o = VO["lam"][0]
    for n, key in enumerate(("lam_q1", "lam_q2", "lam_k1", "lam_k2")):
        v[0:64, o + n] = i[key][0]
    o = VO["dec_aaa_up"][0]
    v[0:64, o:o + 512] = i["w_decay_up"][0]
    v[64:128, o:o + 512] = i["a_up"][0]
    o = VO["g_up"][0]
    v[:, o:o + 512] = i["g_up"][0]
    o = VO["gate_up"][0]
    v[0:16, o:o + 256] = i["w_gate_up_2"][0]
    return v


def kernel(**inputs):
    from concourse import bacc
    from concourse.bass_utils import run_bass_kernel_spmd
    i = {k: np.asarray(v) for k, v in inputs.items()}
    nc = bacc.Bacc("TRN2", target_bir_lowering=False, num_devices=1, dynamic_dma_scratch_size=1024)
    arrays = {"x_in": planes(i["x"][0]), "mem_in": planes(i["mem"][0]), "weights_in": stream(i),
              "constants_in": constants(), "vectors_in": vectors(i)}
    aps = [nc.dram_tensor(n, a.shape, F32, kind="ExternalInput").ap() for n, a in arrays.items()]
    out = nc.dram_tensor("h_out", (P, KT, S), F32, kind="ExternalOutput").ap()
    build(nc, *aps, out)
    r = run_bass_kernel_spmd(nc, [arrays], core_ids=[0])
    h = r.results[0]["h_out"]
    return np.ascontiguousarray(h.transpose(2, 1, 0).reshape(1, S, KT * P))
```

```python
from contextlib import ExitStack
import math
import numpy as np
import concourse.bass as bass
from concourse import mybir

F32 = mybir.dt.float32
F32R = mybir.dt.float32r
ACT = mybir.ActivationFunctionType
ALU = mybir.AluOpType
AX = mybir.AxisListType

P = 128
S = 512
KT = 8
TT = S // P
MEM = 256
RING = 4
BODY = 8
DEC = math.exp(-0.5)
NEG = -1.0e30

STREAM = [("rwkv_lora", 2), ("rwkv_k", 4), ("rwkv_r", 4), ("rwkv_v", 4),
          ("diff_q", 4), ("diff_k", 4), ("diff_v", 4), ("out", 8),
          ("mem_k", 8), ("mem_v", 8), ("mem_q", 8), ("mem_o", 8),
          ("up0a", 16), ("down0a", 16), ("up0b", 16), ("down0b", 16),
          ("i_q", 4), ("i_k", 1), ("misc", 1), ("b_q", 2), ("b_k", 2),
          ("a_q", 4), ("a_k", 4), ("a_v", 4), ("b_v", 4), ("b_og", 4), ("out_ab", 8),
          ("up1a", 16), ("down1a", 16), ("up1b", 16), ("down1b", 16),
          ("c_in", 24), ("out_c", 8),
          ("up2a", 16), ("down2a", 16), ("up2b", 16), ("down2b", 16)]
UNIT = {}
UNITS = 0
for _name, _n in STREAM:
    UNIT[_name] = UNITS
    UNITS += _n
STREAM_UNITS = -(-UNITS // BODY) * BODY

CONSTS = [("ident", 128), ("ones", 128), ("bd_ones", 128), ("rope_a", 128), ("rope_i", 128),
          ("cos_a", 512), ("sin_a", 512), ("cos_i", 512), ("sin_i", 512),
          ("reset64", 512), ("reset128", 512),
          ("bd_strict", 128), ("bd_incl", 128), ("low_mask", 6 * 128), ("gla_mask", 8 * 128),
          ("chunk_bias", 64), ("strict", 128), ("strict_bias", 128), ("scalars", 8)]
CO = {}
N_CONST = 0
for _name, _n in CONSTS:
    CO[_name] = (N_CONST, _n)
    N_CONST += _n

VECS = [("norm_mix", 8), ("norm_mem", 8), ("norm_src", 8), ("norm_mlp", 8), ("norm_final", 8),
        ("g_mix0", 8), ("g_ffn0", 8), ("g_mix1", 8), ("g_ffn1", 8),
        ("mu", 14), ("w0", 4), ("a0", 4), ("k_k", 4), ("k_a", 4), ("r_k", 4), ("lnx_w", 4), ("lnx_b", 4),
        ("lam", 4), ("subln", 1), ("gq_a", 1), ("gk_a", 1), ("gq_c", 1), ("gk_c", 1), ("g_gla", 1),
        ("b_gate", 2), ("dec_aaa_up", 512), ("g_up", 512), ("gate_up", 256)]
VO = {}
N_VEC = 0
for _name, _n in VECS:
    VO[_name] = (N_VEC, _n)
    N_VEC += _n

RMS_EPS, EPS2, GN_EPS = 1e-5, 1e-6, 64e-5
SC = {"eps1": 0, "eps2": 1, "gn": 2, "kkb": 3, "one": 4}
KK_SCALE = 65536.0


def constants():
    c = np.zeros((P, N_CONST), np.float32)

    def put(name, a):
        o, n = CO[name]
        c[:, o:o + n] = a.reshape(P, n)
    i = np.arange(P)
    row, col = i[:, None], i[None, :]
    put("ident", np.eye(P))
    put("ones", np.ones((P, P)))
    put("bd_ones", (row // 64 == col // 64) * 1.0)
    t = np.arange(S)

    def rope(name, head, width):
        rot = width // 4
        half = rot // 2
        inv = np.power(500000.0, -np.arange(half, dtype=np.float32) * 2.0 / rot).astype(np.float32)
        ang = t.astype(np.float32)[None, :] * inv[:, None]
        cos, sin, m = np.ones((P, S)), np.zeros((P, S)), np.zeros((P, P))
        for base in range(0, P, width):
            for j in range(half):
                cos[base + j] = cos[base + half + j] = np.cos(ang[j])
                sin[base + j] = sin[base + half + j] = np.sin(ang[j])
                m[base + half + j, base + j] = -1.0
                m[base + j, base + half + j] = 1.0
        put("cos_" + name, cos)
        put("sin_" + name, sin)
        put("rope_" + name, m)
    rope("a", 0, 128)
    rope("i", 0, 64)
    put("reset64", np.broadcast_to((t % 64 != 0) * 1.0, (P, S)))
    put("reset128", np.broadcast_to((t % 128 != 0) * 1.0, (P, S)))
    same = row // 64 == col // 64
    put("bd_strict", (same & (row < col)) * 1.0)
    put("bd_incl", (same & (row <= col)) * 1.0)
    low = [((row // (2 * s) == col // (2 * s)) & (row % (2 * s) >= s) & (col % (2 * s) < s)) * 1.0
           for s in (1, 2, 4, 8, 16, 32)]
    put("low_mask", np.concatenate(low, 1))
    gla = [((row // (2 * s) == col // (2 * s)) & (col % (2 * s) >= s) & (row % (2 * s) < s)) * 1.0
           for s in (1, 2, 4, 8, 16, 32, 64)] + [(row == col) * 1.0]
    put("gla_mask", np.concatenate(gla, 1))
    put("chunk_bias", np.broadcast_to(np.where(row < 64, NEG, 0.0), (P, 64)))
    put("strict", (col < row) * 1.0)
    put("strict_bias", np.where(col < row, 0.0, NEG))
    s = np.zeros((P, 8))
    s[:, SC["eps1"]], s[:, SC["eps2"]], s[:, SC["gn"]] = RMS_EPS, EPS2, GN_EPS
    s[:, SC["kkb"]] = 0.5 * math.log(KK_SCALE)
    s[:, SC["one"]] = 1.0
    put("scalars", s)
    return c


class Count:

    def __init__(self, sems, own):
        self.sems, self.own, self.n, self.latest = sems, own, {}, None

    def inc(self, name=None):
        name = name or self.own
        self.n[name] = self.n.get(name, 0) + 1
        self.latest = (self.sems[name], self.n[name])
        return self.sems[name], 1


def build(nc, x_d, mem_d, w_d, c_d, v_d, out_d, stop=None):
    ctx = ExitStack()
    with ctx:
        def sb(name, shape):
            return ctx.enter_context(nc.sbuf_tensor(name, shape, F32))

        PART = 16

        def sb_both(name, shape):
            offset = nc.sbuf_base
            t = sb(name, shape)
            return t, [nc.alloc_sbuf_tensor_at(f"{name}_r{a}", [P, min(PART, shape[1] - a), S], F32R, offset=offset + a * S * 4)
                       for a in range(0, shape[1], PART)]
        H = sb("H", [P, KT, S])
        HN, (HNR,) = sb_both("HN", [P, KT, S])
        W = sb("W", [P, RING, KT * P])
        WH = ctx.enter_context(nc.sbuf_tensor("WH", [P, 2, KT * P], F32R))
        WL = ctx.enter_context(nc.sbuf_tensor("WL", [P, 2, KT * P], F32R))
        NA = 61
        AR, AR_PARTS = sb_both("AR", [P, NA, S])
        C = sb("C", [P, N_CONST])
        V = sb("V", [P, N_VEC])
        SM = sb("SM", [P, 192])
        PB = [ctx.enter_context(nc.psum_tensor(f"PB{i}", [P, S], F32)) for i in range(8)]

        names = ["w_used", "w_round", "w_split", "x_hi", "x_lo", "vt_ev", "vt_tr", "hid_sq", "hid_hi", "half_h", "act_step", "dve_step", "pool_step", "stage", "x_in", "mem_in", "c_in", "v_in", "stored",
                 "norm_h", "norm_sq", "norm_acc", "norm_ms", "norm_rs", "norm_out",
                 "ev_act", "ev_dve", "lora_in", "kk_sq", "bonus_in", "prep_mm", "prep_act", "prep_dve",
                 "sig_ready", "a_ready", "kkln_in", "kk_rs", "cs_ready", "exp_ready", "exp_used", "lam_in", "lam_mm", "lam_exp",
                 "sc_mm", "sc_max", "sc_exp", "prob", "tr_mm", "tr_ev", "pv_mm", "o_ev",
                 "on_sq", "on_mm", "on_rs", "on_out",
                 "ch_in", "ch_tr", "ch_trev", "ch_aq", "ch_aqev", "ch_t0", "ch_t0ev", "lv_x", "lv_xev", "lv_y", "lv_yev",
                 "w1_mm", "w1_ev", "kv_mm", "g_ev", "sa_mm", "sa_ev", "gu_mm", "y_mm", "y_ev",
                 "gn_in", "gn_mm", "gn_c", "gn_sq", "gn_rs", "mix_out",
                 "relu", "mlp_a",
                 "rope_mm", "rope_ev", "iw_tr", "iw_ev", "gate_mm", "gate_in", "gate_ln", "gb_ready", "idx_mm", "idx_r", "idx_acc",
                 "a_sq", "a_mm", "a_rs", "a_sc", "lv_d", "lv_e", "lv_in", "lvl_mm", "lvl_ev", "att",
                 "g_eb", "g_ed", "gla_out", "g_ede", "ke_in", "ke_tr", "ke_ev", "kv2_mm", "sh_ev", "go_mm", "go_sq", "go_nm", "go_ln", "go_rs", "go_ev",
                 "c_sq", "c_nm", "c_rs", "c_sc", "c_rln", "c_abs", "c_exp", "c_l", "c_nl", "c_la", "c_prob"]
        sems = {n: ctx.enter_context(nc.semaphore(n)) for n in names}
        slot_loaded = [ctx.enter_context(nc.semaphore(f"slot_loaded{i}")) for i in range(RING)]

        def cst(name, a=0, b=None):
            o, n = CO[name]
            return C[:, o + a:o + (n if b is None else b)]

        def vec(name, a=0, b=None):
            o, n = VO[name]
            return V[:, o + a:o + (n if b is None else b)]

        def sc(name):
            return cst("scalars", SC[name], SC[name] + 1)

        flat = AR[:, :, :].rearrange("p a n -> p (a n)")
        PW = S + 1
        PX = flat[:, 0:14 * PW].rearrange("p (m n) -> p m n", n=PW)
        LORA, GD, K0, R0, V0 = 0, 1, 2, 6, 10
        SIG, CS, AG, KK, BON, GT = (AR[:, a:a + 4, :] for a in (15, 19, 23, 27, 31, 35))
        TMP = AR[:, 39:41, :]
        DQ, DK, DV = (AR[:, a:a + 4, :] for a in (41, 45, 49))
        SQ, ACC, LN, RS = AR[:, 48:56, :], AR[:, 56, :], AR[:, 57, :], AR[:, 58, :]
        PR1, PR2, PT, OSQ, OLN = AR[:, 53:55, :], AR[:, 55:57, :], AR[:, 57:59, :], AR[:, 59, :], AR[:, 60, :]
        def arr(a, b):
            return AR_PARTS[a // PART][:, a % PART:a % PART + b - a, :]
        MAH, MAL, RL = arr(0, 16), arr(16, 32), AR[:, 59:61, :]

        STEPS = {"diff": [(h, t) for h in range(4) for t in range(TT)],
                 "mem": [(h, t) for h in range(4) for t in range(TT)],
                 "A": [(h, t) for t in range(TT) for h in range(4)],
                 "C": [(h, t) for h in range(8) for t in range(TT)]}
        MAPS = {"diff": 2, "mem": 1, "A": 1, "C": 0}
        BASE, EXPB, s0, e0 = {}, {}, 0, 0
        for a in STEPS:
            BASE[a], EXPB[a] = s0, e0
            s0 += len(STEPS[a])
            e0 += len(STEPS[a]) * MAPS[a]
        PIPE = 3
        N_MIX, N_SRC, N_MEM, N_MLP, N_FINAL, N_MIX0, N_FFN0, N_MIX1, N_FFN1 = range(9)
        RES = {N_MEM: 0, N_MLP: 8, N_FINAL: 16, N_FFN0: 24, N_MIX1: 32, N_FFN1: 40, None: 48}

        LAMP, LAME, NLAM, SUBW, KA1 = SM[:, 0:2], SM[:, 2:4], SM[:, 4:5], SM[:, 5:6], SM[:, 6:10]
        ECH = SM[:, 16:48].rearrange("p (a c) -> p a c", c=8)

        def nmax(i, m=0, n=1):
            return SM[:, 48 + 2 * (i % 4) + m:48 + 2 * (i % 4) + m + n]

        def psum_of(i, m=0, n=1):
            return SM[:, 56 + 2 * (i % 4) + m:56 + 2 * (i % 4) + m + n]

        def recip(i, m=0, n=1):
            return SM[:, 64 + 2 * (i % 4) + m:64 + 2 * (i % 4) + m + n]

        def tile(t):
            return slice(t * P, (t + 1) * P)

        def pk(a, n=1, w=None):
            return AR[:, a:a + n, :].rearrange("p a (h n) -> p (a h) n", n=w)
        AQ, BQ = pk(41, 4, 256), pk(45, 4, 256)
        TI, UI, XI = pk(49, 2, 128), pk(51, 2, 128), pk(53, 2, 128)
        TOKA, TOKB, TOKK, TOKV = (pk(a, 1, 128) for a in (55, 56, 57, 58))
        BP, KP = pk(59, 1, 128), pk(60, 1, 128)
        TA, W1, SA, P1 = pk(39, 1, 128), pk(40, 1, 128), pk(18, 1, 128), pk(14 + 7, 1, 128)
        GS = [pk(a, 1, 128) for a in (15, 16, 17)]
        TG = pk(19, 1, 128)

        mview = AR[:, 0:8, :].rearrange("p a (b m) -> p (a b) m", m=MEM)
        MT, MN = mview[:, 0:8, :], mview[:, 8:16, :]
        MK = AR[:, 8:12, :].rearrange("p a (b m) -> p (a b) m", m=MEM)
        MV = AR[:, 12:16, :].rearrange("p (t a) n -> p t (a n)", t=2)
        MNH = arr(36, 40).rearrange("p a (b m) -> p (a b) m", m=MEM)
        MNL = arr(4, 8).rearrange("p a (b m) -> p (a b) m", m=MEM)
        MQ, MO = AR[:, 16:24, :], AR[:, 24:32, :]
        MPR, MPT = AR[:, 32:34, :], AR[:, 34:36, :]


        SPLITS = {"mix": [53, 54, 55, 56, 57, 59, 60, 58], "out": range(24, 32), "src": None, "mem": range(24, 32),
                  "mo": range(16, 24), "mlp0": range(40, 48), "ab": [5, 30, 34, 56, 57, 59, 60, 58],
                  "oab": range(18, 26), "mlp1": range(40, 48), "c": range(48, 56), "oc": range(8, 16),
                  "mlp2": range(40, 48)}
        SPLIT_NO = {name: n for n, name in enumerate(SPLITS)}

        def x_full(x, k):
            return MN[:, k, :] if x == "src" else MO[:, k, :] if x == "mo" else CQ[:, k, :] if x == "oc" else HN[:, k, :]

        def x_hi(x, k):
            return MNH[:, k, :] if x == "src" else arr(SPLITS[x][k], SPLITS[x][k] + 1)[:, 0, :]

        def x_lo(x, k):
            plane = 24 + k if x == "mo" else k if x == "oc" else None
            return MNL[:, k, :] if x == "src" else HNR[:, k, :] if plane is None else arr(plane, plane + 1)[:, 0, :]

        IQ, IK, MISC = AR[:, 0:4, :], AR[:, 4, :], AR[:, 47, :]
        QA, KA, VA = AR[:, 6:10, :], AR[:, 10:14, :], AR[:, 14:18, :]
        GQ, GK, GV, OG = AR[:, 18:20, :], AR[:, 20:22, :], AR[:, 22:26, :], AR[:, 26:30, :]
        SCORE, RLU, T1 = AR[:, 30:34, :], AR[:, 35:37, :], AR[:, 37, :]
        WORK, EQ = AR[:, 35, :], AR[:, 36, :]
        SQA, RA, GB = AR[:, 38:40, :], AR[:, 40:42, :], AR[:, 42:44, :]
        GE = [AR[:, 44:46, :], AR[:, 46:48, :]]
        GQE, GKE, ATT = AR[:, 48:50, :], AR[:, 50:52, :], AR[:, 52:56, :]
        GEB, GED = AR[:, 0:2, :], AR[:, 2:4, :]
        GKT = AR[:, 38:40, :].rearrange("p a (t n) -> p (a t) n", n=256)
        GSH = AR[:, 40:42, :].rearrange("p a (t n) -> p (a t) n", n=256)
        GSQ = AR[:, 44:48, :]
        APR, APT = AR[:, 35:37, :], AR[:, 38:40, :]
        IW = SM[:, 80:112].rearrange("p (t h) -> p t h", h=8)
        TOP = SM[:, 112:120]
        NGT = SM[:, 120:121]
        GQS, GCS = SM[:, 121:122], SM[:, 122:123]
        VT = {"diff": 0, "mem": 4, "ab": 12, "c": 20}
        EV2 = 50
        EV3 = EV2 + 30
        LEVELS = [None, 1, 2, 4, 8, 16, 32, 64]
        LEVEL_AT = {11 + 2 * l: l for l in range(8)}
        INDEX_STEPS = [(t, h) for t in range(1, TT) for h in range(8)]

        def rope_plane(j):
            return IQ[:, j, :] if j < 4 else IK if j == 4 else QA[:, j - 5, :] if j < 9 else KA[:, j - 9, :]

        CQ, CK, CV = AR[:, 0:8, :], AR[:, 8:16, :], AR[:, 16:24, :]
        CL, CN, CPR = (AR[:, a:a + 4, :] for a in (24, 28, 32))
        CR, CSQ, CRS = (AR[:, a:a + 2, :] for a in (36, 38, 40))
        CPT = AR[:, 42:46, :]
        C_ROUNDS = range(-4, 19)
        def PT_of(name):
            return {"diff": PT, "mem": MPT, "A": APT}[name]

        block = ctx.enter_context(nc.Block())

        @block.sync
        def _(sp):
            sp.dma_start(C[:, :], c_d).then_inc(sems["c_in"], 16)
            for j in range(RING):
                sp.dma_start(W[:, j, :], w_d[j, :, :]).then_inc(slot_loaded[j], 16)
            with sp.Fori(1, STREAM_UNITS // RING) as i:
                for j in range(RING):
                    sp.wait_ge(sems["w_split"], i * RING + (j - RING + 1))
                    sp.dma_start(W[:, j, :], w_d[bass.ds(i * RING + j, 1), :, :].rearrange("a p n -> p (a n)"))\
                        .then_inc(slot_loaded[j], 16)
            for k in range(KT):
                sp.wait_ge(sems["norm_h"], RES[None] + k + 1)
                sp.dma_start(out_d[:, k, :], H[:, k, :]).then_inc(sems["stored"], 16)
            sp.wait_ge(sems["stored"], 16 * KT)

        @block.gpsimd
        def _(pool):
            def split_unit(i, j):
                pool.wait_ge(slot_loaded[j % RING], 16 * (BODY // RING * i + (j // RING + 1)))
                if not isinstance(i, int) or j >= 2:
                    pool.wait_ge(sems["w_used"], BODY * i + (j - 1))
                w = W[:, j % RING, :]
                pool.tensor_tensor(WH[:, j % 2, :], w, ones, ALU.mult).then_inc(sems["w_round"], 1)
                pool.wait_ge(sems["w_round"], BODY * i + (j + 1))
                pool.tensor_tensor(WL[:, j % 2, :], w, WH[:, j % 2, :].bitcast(F32), ALU.subtract)\
                    .then_inc(sems["w_split"], 1)
            ones = cst("ones", 0, 1).to_broadcast([P, KT * P])
            pool.wait_ge(sems["c_in"], 16)
            for j in range(BODY):
                split_unit(0, j)
            with pool.Fori(1, STREAM_UNITS // BODY) as i:
                for j in range(BODY):
                    split_unit(i, j)

        @block.scalar
        def _(act):
            A = Count(sems, "act_step")
            ends = [0]

            def end_stage():
                ends[0] += 1
                act.drain().then_inc(sems["stage"], 1)
                act.wait_ge(sems["stage"], 3 * ends[0])

            def f(out, in_, func, **k):
                return act.activation(out, in_, func, **k)

            def rstd(n, eps, w=S):
                act.wait_ge(sems["norm_ms"], n + 1)
                f(LN[:, 0:w], PB[4][:, 0:w], ACT.Ln, scale=1.0 / 1024, bias=sc(eps)).then_inc(*A.inc())
                act.wait_ge(*A.latest)
                f(RS[:, 0:w], LN[:, 0:w], ACT.Exp, scale=-0.5).then_inc(*A.inc("norm_rs"))

            def round_x(x, norm=None):
                for k in range(KT):
                    if norm is not None:
                        act.wait_ge(sems["norm_out"], norm * KT + k + 1)
                    f(x_hi(x, k), x_full(x, k), ACT.Copy).then_inc(*A.inc("x_hi"))

            def used(name, i):
                act.wait_ge(sems["w_used"], UNIT[name] + i + 1)

            act.preload_act_table_set("natural_log")
            act.dma_start(H[:, :, :], x_d).then_inc(sems["x_in"], 16)
            act.dma_start(V[:, :], v_d).then_inc(sems["v_in"], 16)
            act.wait_ge(sems["c_in"], 16)
            act.wait_ge(sems["v_in"], 16)
            act.wait_ge(sems["x_in"], 16)
            for k in range(KT):
                f(SQ[:, k, :], H[:, k, :], ACT.Square).then_inc(*A.inc("norm_sq"))
            rstd(N_MIX, "eps1")
            act.wait_ge(sems["lam_mm"], 1)
            f(LAME, PB[7][:, 0:2], ACT.Exp).then_inc(*A.inc("lam_exp"))
            round_x("mix", N_MIX)

            for m in range(14):
                used("rwkv_lora", m)
                f(PX[:, m, 1:PW], PB[m % 4][:, :], ACT.Copy).then_inc(*A.inc("ev_act"))
                if m == 5:
                    act.wait_ge(sems["lora_in"], 2)
                    f(PX[0:64, LORA, 1:PW], PX[0:64, LORA, 1:PW], ACT.Tanh).then_inc(*A.inc())
                    f(PX[:, GD, 1:PW], PX[:, GD, 1:PW], ACT.Sigmoid).then_inc(*A.inc("sig_ready"))
            for p in range(4):
                act.wait_ge(sems["prep_mm"], p + 1)
                f(SIG[:, p, :], PB[4 + p][:, :], ACT.Sigmoid, bias=vec("w0", p, p + 1)).then_inc(*A.inc("prep_act"))
            for p in range(4):
                act.wait_ge(sems["prep_mm"], 4 + p + 1)
                f(AG[:, p, :], PB[4 + p][:, :], ACT.Sigmoid, bias=vec("a0", p, p + 1)).then_inc(*A.inc("prep_act"))
            for p in range(4):
                act.wait_ge(sems["prep_mm"], 8 + p + 1)
                f(GT[:, p, :], PB[4 + p][:, :], ACT.Copy).then_inc(*A.inc("prep_act"))
            for m in range(4):
                used("diff_q", m)
                f(DQ[:, m, :], PB[(14 + m) % 4][:, :], ACT.Copy, scale=0.125).then_inc(*A.inc("ev_act"))
            for p in range(4):
                act.wait_ge(sems["kkln_in"], p + 1)
                f(CS[:, p, :], CS[:, p, :], ACT.Ln).then_inc(*A.inc())
            act.wait_ge(*A.latest)
            for p in range(4):
                f(CS[:, p, :], CS[:, p, :], ACT.Exp, scale=-0.5, bias=sc("kkb")).then_inc(*A.inc("kk_rs"))
            for m in range(4):
                used("diff_k", m)
                f(DK[:, m, :], PB[(18 + m) % 4][:, :], ACT.Copy).then_inc(*A.inc("ev_act"))
            for p in range(4):
                act.wait_ge(sems["cs_ready"], p + 1)
                f(SIG[:, p, :], SIG[:, p, :], ACT.Exp, scale=-DEC).then_inc(*A.inc("exp_ready"))
                if p >= 2:
                    act.wait_ge(sems["exp_used"], p - 1)
                f(TMP[:, p % 2, :], CS[:, p, :], ACT.Exp, scale=DEC).then_inc(*A.inc("exp_ready"))
                f(CS[:, p, :], CS[:, p, :], ACT.Exp, scale=-DEC).then_inc(*A.inc("exp_ready"))
            for m in range(5):
                if m < 4:
                    used("diff_v", m)
                    f(DV[:, m, :], PB[(22 + m) % 4][:, :], ACT.Copy).then_inc(*A.inc("vt_ev"))
                if m:
                    act.wait_ge(sems["vt_tr"], VT["diff"] + m)
                    f(DV[:, m - 1, :], PB[4 + (m - 1) % 2][:, :], ACT.Copy).then_inc(*A.inc("ev_act"))

            def tr_evac(name, j, n, bank=0):
                b = BASE[name]
                act.wait_ge(sems["tr_mm"], b + j + 1)
                if j >= 2:
                    act.wait_ge(sems["pv_mm"], b + j - 1)
                f(PT_of(name)[:, j % 2, 0:n * P], PB[bank][:, 0:n * P], ACT.Copy).then_inc(*A.inc("tr_ev"))

            steps = STEPS["diff"]
            for i in range(len(steps) + PIPE + 2):
                if i < len(steps):
                    w = (steps[i][1] + 1) * P
                    act.wait_ge(sems["sc_max"], i + 1)
                    if i >= 2:
                        act.wait_ge(sems["tr_mm"], i - 1)
                    f(PR1[:, i % 2, 0:w], PB[4 + 2 * (i % 2)][:, 0:w], ACT.Exp, bias=nmax(i, 0), accum_out=psum_of(i, 0))\
                        .then_inc(*A.inc("sc_exp"))
                    f(PR2[:, i % 2, 0:w], PB[5 + 2 * (i % 2)][:, 0:w], ACT.Exp, bias=nmax(i, 1), accum_out=psum_of(i, 1))\
                        .then_inc(*A.inc("sc_exp"))
                if 2 <= i < len(steps) + 2:
                    tr_evac("diff", i - 2, steps[i - 2][1] + 1)
                j = i - PIPE
                if 0 <= j < len(steps) and steps[j][1] == TT - 1:
                    h = steps[j][0]
                    act.wait_ge(sems["pv_mm"], j + 1)
                    if h:
                        act.wait_ge(sems["on_mm"], h)
                    f(OSQ, PB[2 + h % 2][:, :], ACT.Square).then_inc(*A.inc("on_sq"))
                j = i - PIPE - 1
                if 0 <= j < len(steps) and steps[j][1] == TT - 1:
                    h = steps[j][0]
                    act.wait_ge(sems["on_mm"], h + 1)
                    if h:
                        act.wait_ge(sems["on_out"], h)
                    f(OLN, PB[1][:, :], ACT.Ln, scale=1.0 / P, bias=sc("eps1")).then_inc(*A.inc())
                    act.wait_ge(*A.latest)
                    f(OLN, OLN, ACT.Exp, scale=-0.5).then_inc(*A.inc("on_rs"))
            end_stage()

            for t in range(TT):
                for n, dst in enumerate((TOKA, TOKV, TOKB, TOKK)):
                    act.wait_ge(sems["ch_tr"], 4 * t + n + 1)
                    f(dst, PB[4 + n][:, :].rearrange("p (a n) -> p a n", n=P), ACT.Copy).then_inc(*A.inc("ch_trev"))
                act.wait_ge(sems["w1_mm"], 3 * t + 1)
                f(P1, PB[4][:, :].rearrange("p (a n) -> p a n", n=P), ACT.Copy).then_inc(*A.inc("w1_ev"))
                act.wait_ge(sems["w1_mm"], 3 * t + 2)
                f(TA, PB[5][:, :].rearrange("p (a n) -> p a n", n=P), ACT.Copy).then_inc(*A.inc("w1_ev"))
                act.wait_ge(sems["w1_mm"], 3 * t + 3)
                f(W1, PB[6][:, :].rearrange("p (a n) -> p a n", n=P), ACT.Copy, scale=-1.0).then_inc(*A.inc("w1_ev"))
                act.wait_ge(sems["y_mm"], t + 1)
                f(HN[:, 0:4, tile(t)], PB[7][:, :].rearrange("p (a n) -> p a n", n=P), ACT.Copy).then_inc(*A.inc("y_ev"))
                end_stage()
            act.preload_act_table_set("natural_log")
            for p in range(4):
                act.wait_ge(sems["gn_c"], p + 1)
                f(SIG[:, p, :], HN[:, p, :], ACT.Square).then_inc(*A.inc("gn_sq"))
            for p in range(4):
                act.wait_ge(sems["gn_mm"], 4 + p + 1)
                f(SIG[:, p, :], PB[4 + p][:, :], ACT.Ln, scale=1.0 / 64, bias=sc("gn")).then_inc(*A.inc())
            act.wait_ge(*A.latest)
            for p in range(4):
                f(SIG[:, p, :], SIG[:, p, :], ACT.Exp, scale=-0.5).then_inc(*A.inc("gn_rs"))
            end_stage()

            act.dma_start(MT, mem_d).then_inc(sems["mem_in"], 16)
            round_x("out")
            act.preload_act_table_set("natural_log")
            act.wait_ge(sems["mem_in"], 16)
            for k in range(KT):
                f(SQ[:, k, 0:MEM], MT[:, k, :], ACT.Square).then_inc(*A.inc("norm_sq"))
            rstd(N_SRC, "eps1", MEM)
            round_x("src", N_SRC)
            act.preload_act_table_set("natural_log")
            for k in range(KT):
                act.wait_ge(sems["norm_h"], RES[N_MEM] + k + 1)
                f(SQ[:, k, :], H[:, k, :], ACT.Square).then_inc(*A.inc("norm_sq"))
            rstd(N_MEM, "eps1")
            round_x("mem", N_MEM)
            for m in range(8):
                used("mem_k", m)
                f(MK[:, m, :], PB[m % 4][:, 0:MEM], ACT.Copy).then_inc(*A.inc("ev_act"))
            for m in range(9):
                if m < 8:
                    used("mem_v", m)
                    f(MV[:, :, tile(m)], PB[m % 4][:, 0:MEM].rearrange("p (t n) -> p t n", t=2), ACT.Copy).then_inc(*A.inc("vt_ev"))
                if m:
                    act.wait_ge(sems["vt_tr"], VT["mem"] + m)
                    f(MV[:, :, tile(m - 1)], PB[5 + (m - 1) % 2][:, 0:MEM].rearrange("p (t n) -> p t n", t=2), ACT.Copy)\
                        .then_inc(*A.inc("ev_act"))
            for m in range(8):
                used("mem_q", m)
                f(MQ[:, m, :], PB[m % 4][:, :], ACT.Copy, scale=1.0 / 16).then_inc(*A.inc("ev_act"))
            steps = STEPS["mem"]
            b = BASE["mem"]
            for i in range(len(steps) + PIPE):
                if i < len(steps):
                    act.wait_ge(sems["sc_max"], b + i + 1)
                    if i >= 2:
                        act.wait_ge(sems["tr_mm"], b + i - 1)
                    f(MPR[:, i % 2, 0:MEM], PB[4 + i % 2][:, 0:MEM], ACT.Exp, bias=nmax(i), accum_out=psum_of(i))\
                        .then_inc(*A.inc("sc_exp"))
                if 2 <= i < len(steps) + 2:
                    tr_evac("mem", i - 2, 2)
                if i >= PIPE:
                    h, t = steps[i - PIPE]
                    act.wait_ge(sems["pv_mm"], b + i - PIPE + 1)
                    f(MO[:, 2 * h:2 * h + 2, tile(t)], PB[2 + (i - PIPE) % 2][:, 0:MEM].rearrange("p (j n) -> p j n", j=2), ACT.Copy)\
                        .then_inc(*A.inc("o_ev"))
            act.wait_ge(*A.latest)
            round_x("mo")
            act.preload_act_table_set("natural_log")
            for k in range(KT):
                act.wait_ge(sems["norm_h"], RES[N_MLP] + k + 1)
                f(SQ[:, k, :], H[:, k, :], ACT.Square).then_inc(*A.inc("norm_sq"))
            end_stage()
            rstd(N_MLP, "eps1")
            round_x("mlp0", N_MLP)

            def mlp(n, nxt, eps):
                for half in range(2):
                    done = 32 * n + 16 * half
                    up = UNIT[f"up{n}{'ab'[half]}"]

                    def hidden_tile(i, j):
                        act.wait_ge(sems["w_used"], i * 4 + (up + j + 1))
                        if not isinstance(i, int) or j >= 2:
                            act.wait_ge(sems["mlp_a"], i * 4 + (done + j - 1))
                        act.activation(RL[:, j % 2, :], PB[j][:, :], ACT.Relu).then_inc(sems["relu"], 1)
                        act.wait_ge(sems["relu"], i * 4 + (done + j + 1))
                        act.activation(RL[:, j % 2, :], RL[:, j % 2, :], ACT.Square).then_inc(sems["hid_sq"], 1)
                        act.wait_ge(sems["hid_sq"], i * 4 + (done + j + 1))
                        hi = MAH[:, i * 4 + j, :] if isinstance(i, int) else MAH[:, bass.ds(i * 4 + j, 1), :].rearrange("p a n -> p (a n)")
                        act.activation(hi, RL[:, j % 2, :], ACT.Copy).then_inc(sems["hid_hi"], 1)
                    for j in range(4):
                        hidden_tile(0, j)
                    with act.Fori(1, 4) as i:
                        for j in range(4):
                            hidden_tile(i, j)
                if nxt is None:
                    return
                act.preload_act_table_set("natural_log")
                for k in range(KT):
                    act.wait_ge(sems["norm_h"], RES[nxt] + k + 1)
                    f(SQ[:, k, :], H[:, k, :], ACT.Square).then_inc(*A.inc("norm_sq"))
                if nxt == N_MIX1:
                    end_stage()
                rstd(nxt, eps)
            mlp(0, N_FINAL, "eps1")

            act.preload_act_table_set("natural_log")
            for k in range(KT):
                act.wait_ge(sems["norm_out"], N_FINAL * KT + k + 1)
                f(SQ[:, k, :], H[:, k, :], ACT.Square).then_inc(*A.inc("norm_sq"))
            end_stage()
            rstd(N_MIX0, "eps2")
            round_x("ab", N_MIX0)

            def ev2(i, out, scale=1.0, func=ACT.Copy):
                act.wait_ge(sems["w_used"], UNIT["i_q"] + i + 1)
                f(out, PB[i % 2][:, :], func, scale=scale).then_inc(*A.inc("ev_act"))

            def head_rstd(j, bank, out, done, nm, nr):
                act.wait_ge(sems[nm], j + 1)
                if j >= 2:
                    act.wait_ge(sems[done], j - 1)
                f(out, PB[bank][:, :], ACT.Ln, scale=1.0 / P, bias=sc("eps2")).then_inc(*A.inc())
                act.wait_ge(*A.latest)
                f(out, out, ACT.Exp, scale=-0.5).then_inc(*A.inc(nr))
            for i in range(30):
                dst, s_ = ((IQ[:, i, :], 1.0) if i < 4 else (IK, 1.0) if i == 4 else (MISC, 1.0) if i == 5 else
                           (GQ[:, i - 6, :], 0.125) if i < 8 else (GK[:, i - 8, :], 1.0) if i < 10 else
                           (QA[:, i - 10, :], 1.0) if i < 14 else (KA[:, i - 14, :], 1.0) if i < 18 else
                           (VA[:, i - 18, :], 1.0) if i < 22 else (GV[:, i - 22, :], 1.0) if i < 26 else
                           (OG[:, i - 26, :], 1.0))
                if 19 <= i < 27:
                    last_v = VA[:, i - 19, :] if i < 23 else GV[:, i - 23, :]
                    act.wait_ge(sems["vt_tr"], VT["ab"] + i - 18)
                    f(last_v, PB[2][:, :], ACT.Copy).then_inc(*A.inc("ev_act"))
                if 18 <= i < 26:
                    act.wait_ge(sems["w_used"], UNIT["i_q"] + i + 1)
                    f(dst, PB[i % 2][:, :], ACT.Copy).then_inc(*A.inc("vt_ev"))
                elif i < 26:
                    ev2(i, dst, s_)
                else:
                    ev2(i, dst, 1.0, ACT.Silu)
                if i == 7:
                    for p in range(2):
                        act.wait_ge(sems["gate_in"], p + 1)
                        f(GE[1][:, p, :], GE[0][:, p, :], ACT.Abs).then_inc(*A.inc())
                    act.wait_ge(*A.latest)
                    f(GE[1], GE[1], ACT.Exp, scale=-1.0).then_inc(*A.inc())
                    act.wait_ge(*A.latest)
                    f(GE[1], GE[1], ACT.Ln, bias=sc("one")).then_inc(*A.inc("gate_ln"))
                if 7 <= i < 11:
                    for n in range(6 * (i - 7), 6 * (i - 7) + 6):
                        w = (INDEX_STEPS[n][0] + 1) * P
                        act.wait_ge(sems["idx_mm"], n + 1)
                        if n >= 2:
                            act.wait_ge(sems["idx_acc"], n - 1)
                        f(RLU[:, n % 2, 0:w], PB[6 + n % 2][:, 0:w], ACT.Relu, scale=0.125).then_inc(*A.inc("idx_r"))
                if 10 <= i < 18:
                    j = i - 10
                    if j >= 2:
                        act.wait_ge(sems["a_mm"], j - 1)
                    act.wait_ge(sems["ev_act"], EV2 + i + 1)
                    f(SQA[:, j % 2, :], dst, ACT.Square).then_inc(*A.inc("a_sq"))
                if 11 <= i < 19:
                    head_rstd(i - 11, 2, RA[:, (i - 11) % 2, :], "a_sc", "a_mm", "a_rs")
                if i in LEVEL_AT and LEVEL_AT[i] < 7:
                    l = LEVEL_AT[i] + 1
                    act.wait_ge(sems["lv_d"], l)
                    f(GE[l % 2], GE[l % 2], ACT.Abs).then_inc(*A.inc())
                    act.wait_ge(*A.latest)
                    f(GE[l % 2], GE[l % 2], ACT.Exp, scale=-1.0 / 16).then_inc(*A.inc("lv_e"))
                if i == 12:
                    act.wait_ge(sems["g_ed"], 1)
                    f(GEB, GB, ACT.Exp, scale=1.0 / 16).then_inc(*A.inc("g_eb"))
                    f(GED, GED, ACT.Exp, scale=1.0 / 16).then_inc(*A.inc("g_ede"))
                if i == 26:
                    for n in range(2):
                        act.wait_ge(sems["ke_tr"], n + 1)
                        f(GKT[:, 2 * n:2 * n + 2, :], PB[4 + n][:, :].rearrange("p (t n) -> p t n", n=256), ACT.Copy)\
                            .then_inc(*A.inc("ke_ev"))
                if i == 28:
                    for h in range(4):
                        act.wait_ge(sems["go_mm"], h + 1)
                        f(GSQ[:, h, :], PB[4 + h][:, :], ACT.Square).then_inc(*A.inc("go_sq"))
            for h in range(4):
                act.wait_ge(sems["go_nm"], h + 1)
                f(GSQ[:, h, :], PB[2 + h % 2][:, :], ACT.Ln, scale=1.0 / P, bias=sc("eps2")).then_inc(*A.inc("go_ln"))
            act.wait_ge(*A.latest)
            for h in range(4):
                f(GSQ[:, h, :], GSQ[:, h, :], ACT.Exp, scale=-0.5).then_inc(*A.inc("go_rs"))

            steps = STEPS["A"]
            b = BASE["A"]
            for i in range(len(steps) + PIPE):
                if i < len(steps):
                    w = (steps[i][1] + 1) * P
                    act.wait_ge(sems["sc_max"], b + i + 1)
                    if i >= 2:
                        act.wait_ge(sems["tr_mm"], b + i - 1)
                    f(APR[:, i % 2, 0:w], PB[i % 2][:, 0:w], ACT.Exp, bias=nmax(i), accum_out=psum_of(i))\
                        .then_inc(*A.inc("sc_exp"))
                if 2 <= i < len(steps) + 2:
                    tr_evac("A", i - 2, steps[i - 2][1] + 1, 2)
                if i >= PIPE:
                    h, t = steps[i - PIPE]
                    act.wait_ge(sems["pv_mm"], b + i - PIPE + 1)
                    f(HN[:, h, tile(t)], PB[3 + (i - PIPE) % 2][:, 0:P], ACT.Copy).then_inc(*A.inc("o_ev"))
            act.wait_ge(*A.latest)
            act.wait_ge(sems["gla_out"], 4)
            round_x("oab")
            act.preload_act_table_set("natural_log")
            for k in range(KT):
                act.wait_ge(sems["norm_h"], RES[N_FFN0] + k + 1)
                f(SQ[:, k, :], H[:, k, :], ACT.Square).then_inc(*A.inc("norm_sq"))
            end_stage()
            rstd(N_FFN0, "eps2")
            round_x("mlp1", N_FFN0)
            mlp(1, N_MIX1, "eps2")
            round_x("c", N_MIX1)

            steps = STEPS["C"]
            b = BASE["C"]

            def c_transposed(j):
                w = (steps[j][1] + 1) * P
                act.wait_ge(sems["tr_mm"], b + j + 1)
                if j >= 4:
                    act.wait_ge(sems["pv_mm"], b + j - 3)
                f(CPT[:, j % 4, 0:w], PB[0][:, 0:w], ACT.Copy).then_inc(*A.inc("tr_ev"))

            def c_rms(c, hd):
                act.wait_ge(sems["c_nm"], 2 * hd + c + 1)
                if hd:
                    act.wait_ge(sems["c_sc"], 2 * hd + c - 1)
                f(CRS[:, c, :], PB[7][:, :], ACT.Ln, scale=1.0 / P, bias=sc("eps2")).then_inc(*A.inc("c_rln"))
            for r in C_ROUNDS:
                hd = r // 2 + 2
                new = [(i, (steps[i][1] + 1) * P) for i in (2 * r, 2 * r + 1) if 0 <= i < len(steps)]
                if 0 <= 2 * r - 4 < len(steps):
                    c_transposed(2 * r - 4)
                for i, w in new:
                    act.wait_ge(sems["sc_mm"], b + i + 1)
                    if i >= 4:
                        act.wait_ge(sems["c_nl"], i - 3)
                    f(CL[:, i % 4, 0:w], PB[4 + i % 3][:, 0:w], ACT.Abs).then_inc(*A.inc("c_abs"))
                for i, w in new:
                    act.wait_ge(sems["c_abs"], i + 1)
                    f(CL[:, i % 4, 0:w], CL[:, i % 4, 0:w], ACT.Exp, scale=-1.0).then_inc(*A.inc("c_exp"))
                if r % 2 == 0 and 0 <= hd - 1 < 8:
                    for c in range(2):
                        act.wait_ge(sems["c_rln"], 2 * (hd - 1) + c + 1)
                        f(CRS[:, c, :], CRS[:, c, :], ACT.Exp, scale=-0.5).then_inc(*A.inc("c_rs"))
                for j in (2 * r - 2, 2 * r - 1):
                    if 0 <= j < len(steps):
                        w = (steps[j][1] + 1) * P
                        act.wait_ge(sems["c_la"], j + 1)
                        if j >= 4:
                            act.wait_ge(sems["tr_mm"], b + j - 3)
                        f(CPR[:, j % 4, 0:w], CN[:, j % 4, 0:w], ACT.Exp).then_inc(*A.inc("c_prob"))
                if 0 <= 2 * r - 3 < len(steps):
                    c_transposed(2 * r - 3)
                for i, w in new:
                    act.wait_ge(sems["c_exp"], i + 1)
                    f(CL[:, i % 4, 0:w], CL[:, i % 4, 0:w], ACT.Ln, bias=sc("one")).then_inc(*A.inc("c_l"))
                if r % 2 == 0 and 0 <= hd - 1 < 8:
                    act.wait_ge(sems["vt_tr"], VT["c"] + hd)
                    f(CV[:, hd - 1, :], PB[7][:, :], ACT.Copy).then_inc(*A.inc("ev_act"))
                if r % 2 == 0 and hd < 8:
                    for c, x in enumerate((CQ, CK)):
                        act.wait_ge(sems["w_used"], UNIT["c_in"] + 3 * hd + c + 1)
                        f(x[:, hd, :], PB[2 + c][:, :], ACT.Copy).then_inc(*A.inc("ev_act"))
                        act.wait_ge(*A.latest)
                        if hd:
                            act.wait_ge(sems["c_nm"], 2 * hd + c - 1)
                        f(CSQ[:, c, :], x[:, hd, :], ACT.Square).then_inc(*A.inc("c_sq"))
                if r % 2 and hd < 8:
                    c_rms(0, hd)
                    act.wait_ge(sems["w_used"], UNIT["c_in"] + 3 * hd + 3)
                    f(CV[:, hd, :], PB[2][:, :], ACT.Copy).then_inc(*A.inc("vt_ev"))
                    c_rms(1, hd)
                if r >= 3:
                    h, t = steps[2 * r - 6]
                    act.wait_ge(sems["pv_mm"], b + 2 * r - 4)
                    f(CQ[:, h, t * P:(t + 2) * P], PB[1][:, 0:2 * P], ACT.Copy).then_inc(*A.inc("o_ev"))
            act.wait_ge(*A.latest)
            round_x("oc")
            act.preload_act_table_set("natural_log")
            for k in range(KT):
                act.wait_ge(sems["norm_h"], RES[N_FFN1] + k + 1)
                f(SQ[:, k, :], H[:, k, :], ACT.Square).then_inc(*A.inc("norm_sq"))
            end_stage()
            rstd(N_FFN1, "eps2")
            round_x("mlp2", N_FFN1)
            mlp(2, None, None)

        @block.vector
        def _(dve):
            D = Count(sems, "dve_step")
            ends = [0]

            def end_stage():
                ends[0] += 1
                dve.drain().then_inc(sems["stage"], 1)
                dve.wait_ge(sems["stage"], 3 * ends[0])

            def tt(out, a, b, op):
                return dve.tensor_tensor(out, a, b, op)

            def stt(out, a, scalar, b, op0, op1):
                return dve.scalar_tensor_tensor(out, a, scalar, b, op0, op1)

            def ts(out, a, s1, s2, op0, op1=None):
                if op1 is None:
                    return dve.tensor_scalar(out, a, s1, None, op0)
                return dve.tensor_scalar(out, a, s1, s2, op0, op1)

            def add_squares(n, k, w=S):
                dve.wait_ge(sems["norm_sq"], n * KT + k + 1)
                if k:
                    dve.wait_ge(*D.latest)
                    tt(ACC[:, 0:w], SQ[:, 0, 0:w] if k == 1 else ACC[:, 0:w], SQ[:, k, 0:w], ALU.add)\
                        .then_inc(*D.inc("norm_acc" if k == KT - 1 else None))

            def rest(x, k):
                dve.wait_ge(sems["x_hi"], SPLIT_NO[x] * KT + k + 1)
                tt(x_lo(x, k), x_full(x, k), x_hi(x, k).bitcast(F32), ALU.subtract).then_inc(*D.inc("x_lo"))

            def scale_out(n, src, w, width=S, x=None):
                dve.wait_ge(sems["norm_rs"], n + 1)
                for k in range(KT):
                    stt(x_full(x, k) if x else src(k), src(k), vec(w, k, k + 1), RS[:, 0:width], ALU.mult, ALU.mult)\
                        .then_inc(*D.inc("norm_out"))
                if x:
                    for k in range(KT):
                        rest(x, k)

            def residual(n, unit, bank, per=1):
                for k in range(KT):
                    dve.wait_ge(sems["w_used"], UNIT[unit] + per * (k + 1))
                    tt(H[:, k, :], H[:, k, :], PB[bank(k)][:, :], ALU.add).then_inc(*D.inc("norm_h"))
                    if k:
                        add_squares(n, k - 1)
                add_squares(n, KT - 1)

            def rd(out, in_, op, negate=False):
                return dve.tensor_reduce(out, in_, AX.X, op, negate=negate)

            def mlp(n):
                for half in range(2):
                    done = 32 * n + 16 * half
                    with dve.Fori(0, 4) as i:
                        for j in range(4):
                            dve.wait_ge(sems["hid_hi"], i * 4 + (done + j + 1))
                            lo, hi = (a[:, bass.ds(i * 4 + j, 1), :].rearrange("p a n -> p (a n)") for a in (MAL, MAH))
                            tt(lo, RL[:, j % 2, :], hi.bitcast(F32), ALU.subtract).then_inc(sems["mlp_a"], 1)
                    if half == 0:
                        for k in range(KT):
                            dve.wait_ge(sems["w_used"], UNIT[f"down{n}a"] + 2 * (k + 1))
                            tt(H[:, k, :], H[:, k, :], PB[6 + k % 2][:, :], ALU.add).then_inc(*D.inc("half_h"))
                dve.wait_ge(sems["half_h"], KT * (n + 1))

            dve.memset(PX[:, :, 0:1], 0.0).then_inc(*D.inc())
            dve.wait_ge(sems["v_in"], 16)
            dve.wait_ge(sems["c_in"], 16)
            tt(LAMP, vec("lam", 0, 2), vec("lam", 2, 4), ALU.mult).then_inc(*D.inc("lam_in"))
            ts(SUBW, vec("subln"), 0.8, None, ALU.mult).then_inc(*D.inc())
            ts(KA1, vec("k_a"), -1.0, 1.0, ALU.mult, ALU.add).then_inc(*D.inc())
            for k in range(KT):
                add_squares(N_MIX, k)
            dve.wait_ge(sems["x_in"], 16)
            scale_out(N_MIX, lambda k: H[:, k, :], "norm_mix", x="mix")
            dve.wait_ge(sems["lam_exp"], 1)
            tt(NLAM, LAME[:, 1:2], LAME[:, 0:1], ALU.subtract).then_inc(*D.inc())
            dve.wait_ge(*D.latest)
            ts(NLAM, NLAM, 0.2, None, ALU.subtract).then_inc(*D.inc())

            def shift(m, name=None):
                dve.wait_ge(sems["ev_act"], m + 1)
                cur = PX[:, m, 1:PW]
                tt(TMP[:, m % 2, :], PX[:, m, 0:S], cur, ALU.subtract).then_inc(*D.inc())
                dve.wait_ge(*D.latest)
                stt(cur, TMP[:, m % 2, :], vec("mu", m, m + 1), cur, ALU.mult, ALU.add).then_inc(*D.inc(name))
            shift(LORA, "lora_in")
            shift(GD, "lora_in")
            for p in range(4):
                shift(K0 + p)
            dve.wait_ge(*D.latest)
            for p in range(4):
                ts(KK[:, p, :], PX[:, K0 + p, 1:PW], vec("k_k", p, p + 1), None, ALU.mult).then_inc(*D.inc())
            dve.wait_ge(*D.latest)
            for p in range(4):
                tt(CS[:, p, :], KK[:, p, :], KK[:, p, :], ALU.mult).then_inc(*D.inc("kk_sq"))
            for m in range(R0, 14):
                shift(m)
            for p in range(4):
                dve.wait_ge(sems["prep_act"], 4 + p + 1)
                ts(TMP[:, p % 2, :], AG[:, p, :], vec("k_a", p, p + 1), KA1[:, p:p + 1], ALU.mult, ALU.add).then_inc(*D.inc())
                dve.wait_ge(*D.latest)
                tt(PX[:, K0 + p, 1:PW], PX[:, K0 + p, 1:PW], TMP[:, p % 2, :], ALU.mult).then_inc(*D.inc())
                dve.wait_ge(*D.latest)
                stt(BON[:, p, :], PX[:, R0 + p, 1:PW], vec("r_k", p, p + 1), PX[:, K0 + p, 1:PW], ALU.mult, ALU.mult)\
                    .then_inc(*D.inc("bonus_in"))
            for p in range(4):
                dve.wait_ge(sems["prep_mm"], 12 + p + 1)
                ts(CS[:, p, :], PB[4 + p][:, :], 1e-24, KK_SCALE, ALU.max, ALU.mult).then_inc(*D.inc("kkln_in"))
            for p in range(4):
                dve.wait_ge(sems["kk_rs"], p + 1)
                tt(KK[:, p, :], KK[:, p, :], CS[:, p, :], ALU.mult).then_inc(*D.inc())
                dve.wait_ge(*D.latest)
                tt(AG[:, p, :], AG[:, p, :], KK[:, p, :], ALU.mult).then_inc(*D.inc())
            for p in range(4):
                dve.tensor_tensor_scan(CS[:, p, :], cst("reset64"), SIG[:, p, :], 0.0, ALU.mult, ALU.add).then_inc(*D.inc())
                dve.wait_ge(*D.latest)
                tt(SIG[:, p, :], CS[:, p, :], SIG[:, p, :], ALU.subtract).then_inc(*D.inc("cs_ready"))
            for p in range(4):
                dve.wait_ge(sems["prep_mm"], 16 + p + 1)
                tt(BON[:, p, :], PB[4 + p][:, :], PX[:, V0 + p, 1:PW], ALU.mult).then_inc(*D.inc("prep_dve"))
            for p in range(4):
                dve.wait_ge(sems["exp_ready"], 3 * p + 3)
                tt(KK[:, p, :], KK[:, p, :], SIG[:, p, :], ALU.mult).then_inc(*D.inc())
                tt(AG[:, p, :], AG[:, p, :], TMP[:, p % 2, :], ALU.mult).then_inc(*D.inc())
                tt(PX[:, K0 + p, 1:PW], PX[:, K0 + p, 1:PW], TMP[:, p % 2, :], ALU.mult).then_inc(*D.inc("exp_used"))
                tt(PX[:, R0 + p, 1:PW], PX[:, R0 + p, 1:PW], CS[:, p, :], ALU.mult).then_inc(*D.inc())
            dve.tensor_copy(ECH, CS[:, :, 63::64]).then_inc(*D.inc())
            dve.wait_ge(*D.latest)

            steps = STEPS["diff"]
            for i in range(len(steps) + PIPE + 2):
                if i < len(steps):
                    w = (steps[i][1] + 1) * P
                    dve.wait_ge(sems["sc_mm"], i + 1)
                    banks = [PB[4 + 2 * (i % 2)], PB[5 + 2 * (i % 2)]]
                    for pb in banks:
                        tt(pb[:, w - 64:w], pb[:, w - 64:w], cst("chunk_bias"), ALU.add).then_inc(*D.inc())
                    dve.wait_ge(*D.latest)
                    for m, pb in enumerate(banks):
                        rd(nmax(i, m), pb[:, 0:w], ALU.max, negate=True).then_inc(*D.inc("sc_max" if m else None))
                j = i - 1
                if 0 <= j < len(steps):
                    w = (steps[j][1] + 1) * P
                    dve.wait_ge(sems["sc_exp"], 2 * (j + 1))
                    dve.reciprocal(recip(j, 0, 2), psum_of(j, 0, 2)).then_inc(*D.inc())
                    dve.wait_ge(*D.latest)
                    tt(recip(j, 1), recip(j, 1), NLAM, ALU.mult).then_inc(*D.inc())
                    dve.wait_ge(*D.latest)
                    ts(PR2[:, j % 2, 0:w], PR2[:, j % 2, 0:w], recip(j, 1), None, ALU.mult).then_inc(*D.inc())
                    dve.wait_ge(*D.latest)
                    stt(PR1[:, j % 2, 0:w], PR1[:, j % 2, 0:w], recip(j, 0), PR2[:, j % 2, 0:w], ALU.mult, ALU.add)\
                        .then_inc(*D.inc("prob"))
                j = i - PIPE - 1
                if 0 <= j < len(steps) and steps[j][1] == TT - 1:
                    h = steps[j][0]
                    dve.wait_ge(sems["on_rs"], h + 1)
                    stt(HN[:, 4 + h, :], PB[2 + h % 2][:, :], SUBW, OLN, ALU.mult, ALU.mult).then_inc(*D.inc("on_out"))
            end_stage()

            for g in GS:
                dve.memset(g, 0.0).then_inc(*D.inc())
            dve.wait_ge(*D.latest)

            def two(bank):
                return PB[bank][:, :].rearrange("p (a n) -> p a n", n=256)

            def four(bank):
                return PB[bank][:, :].rearrange("p (a n) -> p a n", n=P)

            def heads4(x, q):
                return x[:, q::2, :]
            masks = cst("bd_strict", 0, 256).unsqueeze(1).to_broadcast([P, 2, 256])
            pairm = cst("low_mask", 0, 128).unsqueeze(1).to_broadcast([P, 4, P])
            pairt = cst("gla_mask", 0, 128).unsqueeze(1).to_broadcast([P, 4, P])
            eye = cst("ident").unsqueeze(1).to_broadcast([P, 4, P])
            for t in range(TT):
                ech = ECH[:, :, 2 * t:2 * t + 2].unsqueeze(3).to_broadcast([P, 4, 2, 64])
                for src, dst in ((AG[:, :, tile(t)], BP), (PX[:, K0:K0 + 4, 1 + t * P:1 + (t + 1) * P], KP)):
                    tt(dst.rearrange("p a (c n) -> p a c n", n=64), src.rearrange("p a (c n) -> p a c n", n=64), ech, ALU.mult)\
                        .then_inc(*D.inc("ch_in"))
                for n in range(8):
                    dve.wait_ge(sems["ch_aq"], 10 * t + n + 1)
                    h = 4 * (n % 4 // 2) + n % 2
                    dst = AQ if n < 4 else BQ
                    tt(dst[:, h:h + 3:2, :], two(n % 4), masks, ALU.mult).then_inc(*D.inc("ch_aqev"))
                for q in range(2):
                    dve.wait_ge(sems["ch_aq"], 10 * t + 8 + q + 1)
                    tt(heads4(TI, q), four(q), pairm, ALU.mult).then_inc(*D.inc("ch_aqev"))
                dve.wait_ge(*D.latest)
                for q in range(2):
                    tt(heads4(TI, q), eye, heads4(TI, q), ALU.subtract).then_inc(*D.inc("ch_t0ev"))
                for q in range(2):
                    tt(heads4(UI, q), AQ[:, q::2, 0:P], pairt, ALU.mult).then_inc(*D.inc())
                dve.wait_ge(*D.latest)
                for q in range(2):
                    tt(heads4(UI, q), eye, heads4(UI, q), ALU.subtract).then_inc(*D.inc("ch_t0ev"))
                for l in range(5):
                    m = cst("low_mask", (l + 1) * P, (l + 2) * P).unsqueeze(1).to_broadcast([P, 4, P])
                    for q in range(2):
                        dve.wait_ge(sems["lv_x"], 10 * t + 2 * l + q + 1)
                        tt(heads4(XI, q), four(q), m, ALU.mult).then_inc(*D.inc("lv_xev"))
                    for q in range(2):
                        dve.wait_ge(sems["lv_y"], 20 * t + 4 * l + 2 * q + 1)
                        tt(heads4(TI, q), heads4(TI, q), four(2 + q), ALU.subtract).then_inc(*D.inc("lv_yev"))
                        dve.wait_ge(sems["lv_y"], 20 * t + 4 * l + 2 * q + 2)
                        tt(heads4(UI, q), heads4(UI, q), four(4 + q), ALU.subtract).then_inc(*D.inc("lv_yev"))
                for c in (2 * t, 2 * t + 1):
                    r = slice(64 * (c % 2), 64 * (c % 2) + 64)
                    g, g1 = GS[c % 3], GS[(c + 1) % 3]
                    tt(TG, g, ECH[:, :, c:c + 1].to_broadcast([P, 4, P]), ALU.mult).then_inc(*D.inc())
                    dve.wait_ge(sems["sa_mm"], c + 1)
                    tt(SA[r], W1[r], four(0)[r], ALU.subtract).then_inc(*D.inc("sa_ev"))
                    dve.wait_ge(sems["gu_mm"], c + 1)
                    tt(g1[0:64, :, 0:64], TG[0:64, :, 0:64], four(1)[0:64, :, 0:64], ALU.add).then_inc(*D.inc())
                    tt(g1[64:128, :, 64:128], TG[64:128, :, 64:128], four(1)[64:128, :, 64:128], ALU.add)\
                        .then_inc(*D.inc("g_ev"))
                    dve.wait_ge(*D.latest)
                end_stage()

            for p in range(4):
                dve.wait_ge(sems["gn_mm"], p + 1)
                stt(HN[:, p, :], PB[p][:, :], -1.0 / 64, HN[:, p, :], ALU.mult, ALU.add).then_inc(*D.inc("gn_c"))
            for p in range(4):
                dve.wait_ge(sems["gn_rs"], p + 1)
                stt(HN[:, p, :], HN[:, p, :], vec("lnx_w", p, p + 1), SIG[:, p, :], ALU.mult, ALU.mult).then_inc(*D.inc())
                dve.wait_ge(*D.latest)
                stt(HN[:, p, :], HN[:, p, :], vec("lnx_b", p, p + 1), BON[:, p, :], ALU.add, ALU.add).then_inc(*D.inc())
                dve.wait_ge(*D.latest)
                tt(HN[:, p, :], HN[:, p, :], GT[:, p, :], ALU.mult).then_inc(*D.inc("mix_out"))
            end_stage()

            for k in range(KT):
                rest("out", k)
            for k in range(KT):
                add_squares(N_SRC, k, MEM)
            dve.wait_ge(sems["mem_in"], 16)
            scale_out(N_SRC, lambda k: MT[:, k, :], "norm_src", MEM, x="src")
            residual(N_MEM, "out", lambda k: k % 4)
            scale_out(N_MEM, lambda k: H[:, k, :], "norm_mem", x="mem")
            steps = STEPS["mem"]
            for i in range(len(steps) + 1):
                if i < len(steps):
                    dve.wait_ge(sems["sc_mm"], BASE["mem"] + i + 1)
                    rd(nmax(i), PB[4 + i % 2][:, 0:MEM], ALU.max, negate=True).then_inc(*D.inc("sc_max"))
                if i:
                    j = i - 1
                    dve.wait_ge(sems["sc_exp"], EXPB["mem"] + j + 1)
                    dve.reciprocal(recip(j), psum_of(j)).then_inc(*D.inc())
                    dve.wait_ge(*D.latest)
                    ts(MPR[:, j % 2, 0:MEM], MPR[:, j % 2, 0:MEM], recip(j), None, ALU.mult).then_inc(*D.inc("prob"))
            for k in range(KT):
                rest("mo", k)
            residual(N_MLP, "mem_o", lambda k: k % 4)
            end_stage()
            scale_out(N_MLP, lambda k: H[:, k, :], "norm_mlp", x="mlp0")
            mlp(0)
            residual(N_FINAL, "down0b", lambda k: 6 + k % 2, 2)
            scale_out(N_FINAL, lambda k: H[:, k, :], "norm_final")

            for k in range(KT):
                add_squares(N_MIX0, k)
            end_stage()
            scale_out(N_MIX0, lambda k: H[:, k, :], "g_mix0", x="ab")
            ts(GQS, vec("gq_a"), P ** -0.5, None, ALU.mult).then_inc(*D.inc())
            ts(GCS, vec("gq_c"), P ** -0.5, None, ALU.mult).then_inc(*D.inc())

            def rope(j):
                kind = "i" if j < 5 else "a"
                x = rope_plane(j)
                dve.wait_ge(sems["rope_mm"], j + 1)
                tt(T1, PB[3][:, :], cst("sin_" + kind), ALU.mult).then_inc(*D.inc())
                tt(x, x, cst("cos_" + kind), ALU.mult).then_inc(*D.inc())
                dve.wait_ge(*D.latest)
                tt(x, x, T1, ALU.add).then_inc(*D.inc("rope_ev"))
            for j in range(5):
                rope(j)
                if j == 4:
                    dve.wait_ge(sems["iw_tr"], 1)
                    ts(IW, PB[2][:, :].rearrange("p (t n) -> p t n", n=P)[:, :, 32:40], 8 ** -0.5, None, ALU.mult, None)\
                        .then_inc(*D.inc("iw_ev"))
            for p in range(2):
                dve.wait_ge(sems["gate_mm"], p + 1)
                ts(GE[0][:, p, :], PB[4 + p][:, :], vec("b_gate", p, p + 1), None, ALU.add).then_inc(*D.inc("gate_in"))
            dve.wait_ge(sems["gate_ln"], 1)
            stt(GB, GE[0], 0.0, GE[1], ALU.min, ALU.subtract).then_inc(*D.inc())
            dve.wait_ge(*D.latest)
            for p in range(2):
                dve.tensor_tensor_scan(GE[0][:, p, :], cst("reset128"), GB[:, p, :], 0.0, ALU.mult, ALU.add).then_inc(*D.inc())
            dve.wait_ge(*D.latest)
            dve.tensor_copy(GB, GE[0]).then_inc(*D.inc("gb_ready"))

            def rel(l, dst):
                s = LEVELS[l]
                g = GB.rearrange("p a (g n) -> p (a g) n", n=2 * s)
                tt(dst.rearrange("p a (g n) -> p (a g) n", n=2 * s), g, g[:, :, s - 1:s].to_broadcast([P, 1024 // (2 * s), 2 * s]),
                   ALU.subtract).then_inc(*D.inc("lv_d"))
            dve.wait_ge(*D.latest)
            rel(1, GE[1])
            rel(2, GE[0])

            for n, (t, h) in enumerate(INDEX_STEPS):
                w = (t + 1) * P
                dve.wait_ge(sems["idx_r"], n + 1)
                if h == 0:
                    ts(SCORE[:, t, 0:w], RLU[:, n % 2, 0:w], IW[:, t, h:h + 1], None, ALU.mult, None).then_inc(*D.inc("idx_acc"))
                else:
                    dve.wait_ge(*D.latest)
                    stt(SCORE[:, t, 0:w], RLU[:, n % 2, 0:w], IW[:, t, h:h + 1], SCORE[:, t, 0:w], ALU.mult, ALU.add)\
                        .then_inc(*D.inc("idx_acc"))
            dve.wait_ge(*D.latest)
            for t in range(1, TT):
                w = (t + 1) * P
                tt(SCORE[:, t, w - 64:w], SCORE[:, t, w - 64:w], cst("chunk_bias"), ALU.add).then_inc(*D.inc())
            dve.wait_ge(sems["idx_mm"], 24)
            b3 = GB.rearrange("p a (t n) -> p (a t) n", n=P)
            tt(GED.rearrange("p a (t n) -> p (a t) n", n=P), b3[:, :, P - 1:P].to_broadcast([P, 8, P]), b3, ALU.subtract)\
                .then_inc(*D.inc("g_ed"))

            def a_scale(j):
                x = rope_plane(5 + j)
                dve.wait_ge(sems["a_rs"], j + 1)
                stt(x, x, GQS if j < 4 else vec("gk_a"), RA[:, j % 2, :], ALU.mult, ALU.mult).then_inc(*D.inc("a_sc"))

            def topk_round(t, n):
                w = (t + 1) * P
                src = SCORE[:, t, 0:w] if n == 0 else WORK[:, 0:w]
                dve.wait_ge(*D.latest)
                dve.max(TOP, src).then_inc(*D.inc())
                dve.wait_ge(*D.latest)
                if n < 15:
                    dve.match_replace(WORK[:, 0:w], TOP, src, -3.0e38).then_inc(*D.inc())
                else:
                    topk_end(t)

            def topk_end(t):
                w = (t + 1) * P
                s = SCORE[:, t, 0:w]
                thr = TOP[:, 7:8]
                ts(EQ[:, 0:w], s, thr, None, ALU.is_equal).then_inc(*D.inc())
                ts(s, s, thr, None, ALU.is_gt).then_inc(*D.inc())
                dve.wait_ge(*D.latest)
                dve.tensor_reduce(NGT, s, AX.X, ALU.add).then_inc(*D.inc())
                dve.tensor_tensor_scan(WORK[:, 0:w], cst("ones", 0, 1).to_broadcast([P, w]), EQ[:, 0:w], 0.0, ALU.mult, ALU.add)\
                    .then_inc(*D.inc())
                dve.wait_ge(*D.latest)
                ts(NGT, NGT, -1.0, 128.0, ALU.mult, ALU.add).then_inc(*D.inc())
                dve.wait_ge(*D.latest)
                stt(EQ[:, 0:w], WORK[:, 0:w], NGT, EQ[:, 0:w], ALU.is_le, ALU.mult).then_inc(*D.inc())
                dve.wait_ge(*D.latest)
                tt(s, s, EQ[:, 0:w], ALU.add).then_inc(*D.inc())
                dve.wait_ge(*D.latest)
                ts(s, s, -1.0, -NEG, ALU.add, ALU.mult).then_inc(*D.inc())

            rounds = [(t, n) for t in range(1, TT) for n in range(16)]
            for i in range(11, 27):
                if i in LEVEL_AT:
                    l = LEVEL_AT[i]
                    mask = cst("gla_mask", 7 * P, 8 * P) if l == 0 else cst("gla_mask", (l - 1) * P, l * P)
                    for n in range(4):
                        dve.wait_ge(sems["lvl_mm"], 4 * l + n + 1)
                        dst, src = (x.rearrange("p (a n) -> p a n", n=P) for x in (ATT[:, n, :], PB[4 + n][:, :]))
                        if l == 0:
                            tt(dst, src, mask.unsqueeze(1).to_broadcast([P, 4, P]), ALU.mult).then_inc(*D.inc("lvl_ev"))
                        else:
                            dve.copy_predicated(dst, mask.bitcast(mybir.dt.uint32).unsqueeze(1).to_broadcast([P, 4, P]), src)\
                                .then_inc(*D.inc("lvl_ev"))
                    if l < 7:
                        dve.wait_ge(sems["lv_e"], l + 1)
                        tt(GQE, GQ, GE[(l + 1) % 2], ALU.mult).then_inc(*D.inc("lv_in"))
                        tt(GKE, GK, GE[(l + 1) % 2], ALU.mult).then_inc(*D.inc("lv_in"))
                    else:
                        dve.wait_ge(sems["g_ede"], 1)
                        tt(GKE, GK, GED, ALU.mult).then_inc(*D.inc("ke_in"))
                        tt(GQE, GQ, GEB, ALU.mult).then_inc(*D.inc("ke_in"))
                    if l + 3 <= 8:
                        dve.wait_ge(sems["lv_in"], 2 * l + 2)
                        if l + 2 > 2:
                            rel(l + 2, GE[l % 2])
                if i < 19:
                    a_scale(i - 11)
                if 12 <= i < 20:
                    rope(5 + i - 12)
                for t, n in rounds[3 * (i - 11):3 * (i - 11) + 3]:
                    topk_round(t, n)
            for t in range(3):
                dve.wait_ge(sems["kv2_mm"], max(t + 1, 2))
                bank, o = (6, 256 * t) if t < 2 else (7, 0)
                dve.wait_ge(sems["g_eb"], 1)
                if t == 0:
                    dve.tensor_copy(GSH[:, 1, :], PB[bank][:, o:o + 256]).then_inc(*D.inc("sh_ev"))
                else:
                    dve.wait_ge(*D.latest)
                    for p in range(2):
                        e = t * P + P - 1
                        stt(GSH[:, t + 1, p * P:(p + 1) * P], GSH[:, t, p * P:(p + 1) * P], GEB[:, p, e:e + 1], PB[bank][:, o + p * P:o + (p + 1) * P], ALU.mult, ALU.add)\
                            .then_inc(*D.inc("sh_ev" if p else None))
            for h in range(4):
                dve.wait_ge(sems["go_rs"], h + 1)
                stt(HN[:, 4 + h, :], PB[4 + h][:, :], vec("g_gla"), GSQ[:, h, :], ALU.mult, ALU.mult).then_inc(*D.inc("go_ev"))
            dve.wait_ge(*D.latest)
            for h in range(4):
                tt(HN[:, 4 + h, :], HN[:, 4 + h, :], OG[:, h, :], ALU.mult).then_inc(*D.inc("gla_out"))

            steps = STEPS["A"]
            for i in range(len(steps) + 1):
                if i < len(steps):
                    h, t = steps[i]
                    w = (t + 1) * P
                    dve.wait_ge(sems["sc_mm"], BASE["A"] + i + 1)
                    pb = PB[i % 2]
                    if t == 0:
                        tt(pb[:, 64:P], pb[:, 64:P], cst("chunk_bias"), ALU.add).then_inc(*D.inc())
                    else:
                        tt(pb[:, 0:w], pb[:, 0:w], SCORE[:, t, 0:w], ALU.add).then_inc(*D.inc())
                    dve.wait_ge(*D.latest)
                    rd(nmax(i), pb[:, 0:w], ALU.max, negate=True).then_inc(*D.inc("sc_max"))
                if i:
                    j = i - 1
                    w = (steps[j][1] + 1) * P
                    dve.wait_ge(sems["sc_exp"], EXPB["A"] + j + 1)
                    dve.reciprocal(recip(j), psum_of(j)).then_inc(*D.inc())
                    dve.wait_ge(*D.latest)
                    ts(APR[:, j % 2, 0:w], APR[:, j % 2, 0:w], recip(j), None, ALU.mult).then_inc(*D.inc("prob"))
            for k in range(KT):
                rest("oab", k)
            residual(N_FFN0, "out_ab", lambda k: k % 4)
            end_stage()
            scale_out(N_FFN0, lambda k: H[:, k, :], "g_ffn0", x="mlp1")
            mlp(1)
            residual(N_MIX1, "down1b", lambda k: 6 + k % 2, 2)
            end_stage()
            scale_out(N_MIX1, lambda k: H[:, k, :], "g_mix1", x="c")

            steps = STEPS["C"]

            def c_scale(c, h):
                x = (CQ, CK)[c][:, h, :]
                dve.wait_ge(sems["c_rs"], 2 * h + c + 1)
                stt(x, x, (GCS, vec("gk_c"))[c], CRS[:, c, :], ALU.mult, ALU.mult).then_inc(*D.inc("c_sc"))
            c_scale(0, 0)
            c_scale(1, 0)
            for i in range(len(steps)):
                if i % 4 == 0 and i // 4 + 1 < 8:
                    c_scale(0, i // 4 + 1)
                    c_scale(1, i // 4 + 1)
                t = steps[i][1]
                w = (t + 1) * P
                z = PB[4 + i % 3]
                nl, rc, la = CL[:, i % 4, 0:w], CR[:, i % 2, 0:w], CN[:, i % 4, 0:w]
                dve.wait_ge(sems["c_l"], i + 1)
                if i >= 4:
                    dve.wait_ge(sems["c_prob"], i - 3)
                stt(la, z[:, 0:w], 0.0, nl, ALU.max, ALU.add).then_inc(*D.inc("c_nl"))
                dve.wait_ge(*D.latest)
                tt(la[:, w - P:w], la[:, w - P:w], cst("strict"), ALU.mult).then_inc(*D.inc())
                dve.wait_ge(*D.latest)
                dve.tensor_tensor_scan(rc[:, ::-1], cst("ones", 0, 1).to_broadcast([P, w]), la[:, ::-1], 0.0, ALU.mult, ALU.add)\
                    .then_inc(*D.inc())
                dve.wait_ge(*D.latest)
                tt(la, z[:, 0:w], rc, ALU.subtract).then_inc(*D.inc())
                dve.wait_ge(*D.latest)
                tt(la[:, w - P:w], la[:, w - P:w], cst("strict_bias"), ALU.add).then_inc(*D.inc("c_la"))
            for k in range(KT):
                rest("oc", k)
            residual(N_FFN1, "out_c", lambda k: k % 4)
            end_stage()
            scale_out(N_FFN1, lambda k: H[:, k, :], "g_ffn1", x="mlp2")
            mlp(2)
            for k in range(KT):
                dve.wait_ge(sems["w_used"], UNIT["down2b"] + 2 * (k + 1))
                tt(H[:, k, :], H[:, k, :], PB[6 + k % 2][:, :], ALU.add).then_inc(*D.inc("norm_h"))

        @block.tensor
        def _(pe):
            T = Count(sems, None)
            ends = [0]
            unit = [0]
            free = [None] * 8

            def end_stage():
                ends[0] += 1
                pe.drain().then_inc(sems["stage"], 1)
                pe.wait_ge(sems["stage"], 3 * ends[0])
                for b in range(8):
                    free[b] = None

            def take(b):
                if free[b] is not None:
                    pe.wait_ge(sems[free[b][0]], free[b][1])
                    free[b] = None

            def mm(out, lhsT, rhs, start=True, stop=True, **k):
                return pe.matmul(out, lhsT, rhs, start=start, stop=stop, **k)

            def tr(out, in_):
                return pe.transpose(out, in_, cst("ident"))

            def weights(u, j):
                pe.wait_ge(sems["w_split"], u + 1)
                return lambda k: (WH[:, j % 2, tile(k)], WL[:, j % 2, tile(k)])

            def first_pair(banks, x, u, width=S):
                for n, b in enumerate(banks):
                    take(b)
                    w = weights(u + n, u + n)
                    for k in range(KT):
                        if n == 0:
                            pe.wait_ge(sems["x_hi"], SPLIT_NO[x] * KT + k + 1)
                        xh = x_hi(x, k)[:, 0:width]
                        pe.matmul(PB[b][:, 0:width], w(k)[0], xh, start=k == 0, stop=False)
                        pe.matmul(PB[b][:, 0:width], w(k)[1], xh, start=False, stop=False)
                for n, b in enumerate(banks):
                    for k in range(KT):
                        if n == 0:
                            pe.wait_ge(sems["x_lo"], SPLIT_NO[x] * KT + k + 1)
                        ins = pe.matmul(PB[b][:, 0:width], WH[:, (u + n) % 2, tile(k)], x_lo(x, k)[:, 0:width], start=False, stop=k == KT - 1)
                    ins.then_inc(sems["w_used"], 1)

            def product(out, lhs, rhs, start=True, stop=True):
                for k in range(KT):
                    (lh, ll), (rh, rl) = lhs(k), rhs(k)
                    pe.matmul(out, lh, rl, start=start and k == 0, stop=False)
                    pe.matmul(out, ll, rh, start=False, stop=False)
                for k in range(KT):
                    ins = pe.matmul(out, lhs(k)[0], rhs(k)[0], start=False, stop=stop and k == KT - 1)
                return ins

            def planes_of(x, a=0, b=S):
                return lambda k: (x_hi(x, k)[:, a:b], x_lo(x, k)[:, a:b])

            def project(n, bank0, ev, x, first=True, width=S, banks=4, evbase=0):
                for m in range(n):
                    u = unit[0]
                    b = (bank0 + m) % banks
                    if first and m == 0:
                        first_pair((b, (b + 1) % banks), x, u, width)
                    elif not first or m > 1:
                        take(b)
                        product(PB[b][:, 0:width], weights(u, u), planes_of(x, 0, width)).then_inc(*T.inc("w_used"))
                    unit[0] += 1
                    free[b] = (ev, evbase + m + 1)

            def to_tokens(bank, src, n, ev, tiles=TT):
                pe.wait_ge(sems["vt_ev"], n + 1)
                take(bank)
                for t in range(tiles):
                    last = tr(PB[bank][:, tile(t)], src(t))
                last.then_inc(*T.inc("vt_tr"))
                free[bank] = ("ev_act", ev)

            def norm_sum(n, width=S):
                pe.wait_ge(sems["norm_acc"], n + 1)
                mm(PB[4][:, 0:width], cst("ones"), ACC[:, 0:width]).then_inc(*T.inc("norm_ms"))
                free[4] = ("norm_rs", n + 1)

            pe.wait_ge(sems["c_in"], 16)
            pe.wait_ge(sems["lam_in"], 1)
            mm(PB[7][:, 0:2], cst("ones"), LAMP).then_inc(*T.inc("lam_mm"))
            free[7] = ("lam_exp", 1)
            norm_sum(N_MIX)

            def prep(n, lhsT, rhs, w=S):
                b = 4 + n % 4
                take(b)
                mm(PB[b][:, :], lhsT, rhs).then_inc(*T.inc("prep_mm"))
                free[b] = ("prep_act", n + 1) if n < 12 else ("kkln_in", n - 11) if n < 16 else ("prep_dve", n - 15)
            project(14, 0, "ev_act", "mix")
            pe.wait_ge(sems["sig_ready"], 1)
            for p in range(4):
                prep(p, vec("dec_aaa_up", p * P, (p + 1) * P)[0:64], PX[0:64, LORA, 1:PW])
            for p in range(4):
                prep(4 + p, vec("dec_aaa_up", p * P, (p + 1) * P)[64:128], PX[64:128, LORA, 1:PW])
            for p in range(4):
                prep(8 + p, vec("g_up", p * P, (p + 1) * P), PX[:, GD, 1:PW])
            project(4, 14, "ev_act", "mix", first=False, evbase=14)
            for p in range(4):
                pe.wait_ge(sems["kk_sq"], p + 1)
                prep(12 + p, cst("bd_ones"), CS[:, p, :])
            project(4, 18, "ev_act", "mix", first=False, evbase=18)
            for p in range(4):
                pe.wait_ge(sems["bonus_in"], p + 1)
                prep(16 + p, cst("bd_ones"), BON[:, p, :])
            for m in range(5):
                if m < 4:
                    project(1, 22 + m, "vt_ev", "mix", first=False, evbase=VT["diff"] + m)
                if m:
                    to_tokens(4 + (m - 1) % 2, lambda t: DV[:, m - 1, tile(t)], VT["diff"] + m - 1, 22 + m)

            steps = STEPS["diff"]
            for i in range(len(steps) + PIPE + 1):
                j = i - PIPE - 1
                if 0 <= j < len(steps) and steps[j][1] == TT - 1:
                    h = steps[j][0]
                    pe.wait_ge(sems["on_sq"], h + 1)
                    take(1)
                    mm(PB[1][:, :], cst("ones"), OSQ).then_inc(*T.inc("on_mm"))
                    free[1] = ("on_rs", h + 1)
                if i < len(steps):
                    h, t = steps[i]
                    w = (t + 1) * P
                    if i == 0:
                        pe.wait_ge(sems["ev_act"], 26)
                    for m in range(2):
                        b = 4 + 2 * (i % 2) + m
                        take(b)
                        r = slice(64 * m, 64 * m + 64)
                        last = mm(PB[b][:, 0:w], DQ[r, h, tile(t)], DK[r, h, 0:w])
                        if m:
                            last.then_inc(*T.inc("sc_mm"))
                        free[b] = ("sc_exp", 2 * (i + 1))
                if 2 <= i < len(steps) + 2:
                    j = i - 2
                    pe.wait_ge(sems["prob"], j + 1)
                    take(0)
                    for k in range(steps[j][1] + 1):
                        last = tr(PB[0][:, tile(k)], PR1[:, j % 2, tile(k)])
                        if k == steps[j][1]:
                            last.then_inc(*T.inc("tr_mm"))
                    free[0] = ("tr_ev", j + 1)
                j = i - PIPE
                if 0 <= j < len(steps):
                    h, t = steps[j]
                    pe.wait_ge(sems["tr_ev"], j + 1)
                    b = 2 + h % 2
                    if t == 0:
                        take(b)
                    for k in range(t + 1):
                        last = mm(PB[b][:, tile(t)], DV[:, h, tile(k)], PT[:, j % 2, tile(k)], start=k == 0, stop=k == t)
                        if k == t:
                            last.then_inc(*T.inc("pv_mm"))
                    if t == TT - 1:
                        free[b] = ("on_out", h + 1)
            end_stage()

            def bank4(b, p):
                return PB[b][:, p * P:(p + 1) * P]
            alpha, beta = (lambda p, t: KK[:, p, tile(t)]), (lambda p, t: AG[:, p, tile(t)])

            def px(m, t, lo=0, n=P):
                return PX[:, m, 1 + t * P + lo:1 + t * P + lo + n]
            for t in range(TT):
                for n, src in enumerate((alpha, lambda p, t: px(V0 + p, t), lambda p, t: BP[:, p, :], lambda p, t: KP[:, p, :])):
                    if n >= 2:
                        pe.wait_ge(sems["ch_in"], 2 * t + n - 1)
                    for p in range(4):
                        last = tr(bank4(4 + n, p), src(p, t))
                        if p == 3:
                            last.then_inc(*T.inc("ch_tr"))
                for n in range(8):
                    if n >= 4:
                        pe.wait_ge(sems["ch_aqev"], 10 * t + n - 3)
                    for e in range(2):
                        h = 4 * (n % 4 // 2) + n % 2 + 2 * e
                        p, r = h // 2, slice(64 * (h % 2), 64 * (h % 2) + 64)
                        lhsT = (beta(p, t) if n < 4 else px(K0 + p, t))[r]
                        o = 256 * e
                        mm(PB[n % 4][:, o:o + P], lhsT, alpha(p, t)[r])
                        last = mm(PB[n % 4][:, o + P:o + 256], lhsT, px(R0 + p, t)[r])
                        if e:
                            last.then_inc(*T.inc("ch_aq"))
                for q in range(2):
                    pe.wait_ge(sems["ch_aqev"], 10 * t + 5 + q)
                    for e in range(4):
                        r = slice(64 * q, 64 * q + 64)
                        last = mm(bank4(q, e), alpha(e, t)[r], beta(e, t)[r])
                        if e == 3:
                            last.then_inc(*T.inc("ch_aq"))
                for l in range(5):
                    for q in range(2):
                        if l == 0:
                            pe.wait_ge(sems["ch_t0ev"], 4 * t + 4)
                        else:
                            pe.wait_ge(sems["lv_yev"], 20 * t + 4 * (l - 1) + 2 * q + 2)
                        for e in range(4):
                            h = 2 * e + q
                            last = mm(bank4(q, e), AQ[:, h, 0:P], TI[:, h, :])
                            if e == 3:
                                last.then_inc(*T.inc("lv_x"))
                    for q in range(2):
                        pe.wait_ge(sems["lv_xev"], 10 * t + 2 * l + q + 1)
                        for e in range(4):
                            h = 2 * e + q
                            last = mm(bank4(2 + q, e), UI[:, h, :], XI[:, h, :])
                            if e == 3:
                                last.then_inc(*T.inc("lv_y"))
                        if l == 0 and q == 0:
                            pe.wait_ge(sems["ch_trev"], 4 * t + 4)
                        for e in range(4):
                            h = 2 * e + q
                            last = mm(bank4(4 + q, e), XI[:, h, :], UI[:, h, :])
                            if e == 3:
                                last.then_inc(*T.inc("lv_y"))
                pe.wait_ge(sems["lv_yev"], 20 * t + 20)
                for h in range(8):
                    last = mm(PB[4][:, h * 64:h * 64 + 64], BQ[:, h, 0:P], TOKV[:, h // 2, 64 * (h % 2):64 * (h % 2) + 64])
                    if h == 7:
                        last.then_inc(*T.inc("w1_mm"))
                for h in range(8):
                    r = slice(64 * (h % 2), 64 * (h % 2) + 64)
                    last = mm(PB[5][r, tile(h // 2)], TOKA[:, h // 2, r], UI[:, h, :])
                    if h == 7:
                        last.then_inc(*T.inc("w1_mm"))
                pe.wait_ge(sems["w1_ev"], 3 * t + 1)
                for h in range(8):
                    last = mm(PB[6][:, h * 64:h * 64 + 64], UI[:, h, :], P1[:, h // 2, 64 * (h % 2):64 * (h % 2) + 64])
                    if h == 7:
                        last.then_inc(*T.inc("w1_mm"))
                pe.wait_ge(sems["w1_ev"], 3 * t + 3)
                for c in (2 * t, 2 * t + 1):
                    r = slice(64 * (c % 2), 64 * (c % 2) + 64)
                    if c:
                        pe.wait_ge(sems["g_ev"], c)
                    for p in range(4):
                        last = mm(PB[0][r, tile(p)], TA[:, p, r], GS[c % 3][:, p, :])
                        if p == 3:
                            last.then_inc(*T.inc("sa_mm"))
                    for p in range(4):
                        mm(PB[1][:, tile(p)], TOKK[r, p, :], TOKV[r, p, :], start=p == 0, stop=False, skip_group_check=True)
                    pe.wait_ge(sems["sa_ev"], c + 1)
                    for p in range(4):
                        last = mm(PB[1][:, tile(p)], TOKB[r, p, :], SA[r, p, :], start=False, stop=True, skip_group_check=True)
                        if p == 3:
                            last.then_inc(*T.inc("gu_mm"))
                for p in range(4):
                    for q in range(2):
                        r = slice(64 * q, 64 * q + 64)
                        mm(PB[7][r, tile(p)], SA[:, p, r], AQ[:, 2 * p + q, P:2 * P], start=True, stop=False, skip_group_check=True)
                        mm(PB[7][r, tile(p)], TOKV[:, p, r], BQ[:, 2 * p + q, P:2 * P], start=False, stop=False, skip_group_check=True)
                    for e in range(2):
                        o = p * P + 64 * e
                        last = mm(PB[7][:, o:o + 64], GS[(2 * t + e) % 3][:, p, :], px(R0 + p, t, 64 * e, 64), start=False, stop=e == 1, skip_group_check=True)
                        if p == 3 and e == 1:
                            last.then_inc(*T.inc("y_mm"))
                end_stage()
            for p in range(4):
                mm(PB[p][:, :], cst("bd_ones"), HN[:, p, :]).then_inc(*T.inc("gn_mm"))
            for p in range(4):
                pe.wait_ge(sems["gn_sq"], p + 1)
                mm(PB[4 + p][:, :], cst("bd_ones"), SIG[:, p, :]).then_inc(*T.inc("gn_mm"))
            end_stage()

            project(4, 0, "norm_h", "out", evbase=RES[N_MEM])
            norm_sum(N_SRC, MEM)
            project(4, 4, "norm_h", "out", first=False, evbase=RES[N_MEM] + 4)
            take(4)
            norm_sum(N_MEM)
            evb = 26
            project(8, 0, "ev_act", "src", width=MEM, evbase=evb)
            for m in range(9):
                if m < 8:
                    project(1, m, "vt_ev", "src", first=False, width=MEM, evbase=VT["mem"] + m)
                if m:
                    to_tokens(5 + (m - 1) % 2, lambda t: MV[:, t, tile(m - 1)], VT["mem"] + m - 1, evb + 8 + m, 2)
            project(8, 0, "ev_act", "mem", evbase=evb + 16)
            steps = STEPS["mem"]
            b0 = BASE["mem"]
            pe.wait_ge(sems["ev_act"], evb + 24)
            for i in range(len(steps) + PIPE):
                if i < len(steps):
                    h, t = steps[i]
                    b = 4 + i % 2
                    take(b)
                    for j in range(2):
                        last = mm(PB[b][:, 0:MEM], MQ[:, 2 * h + j, tile(t)], MK[:, 2 * h + j, :], start=j == 0, stop=j == 1)
                        if j:
                            last.then_inc(*T.inc("sc_mm"))
                    free[b] = ("sc_exp", EXPB["mem"] + i + 1)
                if 2 <= i < len(steps) + 2:
                    j = i - 2
                    pe.wait_ge(sems["prob"], b0 + j + 1)
                    take(0)
                    for k in range(2):
                        last = tr(PB[0][:, tile(k)], MPR[:, j % 2, tile(k)])
                        if k:
                            last.then_inc(*T.inc("tr_mm"))
                    free[0] = ("tr_ev", b0 + j + 1)
                j = i - PIPE
                if j >= 0:
                    h, t = steps[j]
                    pe.wait_ge(sems["tr_ev"], b0 + j + 1)
                    b = 2 + j % 2
                    take(b)
                    for d in range(2):
                        for k in range(2):
                            last = mm(PB[b][:, tile(d)], MV[:, k, h * MEM + d * P:h * MEM + (d + 1) * P], MPT[:, j % 2, tile(k)], start=k == 0, stop=k == 1)
                            if d and k:
                                last.then_inc(*T.inc("pv_mm"))
                    free[b] = ("o_ev", j + 1)
            pe.wait_ge(sems["o_ev"], 16)
            take(0)
            project(8, 0, "norm_h", "mo", evbase=RES[N_MLP])
            take(4)
            end_stage()
            norm_sum(N_MLP)

            def mlp(n, nxt):
                x = f"mlp{n}"
                for half in range(2):
                    done = 32 * n + 16 * half
                    up, down = UNIT[f"up{n}{'ab'[half]}"], UNIT[f"down{n}{'ab'[half]}"]

                    def up_unit(i, j):
                        if half == 0 and isinstance(i, int) and j < 2:
                            if done and j == 0:
                                pe.wait_ge(sems["relu"], done)
                            if j == 0:
                                first_pair((0, 1), x, up)
                            return
                        w = weights(i * 4 + (up + j), j)
                        if done or not isinstance(i, int):
                            pe.wait_ge(sems["relu"], i * 4 + (done + j - 3))
                        product(PB[j][:, :], w, planes_of(x)).then_inc(sems["w_used"], 1)
                    for j in range(4):
                        up_unit(0, j)
                    with pe.Fori(1, 4) as i:
                        for j in range(4):
                            up_unit(i, j)

                    def down_unit(i, m, g):
                        w = weights(i * 4 + (down + 2 * m + g), g)
                        if g == 0 and not isinstance(i, int):
                            if half == 0:
                                pe.wait_ge(sems["half_h"], i * 2 + (KT * n + m - 1))
                            else:
                                pe.wait_ge(sems["norm_h"], i * 2 + (RES[nxt] + m - 1))
                        elif g == 0 and half:
                            pe.wait_ge(sems["half_h"], KT * n + KT - 1 + m)
                        if isinstance(i, int) and m == 0:
                            pe.wait_ge(sems["mlp_a"], done + 8 * (g + 1))
                        product(PB[6 + m][:, :], w, lambda k: (MAH[:, g * KT + k, :], MAL[:, g * KT + k, :]), g == 0, g == 1)\
                            .then_inc(sems["w_used"], 1)
                    for m in range(2):
                        for g in range(2):
                            down_unit(0, m, g)
                    with pe.Fori(1, 4) as i:
                        for m in range(2):
                            for g in range(2):
                                down_unit(i, m, g)
                unit[0] += 64
                if nxt is not None:
                    if nxt == N_MIX1:
                        end_stage()
                    norm_sum(nxt)
            mlp(0, N_FINAL)

            end_stage()
            norm_sum(N_MIX0)

            def rope_mm(j):
                if j < 5:
                    pe.wait_ge(sems["ev_act"], EV2 + j + 1)
                else:
                    pe.wait_ge(sems["a_sc"], j - 4)
                take(3)
                mm(PB[3][:, :], cst("rope_i" if j < 5 else "rope_a"), rope_plane(j)).then_inc(*T.inc("rope_mm"))
                free[3] = ("rope_ev", j + 1)
            for i in range(30):
                if 18 <= i < 26:
                    project(1, i, "vt_ev", "ab", first=False, evbase=VT["ab"] + i - 18, banks=2)
                elif i != 1:
                    project(2 if i == 0 else 1, i, "ev_act", "ab", evbase=EV2 + i, banks=2, first=i == 0)
                if 2 <= i < 7:
                    rope_mm(i - 2)
                if i == 7:
                    pe.wait_ge(sems["ev_act"], EV2 + 6)
                    for t in range(TT):
                        last = tr(PB[2][:, tile(t)], MISC[:, tile(t)])
                        if t == TT - 1:
                            last.then_inc(*T.inc("iw_tr"))
                    free[2] = ("iw_ev", 1)
                    for p in range(2):
                        take(4 + p)
                        mm(PB[4 + p][:, :], vec("gate_up", p * P, (p + 1) * P)[0:16], MISC[0:16, :]).then_inc(*T.inc("gate_mm"))
                        free[4 + p] = ("gate_in", p + 1)
                if 7 <= i < 11:
                    for n in range(6 * (i - 7), 6 * (i - 7) + 6):
                        t, h = INDEX_STEPS[n]
                        if n == 0:
                            pe.wait_ge(sems["rope_ev"], 5)
                        b = 6 + n % 2
                        r = slice(64 * (h % 2), 64 * (h % 2) + 64)
                        take(b)
                        mm(PB[b][:, 0:(t + 1) * P], IQ[r, h // 2, tile(t)], IK[r, 0:(t + 1) * P]).then_inc(*T.inc("idx_mm"))
                        free[b] = ("idx_r", n + 1)
                if 11 <= i < 19:
                    j = i - 11
                    pe.wait_ge(sems["a_sq"], j + 1)
                    take(2)
                    mm(PB[2][:, :], cst("ones"), SQA[:, j % 2, :]).then_inc(*T.inc("a_mm"))
                    free[2] = ("a_rs", j + 1)
                if i in LEVEL_AT:
                    l = LEVEL_AT[i]
                    if l:
                        pe.wait_ge(sems["lv_in"], 2 * l)
                    for n in range(4):
                        q, th = n // 2, n % 2
                        r = slice(64 * q, 64 * q + 64)
                        take(4 + n)
                        for e in range(4):
                            t, p = 2 * th + e // 2, e % 2
                            k_, q_ = (GK, GQ) if l == 0 else (GKE, GQE)
                            last = mm(PB[4 + n][:, tile(e)], k_[r, p, tile(t)], q_[r, p, tile(t)])
                            if e == 3:
                                last.then_inc(*T.inc("lvl_mm"))
                        free[4 + n] = ("lvl_ev", 4 * l + n + 1)
                if 12 <= i < 20:
                    rope_mm(5 + i - 12)
                if 19 <= i < 27:
                    last_v = VA[:, i - 19, :] if i < 23 else GV[:, i - 23, :]
                    to_tokens(2, lambda t: last_v[:, tile(t)], VT["ab"] + i - 19, EV2 + i)
                if i == 26:
                    pe.wait_ge(sems["ke_in"], 2)
                    for n in range(2):
                        take(4 + n)
                        for e in range(4):
                            t, p = 2 * n + e // 2, e % 2
                            last = tr(PB[4 + n][:, tile(e)], GKE[:, p, tile(t)])
                            if e == 3:
                                last.then_inc(*T.inc("ke_tr"))
                        free[4 + n] = ("ke_ev", n + 1)
                if i == 27:
                    pe.wait_ge(sems["ev_act"], EV2 + 26)
                    for t in range(3):
                        if t == 0 or t == 2:
                            take(6 + t // 2)
                        pe.wait_ge(sems["ke_ev"], t // 2 + 1)
                        for h in range(4):
                            r = slice(64 * (h % 2), 64 * (h % 2) + 64)
                            o = (256 * t if t < 2 else 0) + P * (h // 2)
                            last = mm(PB[6 + t // 2][r, o:o + P], GKT[:, t, h * 64:h * 64 + 64], GV[:, h, tile(t)])
                            if h == 3:
                                last.then_inc(*T.inc("kv2_mm"))
                    free[6] = free[7] = ("sh_ev", 3)
                if i == 28:
                    for h in range(4):
                        take(4 + h)
                        for t in range(TT):
                            th, e = t // 2, 2 * (t % 2) + h // 2
                            mm(PB[4 + h][:, tile(t)], GV[:, h, tile(t)], ATT[:, 2 * (h % 2) + th, tile(e)], start=t == 0, stop=t == 0, skip_group_check=True)
                    pe.wait_ge(sems["sh_ev"], 3)
                    for h in range(4):
                        r = slice(64 * (h % 2), 64 * (h % 2) + 64)
                        for t in range(1, TT):
                            last = mm(PB[4 + h][:, tile(t)], GSH[r, t, P * (h // 2):P * (h // 2) + P], GQE[r, h // 2, tile(t)], start=False, stop=True, skip_group_check=True)
                            if t == 3:
                                last.then_inc(*T.inc("go_mm"))
                        free[4 + h] = ("go_ev", h + 1)
            for h in range(4):
                pe.wait_ge(sems["go_sq"], h + 1)
                take(2 + h % 2)
                mm(PB[2 + h % 2][:, :], cst("ones"), GSQ[:, h, :]).then_inc(*T.inc("go_nm"))
                free[2 + h % 2] = ("go_ln", h + 1)

            pe.wait_ge(sems["rope_ev"], 13)
            steps = STEPS["A"]
            b0 = BASE["A"]
            for i in range(len(steps) + PIPE):
                if i < len(steps):
                    h, t = steps[i]
                    w = (t + 1) * P
                    b = i % 2
                    take(b)
                    mm(PB[b][:, 0:w], QA[:, h, tile(t)], KA[:, h, 0:w]).then_inc(*T.inc("sc_mm"))
                    free[b] = ("sc_exp", EXPB["A"] + i + 1)
                if 2 <= i < len(steps) + 2:
                    j = i - 2
                    pe.wait_ge(sems["prob"], b0 + j + 1)
                    take(2)
                    for k in range(steps[j][1] + 1):
                        last = tr(PB[2][:, tile(k)], APR[:, j % 2, tile(k)])
                        if k == steps[j][1]:
                            last.then_inc(*T.inc("tr_mm"))
                    free[2] = ("tr_ev", b0 + j + 1)
                j = i - PIPE
                if j >= 0:
                    h, t = steps[j]
                    pe.wait_ge(sems["tr_ev"], b0 + j + 1)
                    b = 3 + j % 2
                    take(b)
                    for k in range(t + 1):
                        last = mm(PB[b][:, 0:P], VA[:, h, tile(k)], APT[:, j % 2, tile(k)], start=k == 0, stop=k == t)
                        if k == t:
                            last.then_inc(*T.inc("pv_mm"))
                    free[b] = ("o_ev", 16 + j + 1)
            pe.wait_ge(sems["o_ev"], 32)
            take(0)
            project(8, 0, "norm_h", "oab", evbase=RES[N_FFN0])
            take(4)
            end_stage()
            norm_sum(N_FFN0)
            mlp(1, N_MIX1)

            steps = STEPS["C"]
            b0 = BASE["C"]

            def c_transpose(j):
                pe.wait_ge(sems["c_prob"], j + 1)
                take(0)
                for k in range(steps[j][1] + 1):
                    last = tr(PB[0][:, tile(k)], CPR[:, j % 4, tile(k)])
                    if k == steps[j][1]:
                        last.then_inc(*T.inc("tr_mm"))
                free[0] = ("tr_ev", b0 + j + 1)

            def c_norm(c, hd):
                pe.wait_ge(sems["c_sq"], 2 * hd + c + 1)
                take(7)
                mm(PB[7][:, :], cst("ones"), CSQ[:, c, :]).then_inc(*T.inc("c_nm"))
                free[7] = ("c_rln", 2 * hd + c + 1)
            for r in C_ROUNDS:
                hd = r // 2 + 2
                if 0 <= 2 * r - 4 < len(steps):
                    c_transpose(2 * r - 4)
                for i in (2 * r, 2 * r + 1):
                    if 0 <= i < len(steps):
                        h, t = steps[i]
                        w = (t + 1) * P
                        b = 4 + i % 3
                        pe.wait_ge(sems["c_sc"], 2 * h + 2)
                        take(b)
                        mm(PB[b][:, 0:w], CQ[:, h, tile(t)], CK[:, h, 0:w]).then_inc(*T.inc("sc_mm"))
                        free[b] = ("c_la", i + 1)
                if 0 <= 2 * r - 3 < len(steps):
                    c_transpose(2 * r - 3)
                for j in (2 * r - 6, 2 * r - 5):
                    if j >= 0:
                        h, t = steps[j]
                        pe.wait_ge(sems["tr_ev"], b0 + j + 1)
                        pe.wait_ge(sems["ev_act"], EV3 + 3 * h + 3)
                        if j >= 2 and j % 2 == 0:
                            pe.wait_ge(sems["o_ev"], 32 + j // 2)
                        for k in range(t + 1):
                            last = mm(PB[1][:, tile(j % 2)], CV[:, h, tile(k)], CPT[:, j % 4, tile(k)], start=k == 0, stop=k == t)
                            if k == t:
                                last.then_inc(*T.inc("pv_mm"))
                if r % 2 == 0 and 0 <= hd - 1 < 8:
                    to_tokens(7, lambda t: CV[:, hd - 1, tile(t)], VT["c"] + hd - 1, EV3 + 3 * hd)
                if r % 2 == 0 and hd < 8:
                    if hd == 0:
                        project(2, 2, "ev_act", "c", evbase=EV3)
                    else:
                        project(2, 2, "ev_act", "c", first=False, evbase=EV3 + 3 * hd)
                if r % 2 and hd < 8:
                    c_norm(0, hd)
                    project(1, 2, "vt_ev", "c", first=False, evbase=VT["c"] + hd)
                    c_norm(1, hd)
            pe.wait_ge(sems["o_ev"], 48)
            take(0)
            project(8, 0, "norm_h", "oc", evbase=RES[N_FFN1])
            take(4)
            end_stage()
            norm_sum(N_FFN1)
            mlp(2, None)


def planes(a):
    a = np.ascontiguousarray(np.asarray(a).T)
    return np.ascontiguousarray(a.reshape(a.shape[0] // P, P, a.shape[1]).transpose(1, 0, 2))


def units(w):
    k, n = w.shape
    a = w.reshape(k // (KT * P), KT, P, n // P, P).transpose(3, 0, 2, 1, 4)
    return a.reshape(-1, P, KT * P)


def stream(i):
    w_in, w_ab, w_c = i["w_in"][0], i["w_in_ab_2"][0], i["w_in_c_2"][0]
    r = 512
    ab = {}
    o = 0
    for name, n in (("qa", 512), ("ka", 512), ("va", 512), ("iq", 512), ("ik", 64), ("iw", 8),
                    ("qb", 256), ("kb", 256), ("vb", 512), ("g", 16), ("og", 512)):
        ab[name] = w_ab[:, o:o + n]
        o += n
    misc = np.zeros((w_ab.shape[0], P), w_ab.dtype)
    misc[:, 0:16], misc[:, 32:40] = ab["g"], ab["iw"]
    parts = {
        "rwkv_lora": w_in[:, 3 * r:3 * r + 256], "rwkv_k": w_in[:, r:2 * r], "rwkv_r": w_in[:, 0:r],
        "rwkv_v": w_in[:, 2 * r:3 * r], "diff_q": w_in[:, 1792:1792 + r], "diff_k": w_in[:, 1792 + r:1792 + 2 * r],
        "diff_v": w_in[:, 1792 + 2 * r:1792 + 3 * r], "out": i["w_out"][0], "mem_k": i["w_mk"][0], "mem_v": i["w_mv"][0],
        "mem_q": i["w_mq"][0], "mem_o": i["w_mo"][0],
        "a_q": ab["qa"], "a_k": ab["ka"], "a_v": ab["va"], "i_q": ab["iq"],
        "i_k": np.concatenate([ab["ik"], ab["ik"]], 1), "misc": misc, "b_q": ab["qb"], "b_k": ab["kb"],
        "b_v": ab["vb"], "b_og": ab["og"], "out_ab": i["w_out_ab_2"][0],
        "c_in": np.concatenate([w_c[:, c * 1024 + h * P:c * 1024 + (h + 1) * P] for h in range(8) for c in range(3)], 1), "out_c": i["w_out_c_2"][0]}
    for n, (up, down) in enumerate(((i["w_up"][0], i["w_down"][0]), (i["w_up_2"][0], i["w_down_2"][0]),
                                    (i["w_up_2"][1], i["w_down_2"][1]))):
        f = up.shape[1] // 2
        for half in range(2):
            parts[f"up{n}{'ab'[half]}"] = up[:, half * f:(half + 1) * f]
            parts[f"down{n}{'ab'[half]}"] = down[half * f:(half + 1) * f]
    out = np.zeros((STREAM_UNITS, P, KT * P), np.float32)
    for name, n in STREAM:
        out[UNIT[name]:UNIT[name] + n] = units(parts[name])
    return out


def vectors(i):
    v = np.zeros((P, N_VEC), np.float32)

    def put(name, a):
        o, n = VO[name]
        v[:, o:o + n] = a.reshape(n, P).T
    put("norm_mix", i["norm_mix_w"][0])
    put("norm_mem", i["norm_mem_w"][0])
    put("norm_src", i["norm_src_w"][0])
    put("norm_mlp", i["norm_mlp_w"][0])
    put("norm_final", i["norm_final_w"])
    for l in range(2):
        put(f"g_mix{l}", i["g_mix_2"][l])
        put(f"g_ffn{l}", i["g_ffn_2"][l])
    mu = i["mu_shift"][0]
    put("mu", np.concatenate([mu[1536:1792], mu[512:1024], mu[0:512], mu[1024:1536]]))
    for name, key in (("w0", "w_decay0"), ("a0", "a0"), ("k_k", "k_k"), ("k_a", "k_a"), ("r_k", "r_k"),
                      ("lnx_w", "lnx_w"), ("lnx_b", "lnx_b"), ("subln", "subln_w"), ("gq_a", "gq_a_2"), ("gk_a", "gk_a_2"),
                      ("gq_c", "gq_c_2"), ("gk_c", "gk_c_2"), ("g_gla", "g_gla_2"), ("b_gate", "b_gate_2")):
        put(name, i[key][0].reshape(-1))
    o = VO["lam"][0]
    for n, key in enumerate(("lam_q1", "lam_q2", "lam_k1", "lam_k2")):
        v[0:64, o + n] = i[key][0]
    o = VO["dec_aaa_up"][0]
    v[0:64, o:o + 512] = i["w_decay_up"][0]
    v[64:128, o:o + 512] = i["a_up"][0]
    o = VO["g_up"][0]
    v[:, o:o + 512] = i["g_up"][0]
    o = VO["gate_up"][0]
    v[0:16, o:o + 256] = i["w_gate_up_2"][0]
    return v


def kernel(**inputs):
    from concourse import bacc
    from concourse.bass_utils import run_bass_kernel_spmd
    i = {k: np.asarray(v) for k, v in inputs.items()}
    nc = bacc.Bacc("TRN2", target_bir_lowering=False, num_devices=1, dynamic_dma_scratch_size=1024)
    arrays = {"x_in": planes(i["x"][0]), "mem_in": planes(i["mem"][0]), "weights_in": stream(i),
              "constants_in": constants(), "vectors_in": vectors(i)}
    aps = [nc.dram_tensor(n, a.shape, F32, kind="ExternalInput").ap() for n, a in arrays.items()]
    out = nc.dram_tensor("h_out", (P, KT, S), F32, kind="ExternalOutput").ap()
    build(nc, *aps, out)
    r = run_bass_kernel_spmd(nc, [arrays], core_ids=[0])
    h = r.results[0]["h_out"]
    return np.ascontiguousarray(h.transpose(2, 1, 0).reshape(1, S, KT * P))
```
